# Optimizing a Trainium2 kernel written in Bass

```python
import math
import jax, jax.numpy as jnp
from jax import lax
import numpy as np

D_MODEL = 1024
BATCH = 1
SEQ = 256
DEPTH = 2

ATTN_HEAD_DIM = 64
ATTN_HEADS = D_MODEL // (2 * ATTN_HEAD_DIM)
ATTN_WIDTH = ATTN_HEADS * 2 * ATTN_HEAD_DIM
Q_BLOCK = 128
NUM_BUCKETS = 32
MAX_EXACT = NUM_BUCKETS // 2
MAX_DISTANCE = 128
SSD_D_INNER = 2 * D_MODEL
SSD_HEAD_DIM = 64
SSD_HEADS = SSD_D_INNER // SSD_HEAD_DIM
SSD_GROUPS = 4
SSD_D_STATE = 128
SSD_CONV = 4
SSD_CHUNK = 128
SSD_CONV_DIM = SSD_D_INNER + 2 * SSD_GROUPS * SSD_D_STATE
SSD_IN_DIM = 2 * SSD_D_INNER + 2 * SSD_GROUPS * SSD_D_STATE + SSD_HEADS
FFN_DIM = D_MODEL * 7 // 2
N_EXPERTS = 8
TOP_K = 2
NORM_EPS = 1e-6

kernel_name = "hybrid_diffattn_ssd_moe"

def rms_norm(x, w):
    xf = x.astype(jnp.float32)
    y = xf * lax.rsqrt(jnp.mean(xf * xf, axis=-1, keepdims=True) + NORM_EPS)
    return (y * w.astype(jnp.float32)).astype(x.dtype)

def lambda_init_for(layer_idx):
    return 0.8 - 0.6 * math.exp(-0.3 * layer_idx)

def t5_bucket(dist):
    n = jnp.maximum(dist, 0)
    large = MAX_EXACT + (jnp.log(jnp.maximum(n, 1).astype(jnp.float32) / MAX_EXACT)
                         / math.log(MAX_DISTANCE / MAX_EXACT)
                         * (NUM_BUCKETS - MAX_EXACT)).astype(jnp.int32)
    large = jnp.minimum(large, NUM_BUCKETS - 1)
    return jnp.where(n < MAX_EXACT, n, large)

def diff_attention(h, w_in, q_gain, k_gain, lam_params, subln_w, w_out, rel_bias, lambda_init):
    b, s, _ = h.shape
    d = ATTN_HEAD_DIM
    q, k, v = jnp.split(h @ w_in, 3, axis=-1)
    q = rms_norm(q.reshape(b, s, ATTN_HEADS, 2, d), q_gain).transpose(3, 0, 2, 1, 4)
    k = rms_norm(k.reshape(b, s, ATTN_HEADS, 2, d), k_gain).transpose(3, 0, 2, 1, 4)
    q1, q2 = q[0], q[1]
    k1, k2 = k[0], k[1]
    v = v.reshape(b, s, ATTN_HEADS, 2 * d).transpose(0, 2, 1, 3)
    lp = lam_params.astype(jnp.float32)
    lam = jnp.exp(jnp.sum(lp[0] * lp[1])) - jnp.exp(jnp.sum(lp[2] * lp[3])) + lambda_init
    n_blocks = s // Q_BLOCK
    pos = jnp.arange(s, dtype=jnp.int32)
    scale = d ** -0.5

    def to_blocks(t):
        return t.reshape(b, ATTN_HEADS, n_blocks, Q_BLOCK, d).transpose(2, 0, 1, 3, 4)

    def block(args):
        q1b, q2b, qpos = args
        dist = qpos[:, None] - pos[None, :]
        bias = jnp.transpose(rel_bias[t5_bucket(dist)], (2, 0, 1)).astype(jnp.float32)
        visible = dist >= 0

        def probs(qb, kk):
            logits = jnp.einsum('bhqd,bhkd->bhqk', qb, kk).astype(jnp.float32) * scale + bias
            return jax.nn.softmax(jnp.where(visible, logits, -jnp.inf), axis=-1)

        attn = probs(q1b, k1) - lam * probs(q2b, k2)
        return jnp.einsum('bhqk,bhkv->bhqv', attn.astype(v.dtype), v)

    o = lax.map(block, (to_blocks(q1), to_blocks(q2), pos.reshape(n_blocks, Q_BLOCK)))
    o = o.transpose(1, 2, 0, 3, 4).reshape(b, ATTN_HEADS, s, 2 * d)
    o = rms_norm(o, subln_w) * (1.0 - lambda_init)
    o = o.transpose(0, 2, 1, 3).reshape(b, s, ATTN_WIDTH)
    return o @ w_out

def causal_depthwise_conv(x, w, bias):
    y = lax.conv_general_dilated(x, w[:, None, :], window_strides=(1,),
                                 padding=[(w.shape[0] - 1, 0)],
                                 dimension_numbers=('NWC', 'WIO', 'NWC'),
                                 feature_group_count=x.shape[-1])
    return y + bias

def ssd_chunked(x, dt, a, bm, cm):
    b, s, h, p = x.shape
    g, n = bm.shape[-2:]
    r = h // g
    l = SSD_CHUNK
    c = s // l
    xd = (x * dt[..., None]).reshape(b, c, l, g, r, p)
    da = (dt * a).reshape(b, c, l, g, r).transpose(0, 1, 3, 4, 2)
    bm = bm.reshape(b, c, l, g, n)
    cm = cm.reshape(b, c, l, g, n)
    a_cs = jnp.cumsum(da, axis=-1)
    causal = jnp.tril(jnp.ones((l, l), dtype=bool))
    decay_in = jnp.exp(jnp.where(causal, a_cs[..., :, None] - a_cs[..., None, :], -jnp.inf))
    cb = jnp.einsum('bclgn,bcsgn->bcgls', cm, bm)
    y_diag = jnp.einsum('bcgrls,bcsgrp->bclgrp', cb[:, :, :, None] * decay_in, xd)
    decay_states = jnp.exp(a_cs[..., -1:] - a_cs)
    states = jnp.einsum('bclgn,bcgrl,bclgrp->bcgrpn', bm, decay_states, xd)
    chunk_tot = jnp.pad(a_cs[..., -1].transpose(0, 2, 3, 1), ((0, 0), (0, 0), (0, 0), (1, 0)))
    cs2 = jnp.cumsum(chunk_tot, axis=-1)
    causal_c = jnp.tril(jnp.ones((c + 1, c + 1), dtype=bool))
    decay_chunk = jnp.exp(jnp.where(causal_c, cs2[..., :, None] - cs2[..., None, :], -jnp.inf))
    states = jnp.concatenate([jnp.zeros_like(states[:, :1]), states], axis=1)
    states = jnp.einsum('bgrzc,bcgrpn->bzgrpn', decay_chunk, states)[:, :-1]
    y_off = jnp.einsum('bclgn,bcgrpn,bcgrl->bclgrp', cm, states, jnp.exp(a_cs))
    return (y_diag + y_off).reshape(b, s, h, p)

def ssd_mixer(h, w_in, conv_w, conv_b, dt_bias, a_log, d_skip, norm_w, w_out):
    b, s, _ = h.shape
    gn = SSD_GROUPS * SSD_D_STATE
    proj = h @ w_in
    z = proj[..., :SSD_D_INNER]
    xbc = proj[..., SSD_D_INNER:SSD_D_INNER + SSD_CONV_DIM]
    dt = proj[..., SSD_D_INNER + SSD_CONV_DIM:]
    xbc = jax.nn.silu(causal_depthwise_conv(xbc, conv_w, conv_b))
    xs = xbc[..., :SSD_D_INNER].reshape(b, s, SSD_HEADS, SSD_HEAD_DIM).astype(jnp.float32)
    bm = xbc[..., SSD_D_INNER:SSD_D_INNER + gn].reshape(b, s, SSD_GROUPS, SSD_D_STATE).astype(jnp.float32)
    cm = xbc[..., SSD_D_INNER + gn:].reshape(b, s, SSD_GROUPS, SSD_D_STATE).astype(jnp.float32)
    dt = jax.nn.softplus(dt.astype(jnp.float32) + dt_bias.astype(jnp.float32))
    a = -jnp.exp(a_log.astype(jnp.float32))
    y = ssd_chunked(xs, dt, a, bm, cm) + d_skip.astype(jnp.float32)[:, None] * xs
    y = y.reshape(b, s, SSD_D_INNER) * jax.nn.silu(z.astype(jnp.float32))
    y = rms_norm(y.reshape(b, s, SSD_GROUPS, SSD_D_INNER // SSD_GROUPS),
                 norm_w.reshape(SSD_GROUPS, SSD_D_INNER // SSD_GROUPS)).reshape(b, s, SSD_D_INNER)
    return y.astype(h.dtype) @ w_out

def swiglu(h, w_gate, w_up, w_down):
    return (jax.nn.silu(h @ w_gate) * (h @ w_up)) @ w_down

def moe_swiglu(h, router, w_gate, w_up, w_down):
    b, s, d = h.shape
    t = h.reshape(b * s, d)
    logits = (t @ router).astype(jnp.float32)
    top_logits, top_idx = lax.top_k(logits, TOP_K)
    top_w = jax.nn.softmax(top_logits, axis=-1)
    combine = jnp.einsum('tk,tke->te', top_w, jax.nn.one_hot(top_idx, N_EXPERTS, dtype=jnp.float32))
    out = jnp.zeros_like(t)
    for e in range(N_EXPERTS):
        out = out + combine[:, e:e + 1].astype(t.dtype) * swiglu(t, w_gate[e], w_up[e], w_down[e])
    return out.reshape(b, s, d)

def setup_inputs(seed: int = 0) -> dict:
    key = jax.random.key(seed)
    ks = iter(jax.random.split(key, 40))
    n_even = (DEPTH + 1) // 2
    n_odd = DEPTH // 2

    def nrm(shape, scale):
        return jax.random.normal(next(ks), shape, jnp.float32) * scale

    def gain(shape):
        return 1.0 + nrm(shape, 0.02)

    dt0 = jnp.exp(jax.random.uniform(next(ks), (n_odd, SSD_HEADS), jnp.float32)
                  * (math.log(0.1) - math.log(0.001)) + math.log(0.001))
    dt_bias = dt0 + jnp.log(-jnp.expm1(-dt0))
    a_log = jnp.log(jax.random.uniform(next(ks), (n_odd, SSD_HEADS), jnp.float32, minval=1.0, maxval=16.0))
    return {
        "x": nrm((BATCH, SEQ, D_MODEL), 1.0),
        "rel_bias": nrm((NUM_BUCKETS, ATTN_HEADS), 0.5),
        "norm_mix": gain((DEPTH, D_MODEL)),
        "norm_ffn": gain((DEPTH, D_MODEL)),
        "attn_w_in": nrm((n_even, D_MODEL, 3 * ATTN_WIDTH), D_MODEL ** -0.5),
        "attn_q_gain": gain((n_even, ATTN_HEAD_DIM)),
        "attn_k_gain": gain((n_even, ATTN_HEAD_DIM)),
        "attn_lambda": nrm((n_even, 4, ATTN_HEAD_DIM), 0.1),
        "attn_subln": gain((n_even, 2 * ATTN_HEAD_DIM)),
        "attn_w_out": nrm((n_even, ATTN_WIDTH, D_MODEL), ATTN_WIDTH ** -0.5),
        "ffn_w_gate": nrm((n_even, D_MODEL, FFN_DIM), D_MODEL ** -0.5),
        "ffn_w_up": nrm((n_even, D_MODEL, FFN_DIM), D_MODEL ** -0.5),
        "ffn_w_down": nrm((n_even, FFN_DIM, D_MODEL), FFN_DIM ** -0.5),
        "ssd_w_in": nrm((n_odd, D_MODEL, SSD_IN_DIM), D_MODEL ** -0.5),
        "ssd_conv_w": nrm((n_odd, SSD_CONV, SSD_CONV_DIM), SSD_CONV ** -0.5),
        "ssd_conv_b": nrm((n_odd, SSD_CONV_DIM), 0.02),
        "ssd_dt_bias": dt_bias,
        "ssd_a_log": a_log,
        "ssd_d": gain((n_odd, SSD_HEADS)),
        "ssd_norm": gain((n_odd, SSD_D_INNER)),
        "ssd_w_out": nrm((n_odd, SSD_D_INNER, D_MODEL), SSD_D_INNER ** -0.5),
        "moe_router": nrm((n_odd, D_MODEL, N_EXPERTS), D_MODEL ** -0.5),
        "moe_w_gate": nrm((n_odd, N_EXPERTS, D_MODEL, FFN_DIM), D_MODEL ** -0.5),
        "moe_w_up": nrm((n_odd, N_EXPERTS, D_MODEL, FFN_DIM), D_MODEL ** -0.5),
        "moe_w_down": nrm((n_odd, N_EXPERTS, FFN_DIM, D_MODEL), FFN_DIM ** -0.5),
    }

def reference(x, rel_bias, norm_mix, norm_ffn, attn_w_in, attn_q_gain, attn_k_gain, attn_lambda,
              attn_subln, attn_w_out, ffn_w_gate, ffn_w_up, ffn_w_down, ssd_w_in, ssd_conv_w,
              ssd_conv_b, ssd_dt_bias, ssd_a_log, ssd_d, ssd_norm, ssd_w_out, moe_router,
              moe_w_gate, moe_w_up, moe_w_down):
    for i in range(DEPTH):
        j = i // 2
        h = rms_norm(x, norm_mix[i])
        if i % 2 == 0:
            x = x + diff_attention(h, attn_w_in[j], attn_q_gain[j], attn_k_gain[j], attn_lambda[j],
                                   attn_subln[j], attn_w_out[j], rel_bias, lambda_init_for(i))
            h = rms_norm(x, norm_ffn[i])
            x = x + swiglu(h, ffn_w_gate[j], ffn_w_up[j], ffn_w_down[j])
        else:
            x = x + ssd_mixer(h, ssd_w_in[j], ssd_conv_w[j], ssd_conv_b[j], ssd_dt_bias[j],
                              ssd_a_log[j], ssd_d[j], ssd_norm[j], ssd_w_out[j])
            h = rms_norm(x, norm_ffn[i])
            x = x + moe_swiglu(h, moe_router[j], moe_w_gate[j], moe_w_up[j], moe_w_down[j])
    return x


_drawn_inputs = setup_inputs


def setup_inputs(seed=0):
    import zlib

    import numpy as np

    out = dict(_drawn_inputs(seed))
    spreads = {}
    factors = {}
    for name, (base, spread) in spreads.items():
        noise = np.random.default_rng([zlib.crc32(name.encode()), seed]).standard_normal(out[name].shape)
        drawn = base * np.exp(spread * noise) if base else spread * noise
        out[name] = __import__('jax').numpy.asarray(drawn.astype(out[name].dtype))
    for name, factor in factors.items():
        out[name] = (out[name] * factor).astype(out[name].dtype)
    return out
```

```python
import math
from contextlib import ExitStack

import numpy as np

import concourse.bass as bass
from concourse import mybir

F32 = mybir.dt.float32
I32 = mybir.dt.int32
ALU = mybir.AluOpType
ACT = mybir.ActivationFunctionType
AX_X = mybir.AxisListType.X

P = 128
D = 1024
KD = D // P
T = 256
TT = T // P
HEADS = 8
HD = 64
F = 3584
NC_F = F // 512
DI = 2048
GROUPS = 4
NSTATE = 128
SH = 32
HPG = SH // GROUPS
E = 8
SLOTS = 96
PASSES = 3
JOBS = E * PASSES
LAMBDA_INIT = 0.8 - 0.6 * math.exp(0.0)
EPS = 1e-6
MASKED = -1e30
BUCKETS = 32
DENSE_RING = 6
RING = 7
SLOT = 4096

CONSTS = {}
_at = 0
for _name, _n in (("ident", 128), ("anti", 128), ("mean_d", 128), ("mean_hd", 128), ("mean_v", 128),
                  ("mean_g", 128), ("upto", 128), ("before", 128), ("ones", 128), ("slot_no", SLOTS),
                  ("rank_of", E), ("eps", 1), ("one", 1), ("odd_even", 128), ("pair_of", 16)):
    CONSTS[_name] = (_at, _at + _n)
    _at += _n
NCONST = _at
NORM_MIX, NORM_FFN, CONV_B, SSD_NORM, SUBLN, Q_GAIN, K_GAIN = 0, 16, 32, 56, 72, 73, 74
ROWS_B = 75
NDIST = 2 * P + P - 1


def constants():
    c = np.zeros((P, NCONST), np.float32)
    i = np.arange(P)

    def put(name, v):
        a, b = CONSTS[name]
        c[:, a:b] = v

    put("ident", np.eye(P))
    put("anti", np.eye(P)[::-1])
    put("mean_d", 1.0 / D)
    put("mean_hd", (i[:, None] // HD == i[None, :] // HD) / HD)
    put("mean_v", 1.0 / P)
    put("mean_g", 1.0 / (DI // GROUPS))
    put("upto", i[:, None] <= i[None, :])
    put("before", i[:, None] < i[None, :])
    put("ones", 1.0)
    put("slot_no", np.arange(SLOTS)[None, :])
    put("rank_of", (E - np.arange(E))[None, :])
    put("eps", EPS)
    put("one", 1.0)
    put("odd_even", i[:, None] % 2 == i[None, :] // HD)
    put("pair_of", i[:, None] // 2 == np.arange(16)[None, :])
    dist = 255 - np.arange(NDIST)
    n = np.maximum(dist, 0)
    exact = BUCKETS // 2
    large = exact + (np.log(np.maximum(n, 1).astype(np.float32) / np.float32(exact)) / np.float32(math.log(128 / exact))
                     * np.float32(BUCKETS - exact)).astype(np.int32)
    bucket = np.where(n < exact, n, np.minimum(large, BUCKETS - 1))
    hot = np.zeros((BUCKETS + 1, NDIST), np.float32)
    for j in range(NDIST):
        hot[BUCKETS if dist[j] < 0 else bucket[j], j] = 1.0
    return c, hot


N_ROWS, N_MISC = 10, 3


def conv_block(i):
    return 16 + 2 * i if i < 4 else 2 * i - 8


class Chain:

    def __init__(self, eng, sem):
        self.eng, self.sem, self.n = eng, sem, 0

    def link(self, ins):
        self.n += 1
        ins.then_inc(self.sem, 1)
        self.eng.wait_ge(self.sem, self.n)


class Banks:

    def __init__(self, full, free):
        self.full, self.free = full, free
        self.count = [0] * 8
        self.at = {}

    def plan(self, name, bank):
        self.at[name] = (bank, self.count[bank])
        self.count[bank] += 1

    def claim(self, pe, name):
        b, k = self.at[name]
        if k:
            pe.wait_ge(self.free[b], k)

    def finish(self, ins, name):
        ins.then_inc(self.full[self.at[name][0]], 1)

    def ready(self, eng, name):
        b, k = self.at[name]
        eng.wait_ge(self.full[b], k + 1)

    def release(self, ins, name):
        ins.then_inc(self.free[self.at[name][0]], 1)

    def released(self, eng, name):
        b, k = self.at[name]
        eng.wait_ge(self.free[b], k + 1)


def dense_tiles():
    tiles = []
    for t in range(2):
        tiles += [("attn_q", t), ("attn_k", t)]
    tiles += [("attn_v", 0), ("attn_v", 1), ("attn_out", 0), ("attn_out", 1)]
    for c in range(NC_F):
        tiles += [("ffn_gate", c), ("ffn_up", c)]
        if c:
            tiles.append(("ffn_down", c - 1))
    tiles.append(("ffn_down", NC_F - 1))
    tiles += [("ssd_b", 0), ("ssd_c", 0)] + [("ssd_x", t) for t in range(4)] + [("ssd_z", t) for t in range(4)]
    tiles += [("ssd_out", t) for t in range(4)]
    return tiles


def expert_tiles():
    tiles = []
    for c in range(NC_F):
        tiles += [("gate", c), ("up", c)]
        if c:
            tiles.append(("down", c - 1))
    tiles.append(("down", NC_F - 1))
    return tiles


def hybrid_trunk(nc, x, rel_bias, norm_mix, norm_ffn, attn_w_in, attn_q_gain, attn_k_gain, attn_lambda,
                 attn_subln, attn_w_out, ffn_w_gate, ffn_w_up, ffn_w_down, ssd_w_in, ssd_conv_w, ssd_conv_b,
                 ssd_dt_bias, ssd_a_log, ssd_d, ssd_norm, ssd_w_out, moe_router, moe_w_gate, moe_w_up,
                 moe_w_down, const, hot, out):
    DT = dense_tiles()
    DENSE = {name: n for n, name in enumerate(DT)}
    ND = len(DT)
    ET = expert_tiles()
    EXPERT = {name: m for m, name in enumerate(ET)}
    NE = len(ET)
    assert NE % RING == 0
    dense_in_slot = [sum(1 for n in range(ND) if n % DENSE_RING == s) if s < DENSE_RING else 0 for s in range(RING)]

    with ExitStack() as ctx:
        def sb(name, shape, dt=F32):
            return ctx.enter_context(nc.sbuf_tensor(name, shape, dt))

        def sem(name):
            return ctx.enter_context(nc.semaphore(name))

        ring = sb("ring", [P, RING, SLOT])
        cst = sb("cst", [P, NCONST])
        xT = sb("xT", [P, KD, T])
        hT = sb("hT", [P, KD, T])
        colA = sb("colA", [P, 96])
        colB = sb("colB", [P, 80])
        rows = sb("rows", [P, 2, P])
        dcol = sb("dcol", [P, 16])
        small = sb("small", [P, 64])
        rstd = sb("rstd", [P, T])
        WORK = 16800
        work = sb("work", [P, WORK])

        def carve(spec):
            got, at = [], 0
            for shape in spec:
                n = int(np.prod(shape))
                v = work[:, at:at + n]
                if len(shape) > 1:
                    names = " ".join("abc"[:len(shape)])
                    v = v.rearrange(f"p ({names}) -> p {names}", **{"abc"[i]: s for i, s in enumerate(shape)})
                got.append(v)
                at += n
            assert at <= WORK, at
            return got

        qT, kT, V, oT, bias, sqb, rq, L, A, AT, sqo, ro, lam_in, st = carve(
            [(HEADS, T), (HEADS, T), (TT, D), (HEADS, T), (HEADS, T), (2, 512), (2, 512),
             (2, 2 * 384), (2, 384), (2, 384), (2, T), (2, T), (4 * HD,), (2, 16)])
        hid, sg = carve([(2, 4 * T), (4, 512)])
        hid = hid.rearrange("p b (f t) -> p b f t", f=4)
        (xsT, BT, CT, xd, xw, Bn, cbm, stS, dec, eC, cvb, wdt, dtv, dta, da, acs, w0, alog, rg, drow) = carve(
            [(16, T), (4, T), (4, T), (2, 2 * 512), (2, 512), (2, P), (2, 2 * P), (2, 512), (4, 512), (2, 512),
             (2, 512), (KD, SH), (TT, SH), (TT, SH), (TT, SH), (TT, SH), (SH,), (2, SH), (2, T), (32,)])
        zr = ring[:, RING - 1, :].rearrange("p (b t) -> p b t", b=16)
        (xnat, hnat, hTg, ehid, esg, Pm, PT, ysb, ynat, lg, oh, tw, rj, cj, router) = carve(
            [(TT, D), (TT, D), (KD, SLOTS), (2, 4 * SLOTS), (2, 4 * SLOTS), (TT, SLOTS), (TT, P), (KD, SLOTS),
             (D,), (TT, E), (4, TT * E), (12, TT * E), (TT, JOBS + 1), (TT, JOBS), (KD, E)])
        ehid = ehid.rearrange("p b (f t) -> p b f t", f=4)
        flag = sb("flag", [P, 2], I32)
        xin = ring[:, RING - 1, 0:TT * D].rearrange("p (a b) -> p a b", a=TT)
        hankel = ring[:, RING - 1, TT * D:SLOT].rearrange("p (h t) -> p h t", h=HEADS)
        onehot = sb("onehot", [BUCKETS + 1, NDIST])
        relb = sb("relb", [BUCKETS + 1, HEADS])
        ubias = sb("ubias", [HEADS, NDIST])
        scratch = nc.dram_tensor("bias_by_distance", (HEADS, 512), F32).ap()

        def C(name, n=P):
            a, b = CONSTS[name]
            return cst[0:n, a:b]

        bank = [ctx.enter_context(nc.psum_tensor(f"bank{b}", [P, 512], F32)) for b in range(8)]
        full = [sem(f"full{b}") for b in range(8)]
        free = [sem(f"free{b}") for b in range(8)]
        B = Banks(full, free)

        B.plan("rowsA", 4), B.plan("rowsB", 5), B.plan("dcol", 6), B.plan("ubias", 7)
        for i in range(4):
            B.plan(("x", i), 4 + i)
        B.plan(("ms", 0), 4)
        for i in range(9):
            if i < 8:
                B.plan(("qk", i), i % 4)
            if i:
                B.plan(("qk_ms", i - 1), 4 + (i - 1) % 2)
        for i in range(4):
            B.plan(("v", i), 6 + i % 2)
        for i in range(4):
            B.plan(("bias", i), i)
        for i in range(HEADS + 4):
            if i < HEADS:
                B.plan(("s", i, 0), i % 2), B.plan(("s", i, 1), 2 + i % 2)
            if 0 <= i - 2 < HEADS:
                B.plan(("at", i - 2), 4)
            if 0 <= i - 3 < HEADS:
                B.plan(("o", i - 3), 5 + (i - 3) % 2)
            if 0 <= i - 4 < HEADS:
                B.plan(("o_ms", i - 4), 7)
        for b in range(4):
            B.plan(("attn_acc", b), b)
        B.plan(("ms", 1), 4)
        for c in range(NC_F):
            for hf in range(2):
                B.plan(("g", c, hf), 4 + hf), B.plan(("u", c, hf), 6 + hf)
        for b in range(4):
            B.plan(("ffn_acc", b), b)
        B.plan(("ms", 2), 4), B.plan("dt", 5), B.plan("acs", 6)
        for i in range(12):
            B.plan(("conv", i), 4 + i % 4)
        for g in range(GROUPS):
            B.plan(("xn", g, 0), 1), B.plan(("cb", g), 0), B.plan(("xn", g, 1), 2)
            B.plan(("z", g, 0), 0), B.plan(("state", g), 3)
            for half in range(2):
                for c in range(TT):
                    B.plan(("ab", g, half, c), 4 + 2 * half + c)
            B.plan(("z", g, 1), 3)
            for half in range(2):
                B.plan(("y", g, half), 1 + half)
        for g in range(GROUPS):
            B.plan(("y_ms", g), 4 + g)
        for b in range(4):
            B.plan(("ssd_acc", b), b)
        B.plan(("ms", 3), 4)
        for i in range(4):
            B.plan(("xnat", i), i)
        for i in range(4):
            B.plan(("hnat", i), 4 + i)
        B.plan("logits", 0), B.plan("rank", 1)
        dense_uses = list(B.count)

        J = Banks(full, free)
        for c in range(NC_F):
            J.plan(("g", c), c % 2), J.plan(("u", c), 2 + c % 2)
        J.plan(("acc", 0), 4), J.plan(("acc", 1), 5)
        J.plan("PT", 6), J.plan(("gather", 0), 6), J.plan(("gather", 1), 7)
        J.plan(("yt", 0), 7), J.plan(("yt", 1), 6)
        for i in range(4):
            J.plan(("sc", i), 7 - i % 2)
        USES = list(J.count)
        FULL0 = list(dense_uses)
        FULL0[6] += 1
        FULL0[7] += 1
        GATHERED = {("gather", 0), ("gather", 1)}

        def job_ready(eng, name, job):
            b, k = J.at[name]
            eng.wait_ge(full[b], job * USES[b] + (FULL0[b] + k + 1))

        def job_claim(eng, name, job):
            b, k = J.at[name]
            eng.wait_ge(free[b], job * USES[b] + (dense_uses[b] + k))

        def job_released(eng, name, job):
            b, k = J.at[name]
            eng.wait_ge(free[b], job * USES[b] + (dense_uses[b] + k + 1))

        landed = [sem(f"landed{s}") for s in range(RING)]
        down_done = sem("down_done")
        in_x, in_const, in_rows, in_misc, in_lam = (sem(n) for n in ("in_x", "in_const", "in_rows", "in_misc", "in_lam"))
        in_hankel, in_scratch, in_dt, in_router = sem("in_hankel"), sem("in_scratch"), sem("in_dt"), sem("in_router")
        out_done = sem("out_done")
        dve_step, act_step = sem("dve_step"), sem("act_step")
        relb_set = sem("relb_set")
        sq_ready = sem("sq_ready")
        rstd_ready = sem("rstd_ready")
        h_ready = sem("h_ready")
        gains_ready = sem("gains_ready")
        qk_sq, qk_rstd = sem("qk_sq"), sem("qk_rstd")
        lam_dot, lam_exp, lam_ready = sem("lam_dot"), sem("lam_exp"), sem("lam_ready")
        logit_ready, p_ready, attn_ready = sem("logit_ready"), sem("p_ready"), sem("attn_ready")
        o_sq, o_rstd = sem("o_sq"), sem("o_rstd")
        sp_abs, sp_ln, a_exp, da_ready, w0_arg, w0_ready = (sem(n) for n in (
            "sp_abs", "sp_ln", "a_exp", "da_ready", "w0_arg", "w0_ready"))
        conv_first, conv_sum, conv_out = sem("conv_first"), sem("conv_sum"), sem("conv_out")
        xw_ready, arg1_ready, dec_ready, m_ready, ce_ready = (sem(n) for n in (
            "xw_ready", "arg1_ready", "dec_ready", "m_ready", "ce_ready"))
        cbm_ready = sem("cbm_ready")
        z_silu, gated, y_sq, y_rstd, y_ready = (sem(n) for n in ("z_silu", "gated", "y_sq", "y_rstd", "y_ready"))
        top_diff, top_exp, sel_ready, flag_ready = (sem(n) for n in ("top_diff", "top_exp", "sel_ready", "flag_ready"))
        place_ready = sem("place_ready")
        hg_ready = sem("hg_ready")
        pt_ready = sem("pt_ready")
        yt_ready = sem("yt_ready")
        moe_done = sem("moe_done")

        def cols(w, c0):
            return w[:, c0:c0 + 512].rearrange("(k p) n -> p k n", p=P)

        def rws(w, t):
            return w[512 * t:512 * (t + 1), :].rearrange("(k p) n -> p k n", p=P)

        W_IN = ssd_w_in[0]
        SOURCE = {
            "attn_q": lambda t: cols(attn_w_in[0], 512 * t), "attn_k": lambda t: cols(attn_w_in[0], D + 512 * t),
            "attn_v": lambda t: cols(attn_w_in[0], 2 * D + 512 * t), "attn_out": lambda t: rws(attn_w_out[0], t),
            "ffn_gate": lambda t: cols(ffn_w_gate[0], 512 * t), "ffn_up": lambda t: cols(ffn_w_up[0], 512 * t),
            "ffn_down": lambda t: rws(ffn_w_down[0], t),
            "ssd_z": lambda t: cols(W_IN, 512 * t), "ssd_x": lambda t: cols(W_IN, DI + 512 * t),
            "ssd_b": lambda t: cols(W_IN, 2 * DI), "ssd_c": lambda t: cols(W_IN, 2 * DI + 512),
            "ssd_out": lambda t: rws(ssd_w_out[0], t),
        }

        def by_cols(slot):
            return ring[:, slot, :].rearrange("p (k n) -> p k n", k=KD)

        def by_rows(slot):
            return ring[:, slot, :].rearrange("p (k n) -> p k n", k=4)

        def view(kind, slot):
            return by_rows(slot) if kind.endswith("out") or kind.endswith("down") else by_cols(slot)

        def expert_source(kind, c, e):
            if kind == "down":
                w = moe_w_down.rearrange("o e (c k p) n -> (o e) c p k n", k=4, p=P)
                return w[bass.ds(e, 1), c].rearrange("a p k n -> (a p) k n")
            w = (moe_w_gate if kind == "gate" else moe_w_up).rearrange("o e (k p) n -> (o e) p k n", p=P)
            return w[bass.ds(e, 1), :, :, 512 * c:512 * (c + 1)].rearrange("a p k n -> (a p) k n")

        block = ctx.enter_context(nc.Block())

        def dense_tile_used(eng, tile):
            kind, t = tile
            if kind in ("attn_q", "attn_k"):
                B.ready(eng, ("qk", 4 * t + 2 * (kind == "attn_k") + 1))
            elif kind == "attn_v":
                B.ready(eng, ("v", 2 * t + 1))
            elif kind in ("ffn_gate", "ffn_up"):
                B.ready(eng, (kind[4], t, 1))
            elif kind in ("ssd_b", "ssd_c", "ssd_x"):
                B.ready(eng, ("conv", 2 * {"ssd_b": 0, "ssd_c": 1, "ssd_x": 2 + t}[kind] + 1))
            elif kind == "ssd_z":
                B.ready(eng, ("z", t, 1))
            else:
                base, layer, last_t = {"attn_out": (0, "attn_acc", 1), "ffn_down": (1, "ffn_acc", NC_F - 1),
                                       "ssd_out": (NC_F, "ssd_acc", 3)}[kind]
                if t == last_t:
                    B.ready(eng, (layer, 3))
                else:
                    eng.wait_ge(down_done, base + t + 1)
        DENSE_DOWNS = NC_F + 3

        def job_tile_used(eng, tile, job, before):
            kind, c = tile
            if kind == "down" and c < NC_F - 1:
                eng.wait_ge(down_done, job * (NC_F - 1) + (DENSE_DOWNS + c + 1 - before * (NC_F - 1)))
                return
            b, k = J.at[("acc", 1)] if kind == "down" else J.at[(kind[0], c)]
            eng.wait_ge(full[b], job * USES[b] + (FULL0[b] + k + 1 - before * USES[b]))

        @block.sync
        def _(sp):
            sp.dma_start(xin[:, :, :], x[0].rearrange("(a p) n -> p a n", p=P)).then_inc(in_x, 16)
            for n, (kind, t) in enumerate(DT):
                slot = n % DENSE_RING
                if n >= DENSE_RING:
                    dense_tile_used(sp, DT[n - DENSE_RING])
                sp.dma_start(view(kind, slot), SOURCE[kind](t)).then_inc(landed[slot], 16)

            def job_tiles(e, job, first):
                for m, (kind, c) in enumerate(ET):
                    slot = m % RING
                    if not first:
                        job_tile_used(sp, ET[m - RING], job, 1 if m < RING else 0)
                    elif m >= RING:
                        job_tile_used(sp, ET[m - RING], 0, 0)
                    elif slot == RING - 1:
                        B.ready(sp, ("y_ms", GROUPS - 1))
                    else:
                        dense_tile_used(sp, DT[max(n for n in range(ND) if n % DENSE_RING == slot)])
                    sp.dma_start(view(kind, slot), expert_source(kind, c, e)).then_inc(landed[slot], 16)

            job_tiles(0, 0, True)
            with sp.Fori(1, E) as e:
                job_tiles(e, e, False)
            sp.wait_ge(flag_ready, 1)
            more = sp.value_load(flag[0:1, 0:1], min_val=0, max_val=1)
            with sp.If(more > 0):
                with sp.Fori(1, PASSES) as p:
                    with sp.Fori(0, E) as e:
                        job_tiles(e, p * E + e, False)
            sp.wait_ge(moe_done, 1)
            sp.dma_start(out[0].rearrange("(a p) n -> p a n", p=P), xnat[:, :, :]).then_inc(out_done, 16)
            sp.wait_ge(out_done, 16)

        @block.gpsimd
        def _(pool):
            B.released(pool, "ubias")
            pool.dma_start(scratch[:, 0:NDIST], ubias[:, :]).then_inc(in_scratch, 16)
            pool.wait_ge(in_scratch, 16)
            pool.dma_start(hankel[:, :, :],
                           bass.AP(scratch.tensor, 0, [[1, P], [512, HEADS], [1, T]])).then_inc(in_hankel, 16)

            B.released(pool, ("ffn_acc", 3))
            pool.dma_start(wdt[:, :, :], W_IN[:, 2 * DI + 2 * GROUPS * NSTATE:]
                           .rearrange("(k p) n -> p k n", p=P)).then_inc(in_dt, 16)
            pool.dma_start(alog[:, 0, :], ssd_a_log[0:1, :].broadcast_to([P, SH])).then_inc(in_dt, 16)
            pool.dma_start(alog[:, 1, :], ssd_dt_bias[0:1, :].broadcast_to([P, SH])).then_inc(in_dt, 16)
            pool.wait_ge(w0_ready, 1)
            for g in range(GROUPS):
                B.released(pool, ("xn", g, 0))
                if g >= 2:
                    B.ready(pool, ("state", g - 2))
                nc.gpsimd.tensor_tensor(xw[:, g % 2, :].rearrange("p (h d) -> p h d", d=HD),
                                        xd[:, g % 2, 0:512].rearrange("p (h d) -> p h d", d=HD),
                                        w0[:, g * HPG:(g + 1) * HPG].unsqueeze(2).broadcast_to([P, HPG, HD]),
                                        ALU.mult).then_inc(xw_ready, 1)
                for half in range(2):
                    B.released(pool, ("ab", g, half, 1))
                    nc.gpsimd.tensor_tensor(eC[:, half, :].rearrange("p (h l) -> p h l", l=P),
                                            eC[:, half, :].rearrange("p (h l) -> p h l", l=P),
                                            CT[:, g, P:T].unsqueeze(1).broadcast_to([P, 4, P]),
                                            ALU.mult).then_inc(ce_ready, 1)
            B.released(pool, ("ssd_acc", 3))
            pool.dma_start(router[:, :, :], moe_router[0].rearrange("(k p) n -> p k n", p=P)).then_inc(in_router, 16)

        @block.tensor
        def _(pe):
            def mm(o, lhsT, rhs, start, stop, shared=False):
                return nc.tensor.matmul(o, lhsT, rhs, start=start, stop=stop, skip_group_check=shared)

            def arrive(tile):
                n = DENSE[tile]
                pe.wait_ge(landed[n % DENSE_RING], 16 * (n // DENSE_RING + 1))
                return view(tile[0], n % DENSE_RING)

            pe.wait_ge(in_const, 16)
            pe.wait_ge(in_rows, 16 * N_ROWS)
            B.finish(nc.tensor.transpose(bank[4][:, 0:96], rows[0:96, 0, :], cst[0:96, 0:96]), "rowsA")
            B.finish(nc.tensor.transpose(bank[5][:, 0:ROWS_B], rows[0:ROWS_B, 1, :], cst[0:ROWS_B, 0:ROWS_B]), "rowsB")
            pe.wait_ge(in_misc, 16 * N_MISC)
            pe.wait_ge(relb_set, 2)
            B.finish(mm(bank[6][:, 0:16], C("odd_even", SH), small[0:SH, 0:16], True, True), "dcol")
            B.finish(mm(bank[7][0:HEADS, 0:NDIST], relb[:, :], onehot[:, :], True, True), "ubias")

            pe.wait_ge(in_x, 16)
            for i in range(4):
                B.claim(pe, ("x", i))
                for j in range(2):
                    for tt in range(TT):
                        last = nc.tensor.transpose(bank[4 + i][:, j * T + tt * P:j * T + (tt + 1) * P],
                                                   xin[:, tt, (2 * i + j) * P:(2 * i + j + 1) * P], C("ident"))
                B.finish(last, ("x", i))

            def mean_square(n):
                B.claim(pe, ("ms", n))
                for k in range(KD):
                    if k % 2 == 0:
                        pe.wait_ge(sq_ready, 4 * n + k // 2 + 1)
                    last = mm(bank[4][:, 0:T], C("mean_d"), hT[:, k, :], k == 0, k == KD - 1)
                B.finish(last, ("ms", n))

            def project(o, w, col, fresh=None):
                for j in range(2):
                    for k in range(KD):
                        if fresh is not None and j == 0:
                            pe.wait_ge(h_ready, KD * fresh + k + 1)
                        last = mm(o[:, j * T:(j + 1) * T], w[:, k, col + j * P:col + (j + 1) * P], hT[:, k, :],
                                  k == 0, k == KD - 1)
                return last

            def down(acc, w, act, first, last_tile):
                for m in range(KD):
                    b = m // 2
                    if first and m % 2 == 0:
                        B.claim(pe, (acc, b))
                    for r in range(4):
                        last = mm(bank[b][:, (m % 2) * T:(m % 2 + 1) * T], w[:, r, m * P:(m + 1) * P], act(r),
                                  first and m % 2 == 0 and r == 0, last_tile and m % 2 == 1 and r == 3, shared=True)
                    if last_tile and m % 2 == 1:
                        B.finish(last, (acc, b))
                if not last_tile:
                    last.then_inc(down_done, 1)

            mean_square(0)
            for i in range(9):
                if i < 8:
                    t, hf = i // 2, i % 2
                    w = arrive(("attn_q" if t % 2 == 0 else "attn_k", t // 2))
                    B.claim(pe, ("qk", i))
                    B.finish(project(bank[i % 4], w, 256 * hf, 0 if i == 0 else None), ("qk", i))
                if i:
                    B.claim(pe, ("qk_ms", i - 1))
                    pe.wait_ge(qk_sq, i)
                    last = mm(bank[4 + (i - 1) % 2][:, :], C("mean_hd"), sqb[:, (i - 1) % 2, :], True, True)
                    B.finish(last, ("qk_ms", i - 1))
            for i in range(4):
                t, tt = i // 2, i % 2
                w = arrive(("attn_v", t))
                B.claim(pe, ("v", i))
                for k in range(KD):
                    last = mm(bank[6 + i % 2][:, :], hT[:, k, tt * P:(tt + 1) * P], w[:, k, :], k == 0, k == KD - 1)
                B.finish(last, ("v", i))
            pe.wait_ge(in_hankel, 16)
            for i in range(4):
                B.claim(pe, ("bias", i))
                last = mm(bank[i][:, :], C("anti"), hankel[:, 2 * i:2 * i + 2, :], True, True)
                B.finish(last, ("bias", i))
            for i in range(8):
                B.released(pe, ("qk", i))
            for i in range(4):
                B.released(pe, ("v", i))
            for i in range(HEADS + 4):
                if i < HEADS:
                    for m in range(2):
                        B.claim(pe, ("s", i, m))
                        b = bank[2 * m + i % 2]
                        q, k = qT[HD * m:HD * (m + 1), i, :], kT[HD * m:HD * (m + 1), i, :]
                        mm(b[:, 0:P], q[:, 0:P], k[:, 0:P], True, True)
                        B.finish(mm(b[:, P:P + T], q[:, P:T], k[:, :], True, True), ("s", i, m))
                h = i - 2
                if 0 <= h < HEADS:
                    B.claim(pe, ("at", h))
                    pe.wait_ge(attn_ready, h + 1)
                    for j in range(3):
                        last = nc.tensor.transpose(bank[4][:, j * P:(j + 1) * P], A[:, h % 2, j * P:(j + 1) * P],
                                                   C("ident"))
                    B.finish(last, ("at", h))
                h = i - 3
                if 0 <= h < HEADS:
                    B.claim(pe, ("o", h))
                    B.released(pe, ("at", h))
                    b = bank[5 + h % 2]
                    mm(b[:, 0:T], V[:, 0, h * P:(h + 1) * P], AT[:, h % 2, 0:T], True, False)
                    B.finish(mm(b[:, P:T], V[:, 1, h * P:(h + 1) * P], AT[:, h % 2, T:T + P], False, True), ("o", h))
                h = i - 4
                if 0 <= h < HEADS:
                    B.claim(pe, ("o_ms", h))
                    pe.wait_ge(o_sq, h + 1)
                    B.finish(mm(bank[7][:, 0:T], C("mean_v"), sqo[:, h % 2, :], True, True), ("o_ms", h))
            for t in range(2):
                w = arrive(("attn_out", t))
                for h in range(4 * t, 4 * t + 4):
                    B.released(pe, ("o", h))
                down("attn_acc", w, lambda r, t=t: oT[:, 4 * t + r, :], t == 0, t == 1)

            mean_square(1)
            for c in range(NC_F + 1):
                if c < NC_F:
                    for hf in range(2):
                        for kind, b in (("gate", 4 + hf), ("up", 6 + hf)):
                            w = arrive(("ffn_" + kind, c))
                            B.claim(pe, (kind[0], c, hf))
                            fresh = 1 if c == 0 and hf == 0 and kind == "gate" else None
                            B.finish(project(bank[b], w, 256 * hf, fresh), (kind[0], c, hf))
                if c:
                    w = arrive(("ffn_down", c - 1))
                    for hf in range(2):
                        B.released(pe, ("u", c - 1, hf))
                    down("ffn_acc", w, lambda r, c=c: hid[:, (c - 1) % 2, r, :], c == 1, c == NC_F)

            mean_square(2)
            pe.wait_ge(in_dt, 48)
            B.claim(pe, "dt")
            for k in range(KD):
                pe.wait_ge(h_ready, KD * 2 + k + 1)
            for tt in range(TT):
                for k in range(KD):
                    last = mm(bank[5][:, tt * SH:(tt + 1) * SH], hT[:, k, tt * P:(tt + 1) * P], wdt[:, k, :],
                              k == 0, k == KD - 1)
            B.finish(last, "dt")
            for i in range(12):
                t, hf = i // 2, i % 2
                w = arrive([("ssd_b", 0), ("ssd_c", 0), ("ssd_x", 0), ("ssd_x", 1), ("ssd_x", 2), ("ssd_x", 3)][t])
                B.claim(pe, ("conv", i))
                B.finish(project(bank[4 + i % 4], w, 256 * hf), ("conv", i))
                if i == 1:
                    B.claim(pe, "acs")
                    pe.wait_ge(da_ready, 1)
                    for c in range(TT):
                        mm(bank[6][:, c * SH:(c + 1) * SH], C("upto"), da[:, c, :], True, True)
                    B.finish(mm(bank[6][:, 64:64 + SH], C("ones"), da[:, 0, :], True, True), "acs")

            def project_z(g, hf, b):
                w = arrive(("ssd_z", g))
                B.claim(pe, ("z", g, hf))
                B.finish(project(bank[b], w, 256 * hf), ("z", g, hf))

            for g in range(GROUPS):
                pe.wait_ge(conv_out, 4 + 2 * g + 2)
                for c in range(TT):
                    B.claim(pe, ("xn", g, c))
                    for b in range(4):
                        last = nc.tensor.transpose(bank[1 + c][:, b * P:(b + 1) * P],
                                                   xsT[:, 4 * g + b, c * P:(c + 1) * P], C("ident"))
                    B.finish(last, ("xn", g, c))
                    if c == 0:
                        B.claim(pe, ("cb", g))
                        for cc in range(TT):
                            mm(bank[0][:, cc * P:(cc + 1) * P], BT[:, g, cc * P:(cc + 1) * P],
                               CT[:, g, cc * P:(cc + 1) * P], True, True)
                        B.finish(nc.tensor.transpose(bank[0][:, T:T + P], BT[:, g, 0:P], C("ident")), ("cb", g))
                project_z(g, 0, 0)
                B.claim(pe, ("state", g))
                pe.wait_ge(xw_ready, g + 1)
                B.finish(mm(bank[3][:, :], Bn[:, g % 2, :], xw[:, g % 2, :], True, True), ("state", g))
                for half in range(2):
                    for c in range(TT):
                        B.claim(pe, ("ab", g, half, c))
                        for q in range(4):
                            h = g * HPG + 4 * half + q
                            last = mm(bank[4 + 2 * half + c][:, q * P:(q + 1) * P],
                                      da[:, c, h:h + 1].broadcast_to([P, P]), C("upto"), True, True)
                        B.finish(last, ("ab", g, half, c))
                project_z(g, 1, 3)
                B.released(pe, ("xn", g, 1))
                B.released(pe, ("state", g))
                for half in range(2):
                    B.claim(pe, ("y", g, half))
                    pe.wait_ge(m_ready, 4 * g + 2 * half + 2)
                    pe.wait_ge(ce_ready, 2 * g + half + 1)
                    for q in range(4):
                        o = bank[1 + half][HD * (q % 2):HD * (q % 2 + 1), (q // 2) * T:(q // 2 + 1) * T]
                        ch = (4 * half + q) * HD
                        mm(o[:, 0:P], xd[:, g % 2, ch:ch + HD], dec[:, 2 * half, q * P:(q + 1) * P], True, True)
                        mm(o[:, P:T], xd[:, g % 2, 512 + ch:512 + ch + HD], dec[:, 2 * half + 1, q * P:(q + 1) * P],
                           True, False)
                        last = mm(o[:, P:T], stS[:, g % 2, ch:ch + HD], eC[:, half, q * P:(q + 1) * P], False, True)
                    B.finish(last, ("y", g, half))
            for g in range(GROUPS):
                B.claim(pe, ("y_ms", g))
                pe.wait_ge(y_sq, g + 1)
                for b in range(4):
                    last = mm(bank[4 + g][:, 0:T], C("mean_g"), zr[:, 4 * g + b, :], b == 0, b == 3)
                B.finish(last, ("y_ms", g))
            for g in range(GROUPS):
                w = arrive(("ssd_out", g))
                pe.wait_ge(y_ready, g + 1)
                down("ssd_acc", w, lambda r, g=g: xsT[:, 4 * g + r, :], g == 0, g == 3)

            mean_square(3)
            for i in range(4):
                tt, half = i // 2, i % 2
                B.claim(pe, ("xnat", i))
                for b in range(4):
                    last = nc.tensor.transpose(bank[i][:, b * P:(b + 1) * P], xT[:, 4 * half + b, tt * P:(tt + 1) * P],
                                               C("ident"))
                B.finish(last, ("xnat", i))
            for k in range(KD):
                pe.wait_ge(h_ready, KD * 3 + k + 1)
            pe.wait_ge(in_router, 16)
            B.claim(pe, "logits")
            for tt in range(TT):
                for k in range(KD):
                    last = mm(bank[0][:, tt * E:(tt + 1) * E], hT[:, k, tt * P:(tt + 1) * P], router[:, k, :],
                              k == 0, k == KD - 1)
            B.finish(last, "logits")
            for i in range(4):
                tt, half = i // 2, i % 2
                B.claim(pe, ("hnat", i))
                for b in range(4):
                    last = nc.tensor.transpose(bank[4 + i][:, b * P:(b + 1) * P],
                                               hT[:, 4 * half + b, tt * P:(tt + 1) * P], C("ident"))
                B.finish(last, ("hnat", i))
            B.claim(pe, "rank")
            pe.wait_ge(sel_ready, 1)
            sel = oh[:, 2, :]
            mm(bank[1][:, 0:E], C("before"), sel[:, 0:E], True, True)
            mm(bank[1][:, E:2 * E], C("ones"), sel[:, 0:E], True, False)
            mm(bank[1][:, E:2 * E], C("before"), sel[:, E:2 * E], False, True)
            mm(bank[1][:, 2 * E:3 * E], C("ones"), sel[:, 0:E], True, False)
            B.finish(mm(bank[1][:, 2 * E:3 * E], C("ones"), sel[:, E:2 * E], False, True), "rank")

            def gather(job):
                pe.wait_ge(place_ready, job + 1)
                for half in range(2):
                    for b in range(4):
                        d = 4 * half + b
                        for tt in range(TT):
                            last = mm(bank[6 + half][:, b * SLOTS:(b + 1) * SLOTS], hnat[:, tt, d * P:(d + 1) * P],
                                      Pm[:, tt, :], tt == 0, tt == 1)
                    last.then_inc(full[6 + half], 1)

            for i in range(4):
                B.released(pe, ("hnat", i))
            gather(0)

            def job_body(job):
                def arrived(tile):
                    m = EXPERT[tile]
                    s = m % RING
                    pe.wait_ge(landed[s], job * (16 * NE // RING) + 16 * (dense_in_slot[s] + m // RING + 1))
                    return view(tile[0], s)

                def down_chunk(c):
                    w = arrived(("down", c))
                    job_released(pe, ("u", c), job)
                    for m in range(KD):
                        b = 4 + m // 4
                        if c == 0 and m % 4 == 0:
                            job_claim(pe, ("acc", m // 4), job)
                        for r in range(4):
                            last = mm(bank[b][:, (m % 4) * SLOTS:(m % 4 + 1) * SLOTS], w[:, r, m * P:(m + 1) * P],
                                      ehid[:, c % 2, r, :], c == 0 and m % 4 == 0 and r == 0,
                                      c == NC_F - 1 and m % 4 == 3 and r == 3, shared=True)
                        if c == NC_F - 1 and m % 4 == 3:
                            last.then_inc(full[b], 1)
                    if c < NC_F - 1:
                        last.then_inc(down_done, 1)

                pe.wait_ge(hg_ready, job * 2 + 2)
                for c in range(NC_F):
                    for kind, b in (("gate", c % 2), ("up", 2 + c % 2)):
                        w = arrived((kind, c))
                        job_claim(pe, (kind[0], c), job)
                        for j in range(4):
                            for k in range(KD):
                                last = mm(bank[b][:, j * SLOTS:(j + 1) * SLOTS], w[:, k, j * P:(j + 1) * P],
                                          hTg[:, k, :], k == 0, k == KD - 1)
                        last.then_inc(full[b], 1)
                    if c == 0:
                        pe.wait_ge(free[6], job * 2 + dense_uses[6])
                        for tt in range(TT):
                            last = nc.tensor.transpose(bank[6][0:SLOTS, tt * P:(tt + 1) * P], Pm[:, tt, :], C("ident"))
                        last.then_inc(full[6], 1)
                    else:
                        down_chunk(c - 1)
                pe.wait_ge(pt_ready, job + 1)
                pe.wait_ge(free[7], job * 2 + dense_uses[7])
                gather(job + 1)
                down_chunk(NC_F - 1)
                pe.wait_ge(hg_ready, job * 2 + 4)
                for half in range(2):
                    job_released(pe, ("acc", half), job)
                    for b in range(4):
                        last = nc.tensor.transpose(bank[7 - half][0:SLOTS, b * P:(b + 1) * P], ysb[:, 4 * half + b, :],
                                                   C("ident"))
                    last.then_inc(full[7 - half], 1)
                for i in range(4):
                    tt, half = i // 2, i % 2
                    if i < 2:
                        pe.wait_ge(yt_ready, job * 2 + 2)
                    else:
                        pe.wait_ge(free[7 - i % 2], job * 2 + (dense_uses[7 - i % 2] + 1))
                    mm(bank[7 - i % 2][:, :], PT[0:SLOTS, tt, :], ynat[0:SLOTS, half * 512:(half + 1) * 512],
                       True, True).then_inc(full[7 - i % 2], 1)

            with pe.Fori(0, E) as job:
                job_body(job)
            pe.wait_ge(flag_ready, 1)
            more = pe.value_load(flag[0:1, 0:1], min_val=0, max_val=1)
            with pe.If(more > 0):
                with pe.Fori(E, JOBS) as job:
                    job_body(job)

        @block.scalar
        def _(act):
            chain = Chain(act, act_step)
            fn = nc.scalar.activation

            act.dma_start(cst[:, :], const).then_inc(in_const, 16)
            for src, part, r0, c0 in (
                    (ssd_conv_w[0].rearrange("j (b p) -> (j b) p", p=P), 0, 0, 0),
                    (norm_mix.rearrange("i (b p) -> (i b) p", p=P), 1, NORM_MIX, 0),
                    (norm_ffn.rearrange("i (b p) -> (i b) p", p=P), 1, NORM_FFN, 0),
                    (ssd_conv_b[0].rearrange("(b p) -> b p", p=P), 1, CONV_B, 0),
                    (ssd_norm[0].rearrange("(b p) -> b p", p=P), 1, SSD_NORM, 0),
                    (attn_subln, 1, SUBLN, 0),
                    (attn_q_gain, 1, Q_GAIN, 0), (attn_q_gain, 1, Q_GAIN, HD),
                    (attn_k_gain, 1, K_GAIN, 0), (attn_k_gain, 1, K_GAIN, HD)):
                n, wd = src.shape
                act.dma_start(rows[r0:r0 + n, part, c0:c0 + wd], src).then_inc(in_rows, 16)
            act.dma_start(small[0:SH, 16:17], ssd_d[0].rearrange("(n a) -> n a", a=1)).then_inc(in_misc, 16)
            act.dma_start(relb[0:BUCKETS, :], rel_bias).then_inc(in_misc, 16)
            act.dma_start(onehot[:, :], hot).then_inc(in_misc, 16)
            act.dma_start(lam_in, attn_lambda.rearrange("o a d -> o (a d)").broadcast_to([P, 4 * HD])).then_inc(in_lam, 16)

            B.ready(act, "rowsA")
            B.release(nc.scalar.copy(colA[:, :], bank[4][:, 0:96]), "rowsA")
            B.ready(act, "rowsB")
            B.release(nc.scalar.copy(colB[:, 0:ROWS_B], bank[5][:, 0:ROWS_B]), "rowsB")
            B.ready(act, "dcol")
            B.release(nc.scalar.copy(dcol[:, :], bank[6][:, 0:16]), "dcol")
            B.ready(act, "ubias")
            B.release(nc.scalar.copy(ubias[:, :], bank[7][0:HEADS, 0:NDIST]), "ubias")

            def norm(n):
                for b in range(4):
                    B.released(act, ((("x", "attn_acc", "ffn_acc", "ssd_acc")[n]), b))
                    fn(hT[:, 2 * b:2 * b + 2, :], xT[:, 2 * b:2 * b + 2, :], ACT.Square).then_inc(sq_ready, 1)
                B.ready(act, ("ms", n))
                B.release(fn(rstd[:, :], bank[4][:, 0:T], ACT.Ln, bias=C("eps")), ("ms", n))
                B.released(act, ("ms", n))
                fn(rstd[:, :], rstd[:, :], ACT.Exp, scale=-0.5).then_inc(rstd_ready, 1)

            norm(0)
            act.wait_ge(lam_dot, 2)
            fn(small[:, 22:24], small[:, 20:22], ACT.Exp).then_inc(lam_exp, 1)
            for i in range(9):
                if i < 8:
                    B.ready(act, ("qk", i))
                    if i >= 2:
                        B.ready(act, ("qk_ms", i - 2))
                    fn(sqb[:, i % 2, :], bank[i % 4][:, :], ACT.Square).then_inc(qk_sq, 1)
                if i:
                    k = i - 1
                    B.ready(act, ("qk_ms", k))
                    if k >= 2:
                        B.released(act, ("qk", k - 2))
                    B.release(fn(rq[:, k % 2, :], bank[4 + k % 2][:, :], ACT.Ln, bias=C("eps")), ("qk_ms", k))
                    B.released(act, ("qk_ms", k))
                    fn(rq[:, k % 2, :], rq[:, k % 2, :], ACT.Exp, scale=-0.5).then_inc(qk_rstd, 1)
            for i in range(4):
                t, tt = i // 2, i % 2
                B.ready(act, ("v", i))
                B.release(nc.scalar.copy(V[:, tt, t * 512:(t + 1) * 512], bank[6 + i % 2][:, :]), ("v", i))
            for i in range(4):
                B.ready(act, ("bias", i))
                B.release(nc.scalar.copy(bias[:, 2 * i:2 * i + 2, :], bank[i][:, :]), ("bias", i))
            for i in range(HEADS + 4):
                if i < HEADS:
                    act.wait_ge(logit_ready, i + 1)
                    for m in range(2):
                        for qb in range(2):
                            a, n = m * 384 + qb * P, P + qb * P
                            j = 2 * m + qb
                            last = fn(L[:, i % 2, a:a + n], L[:, i % 2, a:a + n], ACT.Exp,
                                      bias=st[:, i % 2, 4 + j:5 + j], accum_out=st[:, i % 2, 8 + j:9 + j])
                    last.then_inc(p_ready, 1)
                h = i - 2
                if 0 <= h < HEADS:
                    B.ready(act, ("at", h))
                    if h >= 2:
                        B.ready(act, ("o", h - 2))
                    B.release(nc.scalar.copy(AT[:, h % 2, :], bank[4][:, 0:384]), ("at", h))
                h = i - 3
                if 0 <= h < HEADS:
                    B.ready(act, ("o", h))
                    if h >= 2:
                        B.ready(act, ("o_ms", h - 2))
                    fn(sqo[:, h % 2, :], bank[5 + h % 2][:, 0:T], ACT.Square).then_inc(o_sq, 1)
                h = i - 4
                if 0 <= h < HEADS:
                    B.ready(act, ("o_ms", h))
                    if h >= 2:
                        B.released(act, ("o", h - 2))
                    B.release(fn(ro[:, h % 2, :], bank[7][:, 0:T], ACT.Ln, bias=C("eps")), ("o_ms", h))
                    B.released(act, ("o_ms", h))
                    fn(ro[:, h % 2, :], ro[:, h % 2, :], ACT.Exp, scale=-0.5).then_inc(o_rstd, 1)

            norm(1)
            units = [(c, hf) for c in range(NC_F) for hf in range(2)]
            for i, (c, hf) in enumerate(units):
                B.ready(act, ("g", c, hf))
                if i >= 4:
                    B.released(act, ("u",) + units[i - 4])
                B.release(fn(sg[:, i % 4, :], bank[4 + hf][:, :], ACT.Silu), ("g", c, hf))

            norm(2)
            act.wait_ge(in_dt, 48)
            fn(alog[:, 0, :], alog[:, 0, :], ACT.Exp).then_inc(a_exp, 1)
            act.wait_ge(sp_abs, 1)
            chain.link(fn(dta[:, :, :], dta[:, :, :], ACT.Exp, scale=-1.0))
            fn(dta[:, :, :], dta[:, :, :], ACT.Ln, bias=C("one")).then_inc(sp_ln, 1)
            act.wait_ge(w0_arg, 1)
            fn(w0, w0, ACT.Exp).then_inc(w0_ready, 1)
            for i in range(13):
                if i < 12:
                    B.ready(act, ("conv", i))
                    if i >= 2:
                        act.wait_ge(conv_out, i - 1)
                    for j in range(2):
                        blk = conv_block(i) + j
                        last = fn(cvb[:, i % 2, j * T:(j + 1) * T], bank[4 + i % 4][:, j * T:(j + 1) * T], ACT.Identity,
                                  bias=colB[:, CONV_B + blk:CONV_B + blk + 1], scale=colA[:, 72 + blk:73 + blk])
                    last.then_inc(conv_first, 1)
                if i:
                    k = i - 1
                    B.released(act, ("conv", k))
                    dest = BT if k < 2 else CT if k < 4 else xsT
                    r = 2 * k - (0 if k < 2 else 4 if k < 4 else 8)
                    fn(dest[:, r:r + 2, :], cvb[:, k % 2, :], ACT.Silu).then_inc(conv_out, 1)
            for g in range(GROUPS):
                B.ready(act, ("z", g, 0))
                B.release(nc.scalar.copy(zr[:, 4 * g:4 * g + 2, :], bank[0][:, :]), ("z", g, 0))
                B.ready(act, ("state", g))
                if g >= 2:
                    B.ready(act, ("y", g - 2, 1))
                B.release(nc.scalar.copy(stS[:, g % 2, :], bank[3][:, :]), ("state", g))
                for half in range(2):
                    for c in range(TT):
                        if c == 0:
                            B.released(act, ("ab", g, half, 0))
                        else:
                            act.wait_ge(arg1_ready, 2 * g + half + 1)
                        fn(dec[:, 2 * half + c, :], dec[:, 2 * half + c, :], ACT.Exp).then_inc(dec_ready, 1)
                    B.ready(act, ("ab", g, half, 1))
                    if g:
                        B.ready(act, ("y", g - 1, half))
                    B.release(fn(eC[:, half, :], bank[4 + 2 * half + 1][:, :], ACT.Exp), ("ab", g, half, 1))
                B.ready(act, ("z", g, 1))
                B.release(nc.scalar.copy(zr[:, 4 * g + 2:4 * g + 4, :], bank[3][:, :]), ("z", g, 1))
            for g in range(GROUPS):
                for hf in range(2):
                    B.released(act, ("z", g, hf))
                fn(zr[:, 4 * g:4 * g + 4, :], zr[:, 4 * g:4 * g + 4, :], ACT.Silu).then_inc(z_silu, 1)
            for g in range(GROUPS):
                act.wait_ge(gated, g + 1)
                fn(zr[:, 4 * g:4 * g + 4, :], xsT[:, 4 * g:4 * g + 4, :], ACT.Square).then_inc(y_sq, 1)
            for g in range(GROUPS):
                B.ready(act, ("y_ms", g))
                if g >= 2:
                    act.wait_ge(y_ready, g - 1)
                B.release(fn(rg[:, g % 2, :], bank[4 + g][:, 0:T], ACT.Ln, bias=C("eps")), ("y_ms", g))
                B.released(act, ("y_ms", g))
                fn(rg[:, g % 2, :], rg[:, g % 2, :], ACT.Exp, scale=-0.5).then_inc(y_rstd, 1)

            norm(3)
            for i in range(4):
                B.ready(act, ("xnat", i))
                B.release(nc.scalar.copy(xnat[:, i // 2, (i % 2) * 512:(i % 2 + 1) * 512], bank[i][:, :]), ("xnat", i))
            for i in range(4):
                B.ready(act, ("hnat", i))
                B.release(nc.scalar.copy(hnat[:, i // 2, (i % 2) * 512:(i % 2 + 1) * 512], bank[4 + i][:, :]), ("hnat", i))
            act.wait_ge(top_diff, 1)
            fn(tw[:, 1, 0:TT], tw[:, 0, 0:TT], ACT.Exp).then_inc(top_exp, 1)

            def gathered(job_full):
                for half in range(2):
                    b = 6 + half
                    act.wait_ge(full[b], job_full(b))
                    nc.scalar.copy(hTg[:, 4 * half:4 * half + 4, :], bank[b][:, 0:4 * SLOTS]).then_inc(hg_ready, 1)

            gathered(lambda b: FULL0[b])

            def job_body(job):
                for c in range(NC_F):
                    job_ready(act, ("g", c), job)
                    act.wait_ge(free[2 + c % 2], job * USES[2 + c % 2] + (dense_uses[2 + c % 2] + c // 2))
                    fn(esg[:, c % 2, :], bank[c % 2][:, 0:4 * SLOTS], ACT.Silu).then_inc(free[c % 2], 1)
                    if c == 0:
                        job_ready(act, "PT", job)
                        nc.scalar.copy(PT[0:SLOTS, :, :], bank[6][0:SLOTS, 0:T]).then_inc(pt_ready, 1)
                gathered(lambda b: job * USES[b] + (FULL0[b] + J.at[("gather", b - 6)][1] + 1))
                for half in range(2):
                    job_ready(act, ("acc", half), job)
                    nc.scalar.copy(ysb[:, 4 * half:4 * half + 4, :], bank[4 + half][:, 0:4 * SLOTS])\
                        .then_inc(free[4 + half], 1)
                for half in range(2):
                    job_ready(act, ("yt", half), job)
                    nc.scalar.copy(ynat[0:SLOTS, half * 512:(half + 1) * 512], bank[7 - half][0:SLOTS, :])\
                        .then_inc(yt_ready, 1)

            with act.Fori(0, E) as job:
                job_body(job)
            act.wait_ge(flag_ready, 1)
            more = act.value_load(flag[0:1, 0:1], min_val=0, max_val=1)
            with act.If(more > 0):
                with act.Fori(E, JOBS) as job:
                    job_body(job)

        @block.vector
        def _(dve):
            chain = Chain(dve, dve_step)
            link = chain.link
            V_ = nc.vector
            tt_, ts_, stt = V_.tensor_tensor, V_.tensor_scalar, V_.scalar_tensor_tensor

            dve.wait_ge(in_const, 16)
            dve.wait_ge(in_misc, 16 * N_MISC)
            V_.memset(relb[BUCKETS:BUCKETS + 1, :], MASKED).then_inc(relb_set, 1)
            ts_(small[0:SH, 0:16], C("pair_of", SH), small[0:SH, 16:17], None, ALU.mult).then_inc(relb_set, 1)
            dve.wait_ge(in_lam, 16)
            for j in range(2):
                V_.tensor_tensor_reduce(lam_in[:, 2 * j * HD:(2 * j + 1) * HD], lam_in[:, 2 * j * HD:(2 * j + 1) * HD],
                                        lam_in[:, (2 * j + 1) * HD:(2 * j + 2) * HD], 1.0, 0.0, ALU.mult, ALU.add,
                                        small[:, 20 + j:21 + j]).then_inc(lam_dot, 1)
            B.released(dve, "rowsB")
            link(ts_(small[:, 25:26], colB[:, Q_GAIN:Q_GAIN + 1], HD ** -0.5, None, ALU.mult))
            link(ts_(small[:, 26:27], colB[:, SUBLN:SUBLN + 1], 1.0 - LAMBDA_INIT, None, ALU.mult))
            for i in range(4):
                B.ready(dve, ("x", i))
                B.release(V_.tensor_copy(xT[:, 2 * i:2 * i + 2, :], bank[4 + i][:, :]), ("x", i))

            def norm(n):
                col = (NORM_MIX, NORM_FFN)[n % 2] + KD * (n // 2)
                dve.wait_ge(rstd_ready, n + 1)
                for k in range(KD):
                    stt(out=hT[:, k, :], in0=xT[:, k, :], scalar=colB[:, col + k:col + k + 1], in1=rstd[:, :],
                        op0=ALU.mult, op1=ALU.mult).then_inc(h_ready, 1)

            def residual(acc):
                for b in range(4):
                    B.ready(dve, (acc, b))
                    B.release(tt_(xT[:, 2 * b:2 * b + 2, :], xT[:, 2 * b:2 * b + 2, :],
                                  bank[b][:, :].rearrange("p (a t) -> p a t", a=2), ALU.add), (acc, b))

            norm(0)
            dve.wait_ge(lam_exp, 1)
            link(tt_(small[:, 24:25], small[:, 23:24], small[:, 22:23], ALU.subtract))
            ts_(small[:, 24:25], small[:, 24:25], -LAMBDA_INIT, None, ALU.add).then_inc(lam_ready, 1)
            for i in range(8):
                t, hf = i // 2, i % 2
                dest, gain = (qT, small[:, 25:26]) if t % 2 == 0 else (kT, colB[:, K_GAIN:K_GAIN + 1])
                h = 4 * (t // 2) + 2 * hf
                dve.wait_ge(qk_rstd, i + 1)
                B.ready(dve, ("qk", i))
                B.release(stt(out=dest[:, h:h + 2, :], in0=bank[i % 4][:, :].rearrange("p (a t) -> p a t", a=2),
                              scalar=gain, in1=rq[:, i % 2, :].rearrange("p (a t) -> p a t", a=2),
                              op0=ALU.mult, op1=ALU.mult), ("qk", i))
            for i in range(4):
                B.released(dve, ("bias", i))
            dve.wait_ge(lam_ready, 1)
            for i in range(HEADS + 4):
                if i < HEADS:
                    s = st[:, i % 2, :]
                    if i >= 2:
                        dve.wait_ge(attn_ready, i - 1)
                    for m in range(2):
                        B.ready(dve, ("s", i, m))
                        b = bank[2 * m + i % 2]
                        for qb in range(2):
                            a, n = qb * P, P + qb * P
                            j = 2 * m + qb
                            last = V_.tensor_tensor_reduce(L[:, i % 2, m * 384 + a:m * 384 + a + n], b[:, a:a + n],
                                                           bias[:, i, T - n:T], 1.0, -3e38, ALU.add, ALU.max,
                                                           s[:, j:j + 1])
                        B.release(last, ("s", i, m))
                    for m in range(2):
                        B.released(dve, ("s", i, m))
                    ts_(s[:, 4:8], s[:, 0:4], -1.0, None, ALU.mult).then_inc(logit_ready, 1)
                h = i - 1
                if 0 <= h < HEADS:
                    s = st[:, h % 2, :]
                    dve.wait_ge(p_ready, h + 1)
                    if h >= 2:
                        B.ready(dve, ("at", h - 2))
                    link(V_.reciprocal(s[:, 8:12], s[:, 8:12]))
                    link(ts_(s[:, 12:14], s[:, 10:12], small[:, 24:25], None, ALU.mult))
                    for qb in range(2):
                        a, n = qb * P, P + qb * P
                        last = ts_(A[:, h % 2, a:a + n], L[:, h % 2, a:a + n], s[:, 8 + qb:9 + qb], None, ALU.mult)
                    link(last)
                    for qb in range(2):
                        a, n = qb * P, P + qb * P
                        last = stt(out=A[:, h % 2, a:a + n], in0=L[:, h % 2, 384 + a:384 + a + n],
                                   scalar=s[:, 12 + qb:13 + qb], in1=A[:, h % 2, a:a + n], op0=ALU.mult, op1=ALU.add)
                    last.then_inc(attn_ready, 1)
                h = i - 4
                if 0 <= h < HEADS:
                    dve.wait_ge(o_rstd, h + 1)
                    B.release(stt(out=oT[:, h, :], in0=bank[5 + h % 2][:, 0:T], scalar=small[:, 26:27],
                                  in1=ro[:, h % 2, :], op0=ALU.mult, op1=ALU.mult), ("o", h))
            residual("attn_acc")

            norm(1)
            for i, (c, hf) in enumerate((c, hf) for c in range(NC_F) for hf in range(2)):
                B.released(dve, ("g", c, hf))
                B.ready(dve, ("u", c, hf))
                B.release(tt_(hid[:, c % 2, 2 * hf:2 * hf + 2, :], sg[:, i % 4, :].rearrange("p (a t) -> p a t", a=2),
                              bank[6 + hf][:, :].rearrange("p (a t) -> p a t", a=2), ALU.mult), ("u", c, hf))
            residual("ffn_acc")

            norm(2)
            dve.wait_ge(in_dt, 48)
            B.ready(dve, "dt")
            B.release(tt_(dtv[:, :, :], bank[5][:, 0:TT * SH].rearrange("p (c h) -> p c h", c=TT),
                          alog[:, 1, :].unsqueeze(1).broadcast_to([P, TT, SH]), ALU.add), "dt")
            B.released(dve, "dt")
            stt(out=dta[:, :, :], in0=dtv[:, :, :], scalar=-1.0, in1=dtv[:, :, :], op0=ALU.mult,
                op1=ALU.max).then_inc(sp_abs, 1)
            dve.wait_ge(sp_ln, 1)
            link(stt(out=dtv[:, :, :], in0=dtv[:, :, :], scalar=0.0, in1=dta[:, :, :], op0=ALU.max, op1=ALU.add))
            dve.wait_ge(a_exp, 1)
            stt(out=da[:, :, :], in0=dtv[:, :, :], scalar=-1.0,
                in1=alog[:, 0, :].unsqueeze(1).broadcast_to([P, TT, SH]), op0=ALU.mult, op1=ALU.mult).then_inc(da_ready, 1)
            B.ready(dve, "acs")
            link(V_.tensor_copy(acs[:, :, :], bank[6][:, 0:TT * SH].rearrange("p (c h) -> p c h", c=TT)))
            link(tt_(w0, bank[6][:, 64:64 + SH], acs[:, 0, :], ALU.subtract))
            B.release(V_.tensor_copy(small[:, 30:31], small[:, 24:25]), "acs")
            V_.tensor_copy(small[:, 31:32], small[:, 24:25]).then_inc(w0_arg, 1)
            for i in range(12):
                dve.wait_ge(conv_first, i + 1)
                for tap in range(3):
                    sh = 3 - tap
                    for j in range(2):
                        blk = conv_block(i) + j
                        o = cvb[:, i % 2, j * T + sh:(j + 1) * T]
                        last = stt(out=o, in0=bank[4 + i % 4][:, j * T:(j + 1) * T - sh],
                                   scalar=colA[:, 24 * tap + blk:24 * tap + blk + 1], in1=o, op0=ALU.mult, op1=ALU.add)
                    if tap < 2:
                        link(last)
                B.release(last, ("conv", i))
            for g in range(GROUPS):
                for c in range(TT):
                    B.ready(dve, ("xn", g, c))
                    if g >= 2 and c == 0:
                        B.ready(dve, ("y", g - 2, 1))
                    B.release(tt_(xd[:, g % 2, c * 512:(c + 1) * 512].rearrange("p (h d) -> p h d", d=HD),
                                  bank[1 + c][:, :].rearrange("p (h d) -> p h d", d=HD),
                                  dtv[:, c, g * HPG:(g + 1) * HPG].unsqueeze(2).broadcast_to([P, HPG, HD]), ALU.mult),
                              ("xn", g, c))
                    if c == 0:
                        B.ready(dve, ("cb", g))
                        if g >= 2:
                            B.ready(dve, ("state", g - 2))
                        tt_(cbm[:, g % 2, :].rearrange("p (c l) -> p c l", l=P),
                            bank[0][:, 0:T].rearrange("p (c l) -> p c l", l=P),
                            C("upto").unsqueeze(1).broadcast_to([P, TT, P]), ALU.mult).then_inc(cbm_ready, 1)
                        B.release(V_.tensor_copy(Bn[:, g % 2, :], bank[0][:, T:T + P]), ("cb", g))
                for half in range(2):
                    for c in range(TT):
                        B.ready(dve, ("ab", g, half, c))
                        if g and c == 0:
                            B.ready(dve, ("y", g - 1, half))
                        for q in range(4):
                            h = g * HPG + 4 * half + q
                            last = ts_(dec[:, 2 * half + c, q * P:(q + 1) * P],
                                       bank[4 + 2 * half + c][:, q * P:(q + 1) * P], acs[:, c, h:h + 1], 0.0,
                                       ALU.subtract, ALU.min)
                        if c == 0:
                            B.release(last, ("ab", g, half, 0))
                        else:
                            last.then_inc(arg1_ready, 1)
                dve.wait_ge(cbm_ready, g + 1)
                for half in range(2):
                    for c in range(TT):
                        dve.wait_ge(dec_ready, 4 * g + 2 * half + c + 1)
                        o = dec[:, 2 * half + c, :].rearrange("p (h l) -> p h l", l=P)
                        tt_(o, o, cbm[:, g % 2, c * P:(c + 1) * P].unsqueeze(1).broadcast_to([P, 4, P]),
                            ALU.mult).then_inc(m_ready, 1)
                for half in range(2):
                    B.ready(dve, ("y", g, half))
                    for j in range(2):
                        blk = 4 * g + 2 * half + j
                        last = stt(out=xsT[:, blk, :], in0=xsT[:, blk, :], scalar=dcol[:, blk:blk + 1],
                                   in1=bank[1 + half][:, j * T:(j + 1) * T], op0=ALU.mult, op1=ALU.add)
                    B.release(last, ("y", g, half))
            for g in range(GROUPS):
                dve.wait_ge(z_silu, g + 1)
                B.released(dve, ("y", g, 1))
                tt_(xsT[:, 4 * g:4 * g + 4, :], xsT[:, 4 * g:4 * g + 4, :], zr[:, 4 * g:4 * g + 4, :],
                    ALU.mult).then_inc(gated, 1)
            for g in range(GROUPS):
                dve.wait_ge(y_rstd, g + 1)
                for b in range(4):
                    blk = 4 * g + b
                    last = stt(out=xsT[:, blk, :], in0=xsT[:, blk, :], scalar=colB[:, SSD_NORM + blk:SSD_NORM + blk + 1],
                               in1=rg[:, g % 2, :], op0=ALU.mult, op1=ALU.mult)
                last.then_inc(y_ready, 1)
            residual("ssd_acc")

            norm(3)
            def per_expert(v):
                return v.rearrange("p (t e) -> p t e", e=E)

            B.ready(dve, "logits")
            lg_ = lg[:, :, :]
            B.release(V_.tensor_copy(lg_, bank[0][:, 0:TT * E].rearrange("p (t e) -> p t e", e=E)), "logits")
            B.released(dve, "logits")
            order = C("rank_of").unsqueeze(1).broadcast_to([P, TT, E])
            tmp = per_expert(tw[:, 2, :])

            def best(v, oh_k, m_k, s_k):
                link(V_.tensor_reduce(m_k, v, AX_X, ALU.max))
                link(tt_(tmp, v, m_k.unsqueeze(2).broadcast_to([P, TT, E]), ALU.is_ge))
                link(tt_(tmp, tmp, order, ALU.mult))
                link(V_.tensor_reduce(s_k, tmp, AX_X, ALU.max))
                link(tt_(oh_k, order, s_k.unsqueeze(2).broadcast_to([P, TT, E]), ALU.is_equal))

            oh1, oh2, sel, comb = (per_expert(oh[:, j, :]) for j in range(4))
            m1, m2, s1, s2 = (tw[:, 3 + j, 0:TT] for j in range(4))
            best(lg_, oh1, m1, s1)
            lg2 = per_expert(tw[:, 7, :])
            link(stt(out=lg2, in0=oh1, scalar=-3e38, in1=lg_, op0=ALU.mult, op1=ALU.add))
            best(lg2, oh2, m2, s2)
            tt_(tw[:, 0, 0:TT], m2, m1, ALU.subtract).then_inc(top_diff, 1)
            tt_(sel, oh1, oh2, ALU.add).then_inc(sel_ready, 1)
            dve.wait_ge(top_exp, 1)
            w1, w2, den = tw[:, 8, 0:TT], tw[:, 9, 0:TT], tw[:, 10, 0:TT]
            link(ts_(den, tw[:, 1, 0:TT], 1.0, None, ALU.add))
            link(V_.reciprocal(w1, den))
            link(tt_(w2, w1, tw[:, 1, 0:TT], ALU.mult))
            link(tt_(comb, oh1, w1.unsqueeze(2).broadcast_to([P, TT, E]), ALU.mult))
            link(tt_(tmp, oh2, w2.unsqueeze(2).broadcast_to([P, TT, E]), ALU.mult))
            link(tt_(comb, comb, tmp, ALU.add))
            for p in range(PASSES):
                link(V_.tensor_copy(cj[:, :, p * E:(p + 1) * E], comb))
            B.ready(dve, "rank")
            dve.wait_ge(sel_ready, 1)
            rank = per_expert(tw[:, 11, :])
            link(stt(out=rank, in0=bank[1][:, 0:2 * E].rearrange("p (t e) -> p t e", e=E), scalar=1.0, in1=sel,
                     op0=ALU.add, op1=ALU.mult))
            for p in range(PASSES):
                link(ts_(rj[:, :, p * E:(p + 1) * E], rank, -1.0 - p * SLOTS, None, ALU.add))
            link(V_.memset(rj[:, :, JOBS:JOBS + 1], -1.0))
            link(V_.tensor_reduce(tw[:, 0, 0:1], bank[1][:, 2 * E:3 * E], AX_X, ALU.max))
            B.release(ts_(flag[:, 0:1], tw[:, 0, 0:1], float(SLOTS), None, ALU.is_gt), "rank")
            B.released(dve, "rank")
            V_.tensor_copy(flag[:, 1:2], flag[:, 0:1]).then_inc(flag_ready, 1)

            def places(job):
                for tt in range(TT):
                    last = ts_(Pm[:, tt, :], C("slot_no"), rj[:, tt, bass.ds(job, 1)], None, ALU.is_equal)
                last.then_inc(place_ready, 1)

            places(0)
            for i in range(4):
                B.released(dve, ("xnat", i))

            def job_body(job):
                for c in range(NC_F):
                    b, k = J.at[("g", c)]
                    dve.wait_ge(free[b], job * USES[b] + (dense_uses[b] + k + 1))
                    job_ready(dve, ("u", c), job)
                    tt_(ehid[:, c % 2, :, :], esg[:, c % 2, :].rearrange("p (f t) -> p f t", f=4),
                        bank[2 + c % 2][:, 0:4 * SLOTS].rearrange("p (f t) -> p f t", f=4),
                        ALU.mult).then_inc(free[2 + c % 2], 1)
                    if c == 1:
                        job_ready(dve, "PT", job)
                        places(job + 1)
                for i in range(4):
                    tt, half = i // 2, i % 2
                    job_ready(dve, ("sc", i), job)
                    o = xnat[:, tt, half * 512:(half + 1) * 512]
                    stt(out=o, in0=bank[7 - i % 2][:, :], scalar=cj[:, tt, bass.ds(job, 1)], in1=o,
                        op0=ALU.mult, op1=ALU.add).then_inc(free[7 - i % 2], 1)
                for b in (6, 7):
                    dve.wait_ge(free[b], job * 2 + (dense_uses[b] + 2))

            with dve.Fori(0, E) as job:
                job_body(job)
            more = dve.value_load(flag[0:1, 0:1], min_val=0, max_val=1)
            with dve.If(more > 0):
                with dve.Fori(E, JOBS) as job:
                    job_body(job)
            V_.memset(small[:, 40:41], 0.0).then_inc(moe_done, 1)


INPUTS = ["x", "rel_bias", "norm_mix", "norm_ffn", "attn_w_in", "attn_q_gain", "attn_k_gain", "attn_lambda",
          "attn_subln", "attn_w_out", "ffn_w_gate", "ffn_w_up", "ffn_w_down", "ssd_w_in", "ssd_conv_w",
          "ssd_conv_b", "ssd_dt_bias", "ssd_a_log", "ssd_d", "ssd_norm", "ssd_w_out", "moe_router",
          "moe_w_gate", "moe_w_up", "moe_w_down"]


def kernel(**inputs):
    import concourse.bacc as bacc
    from concourse.bass_utils import run_bass_kernel_spmd

    nc = bacc.Bacc("TRN2", target_bir_lowering=False, num_devices=1)
    const, hot = constants()
    arrays = {name: np.ascontiguousarray(inputs[name]) for name in INPUTS}
    arrays["const"], arrays["hot"] = const, hot
    args = [nc.dram_tensor(name, a.shape, mybir.dt.from_np(a.dtype), kind="ExternalInput").ap()
            for name, a in arrays.items()]
    args.append(nc.dram_tensor("out", (1, T, D), F32, kind="ExternalOutput").ap())
    hybrid_trunk(nc, *args)
    result = run_bass_kernel_spmd(nc, [arrays], core_ids=[0])
    return result.results[0]["out"]
```

```python
import math
from contextlib import ExitStack

import numpy as np

import concourse.bass as bass
from concourse import mybir

F32 = mybir.dt.float32
F32R = mybir.dt.float32r
I32 = mybir.dt.int32
ALU = mybir.AluOpType
ACT = mybir.ActivationFunctionType
AX_X = mybir.AxisListType.X

P = 128
D = 1024
KD = D // P
T = 256
TT = T // P
HEADS = 8
HD = 64
F = 3584
NC_F = F // 512
DI = 2048
GROUPS = 4
NSTATE = 128
SH = 32
HPG = SH // GROUPS
E = 8
SLOTS = 96
PASSES = 3
JOBS = E * PASSES
LAMBDA_INIT = 0.8 - 0.6 * math.exp(0.0)
EPS = 1e-6
MASKED = -1e30
BUCKETS = 32
DENSE_RING = 3
RING = 7
SPLITS = 4
QUARTER = 1024
SLOT = 4096

CONSTS = {}
_at = 0
for _name, _n in (("ident", 128), ("anti", 128), ("mean_d", 128), ("mean_hd", 128), ("mean_v", 128),
                  ("mean_g", 128), ("upto", 128), ("before", 128), ("ones", 128), ("slot_no", SLOTS),
                  ("rank_of", E), ("eps", 1), ("one", 1), ("odd_even", 128), ("pair_of", 16)):
    CONSTS[_name] = (_at, _at + _n)
    _at += _n
NCONST = _at
NORM_MIX, NORM_FFN, CONV_B, SSD_NORM, SUBLN, Q_GAIN, K_GAIN = 0, 16, 32, 56, 72, 73, 74
ROWS_B = 75
NDIST = 2 * P + P - 1


def constants():
    c = np.zeros((P, NCONST), np.float32)
    i = np.arange(P)

    def put(name, v):
        a, b = CONSTS[name]
        c[:, a:b] = v

    put("ident", np.eye(P))
    put("anti", np.eye(P)[::-1])
    put("mean_d", 1.0 / D)
    put("mean_hd", (i[:, None] // HD == i[None, :] // HD) / HD)
    put("mean_v", 1.0 / P)
    put("mean_g", 1.0 / (DI // GROUPS))
    put("upto", i[:, None] <= i[None, :])
    put("before", i[:, None] < i[None, :])
    put("ones", 1.0)
    put("slot_no", np.arange(SLOTS)[None, :])
    put("rank_of", (E - np.arange(E))[None, :])
    put("eps", EPS)
    put("one", 1.0)
    put("odd_even", i[:, None] % 2 == i[None, :] // HD)
    put("pair_of", i[:, None] // 2 == np.arange(16)[None, :])
    dist = 255 - np.arange(NDIST)
    n = np.maximum(dist, 0)
    exact = BUCKETS // 2
    large = exact + (np.log(np.maximum(n, 1).astype(np.float32) / np.float32(exact)) / np.float32(math.log(128 / exact))
                     * np.float32(BUCKETS - exact)).astype(np.int32)
    bucket = np.where(n < exact, n, np.minimum(large, BUCKETS - 1))
    hot = np.zeros((BUCKETS + 1, NDIST), np.float32)
    for j in range(NDIST):
        hot[BUCKETS if dist[j] < 0 else bucket[j], j] = 1.0
    return c, hot


N_ROWS, N_MISC = 10, 3


def conv_block(i):
    return 16 + 2 * i if i < 4 else 2 * i - 8


class Chain:

    def __init__(self, eng, sem):
        self.eng, self.sem, self.n = eng, sem, 0

    def link(self, ins):
        self.n += 1
        ins.then_inc(self.sem, 1)
        self.eng.wait_ge(self.sem, self.n)


class Banks:

    def __init__(self, full, free):
        self.full, self.free = full, free
        self.count = [0] * 8
        self.at = {}

    def plan(self, name, bank):
        self.at[name] = (bank, self.count[bank])
        self.count[bank] += 1

    def claim(self, pe, name):
        b, k = self.at[name]
        if k:
            pe.wait_ge(self.free[b], k)

    def finish(self, ins, name):
        ins.then_inc(self.full[self.at[name][0]], 1)

    def ready(self, eng, name):
        b, k = self.at[name]
        eng.wait_ge(self.full[b], k + 1)

    def release(self, ins, name):
        ins.then_inc(self.free[self.at[name][0]], 1)

    def released(self, eng, name):
        b, k = self.at[name]
        eng.wait_ge(self.free[b], k + 1)


def dense_tiles():
    tiles = []
    for t in range(2):
        tiles += [("attn_q", t), ("attn_k", t)]
    tiles += [("attn_v", 0), ("attn_v", 1), ("attn_out", 0), ("attn_out", 1)]
    for c in range(NC_F):
        tiles += [("ffn_gate", c), ("ffn_up", c)]
        if c:
            tiles.append(("ffn_down", c - 1))
    tiles.append(("ffn_down", NC_F - 1))
    tiles += [("ssd_b", 0), ("ssd_c", 0)] + [("ssd_x", t) for t in range(4)] + [("ssd_z", t) for t in range(4)]
    tiles += [("ssd_out", t) for t in range(4)]
    return tiles


def expert_tiles():
    tiles = []
    for c in range(NC_F):
        tiles += [("gate", c), ("up", c)]
        if c:
            tiles.append(("down", c - 1))
    tiles.append(("down", NC_F - 1))
    return tiles


def hybrid_trunk(nc, x, rel_bias, norm_mix, norm_ffn, attn_w_in, attn_q_gain, attn_k_gain, attn_lambda,
                 attn_subln, attn_w_out, ffn_w_gate, ffn_w_up, ffn_w_down, ssd_w_in, ssd_conv_w, ssd_conv_b,
                 ssd_dt_bias, ssd_a_log, ssd_d, ssd_norm, ssd_w_out, moe_router, moe_w_gate, moe_w_up,
                 moe_w_down, const, hot, out):
    DT = dense_tiles()
    DENSE = {name: n for n, name in enumerate(DT)}
    ND = len(DT)
    ET = expert_tiles()
    EXPERT = {name: m for m, name in enumerate(ET)}
    NE = len(ET)
    assert NE % RING == 0

    with ExitStack() as ctx:
        def sb(name, shape, dt=F32):
            return ctx.enter_context(nc.sbuf_tensor(name, shape, dt))

        def sem(name):
            return ctx.enter_context(nc.semaphore(name))

        cst = sb("cst", [P, NCONST])
        colA = sb("colA", [P, 96])
        colB = sb("colB", [P, 80])
        rows = sb("rows", [P, 2, P])
        dcol = sb("dcol", [P, 16])
        small = sb("small", [P, 64])
        rstd = sb("rstd", [P, T])
        relb = sb("relb", [BUCKETS + 1, HEADS])
        flag = sb("flag", [P, 2], I32)
        tables = sb("tables", [P, 768])
        wsplit = sb("wsplit", [P, SPLITS, 2, QUARTER], F32R)
        hTg = sb("hTg", [P, 2, KD, SLOTS], F32R)
        ehidT = sb("ehidT", [P, 2, 2, 4, SLOTS], F32R)
        HEAD = KD * T
        SLOT_AT = 4 * HEAD
        mem = sb("mem", [P, SLOT_AT + RING * SLOT])
        xT = mem[:, 0:HEAD].rearrange("p (k t) -> p k t", k=KD)
        hT = mem[:, HEAD:2 * HEAD].rearrange("p (k t) -> p k t", k=KD)

        def slot_mem(s):
            return mem[:, SLOT_AT + s * SLOT:SLOT_AT + (s + 1) * SLOT]

        DENSE_SLOT = [4, 5, 6]
        EXPERT_SLOT = [3, 0, 1, 2, 4, 5, 6]

        def carve(spec, region, at, end):
            got = []
            for shape in spec:
                n = int(np.prod(shape))
                v = region[:, at:at + n]
                if len(shape) > 1:
                    names = " ".join("abc"[:len(shape)])
                    v = v.rearrange(f"p ({names}) -> p {names}", **{"abc"[i]: s for i, s in enumerate(shape)})
                got.append(v)
                at += n
            assert at <= end, (at, end)
            return got

        LAYER = (mem, 2 * HEAD, SLOT_AT + 3 * SLOT)
        spec = [(HEADS, T), (HEADS, T), (TT, D), (HEADS, T), (HEADS, T), (2, 384), (2, 384), (2, T), (2, T),
                (4 * HD,), (2, 16)]
        qT, kT, V, oT, bias, A, AT, sqo, ro, lam_in, st, sqb, rq = carve(spec + [(2, 512), (2, 512)], *LAYER)
        L = carve(spec + [(2, 2 * 384)], *LAYER)[-1]
        hid, sg = carve([(2, 4 * T), (4, 512)], *LAYER)
        hid = hid.rearrange("p b (f t) -> p b f t", f=4)
        (xsT, BT, CT, xd, xw, Bn, cbm, stS, dec, eC, cvb, wdt, dtv, dta, da, acs, w0, alog, rg) = carve(
            [(16, T), (4, T), (4, T), (2, 2 * 512), (2, 512), (2, P), (2, 2 * P), (2, 512), (4, 512), (2, 512),
             (2, 512), (KD, SH), (TT, SH), (TT, SH), (TT, SH), (TT, SH), (SH,), (2, SH), (2, T)], *LAYER)
        zr = slot_mem(3).rearrange("p (b t) -> p b t", b=16)
        xin = slot_mem(3)[:, 0:TT * D].rearrange("p (a b) -> p a b", a=TT)
        hankel = slot_mem(3)[:, TT * D:SLOT].rearrange("p (h t) -> p h t", h=HEADS)
        onehot, ubias = tables[0:BUCKETS + 1, 0:NDIST], tables[0:HEADS, 384:384 + NDIST]
        scratch = nc.dram_tensor("bias_by_distance", (HEADS, 512), F32).ap()
        xnat, hnat = carve([(TT, D), (TT, D)], mem, 2 * HEAD, SLOT_AT)
        ehid, esg, Pm, PT, ynat = carve([(512,), (2, 512), (TT, SLOTS), (TT, P), (D,)], mem, 0, 2 * HEAD)
        lg, oh, tw, rj, cj, router = carve(
            [(TT, E), (4, TT * E), (12, TT * E), (TT, JOBS + 1), (TT, JOBS), (KD, E)], tables, 0, 768)

        dense_in_slot = [sum(1 for n in range(ND) if DENSE_SLOT[n % DENSE_RING] == s) for s in range(RING)]

        def expert_landed(eng, tile, job):
            m = EXPERT[tile]
            s = EXPERT_SLOT[m % RING]
            eng.wait_ge(landed[s], job * (16 * NE // RING) + 16 * (dense_in_slot[s] + m // RING + 1))
            return view(tile[0], s)

        def quarter(w, q):
            n = w.shape[1] // 4
            return w[:, n * q:n * (q + 1), :]

        def C(name, n=P):
            a, b = CONSTS[name]
            return cst[0:n, a:b]

        bank = [ctx.enter_context(nc.psum_tensor(f"bank{b}", [P, 512], F32)) for b in range(8)]
        full = [sem(f"full{b}") for b in range(8)]
        free = [sem(f"free{b}") for b in range(8)]
        B = Banks(full, free)

        B.plan("rowsA", 4), B.plan("rowsB", 5), B.plan("dcol", 6), B.plan("ubias", 7)
        for i in range(4):
            B.plan(("x", i), 4 + i)
        B.plan(("ms", 0), 4)
        for i in range(9):
            if i < 8:
                B.plan(("qk", i), i % 4)
            if i:
                B.plan(("qk_ms", i - 1), 4 + (i - 1) % 2)
        for i in range(4):
            B.plan(("v", i), 6 + i % 2)
        for i in range(4):
            B.plan(("bias", i), i)
        for i in range(HEADS + 4):
            if i < HEADS:
                B.plan(("s", i, 0), i % 2), B.plan(("s", i, 1), 2 + i % 2)
            if 0 <= i - 2 < HEADS:
                B.plan(("at", i - 2), 4)
            if 0 <= i - 3 < HEADS:
                B.plan(("o", i - 3), 5 + (i - 3) % 2)
            if 0 <= i - 4 < HEADS:
                B.plan(("o_ms", i - 4), 7)
        for b in range(4):
            B.plan(("attn_acc", b), b)
        B.plan(("ms", 1), 4)
        for c in range(NC_F):
            for hf in range(2):
                B.plan(("g", c, hf), 4 + hf), B.plan(("u", c, hf), 6 + hf)
        for b in range(4):
            B.plan(("ffn_acc", b), b)
        B.plan(("ms", 2), 4), B.plan("dt", 5), B.plan("acs", 6)
        for i in range(12):
            B.plan(("conv", i), 4 + i % 4)
        for g in range(GROUPS):
            B.plan(("xn", g, 0), 1), B.plan(("cb", g), 0), B.plan(("xn", g, 1), 2)
            B.plan(("z", g, 0), 0), B.plan(("state", g), 3)
            for half in range(2):
                for c in range(TT):
                    B.plan(("ab", g, half, c), 4 + 2 * half + c)
            B.plan(("z", g, 1), 3)
            for half in range(2):
                B.plan(("y", g, half), 1 + half)
        for g in range(GROUPS):
            B.plan(("y_ms", g), 4 + g)
        for b in range(4):
            B.plan(("ssd_acc", b), b)
        B.plan(("ms", 3), 4)
        for i in range(4):
            B.plan(("xnat", i), i)
        for i in range(4):
            B.plan(("hnat", i), 4 + i)
        B.plan("logits", 0), B.plan("rank", 1)
        dense_uses = list(B.count)

        J = Banks(full, free)
        for c in range(NC_F):
            J.plan(("g", c), c % 2), J.plan(("hidT", c), 6)
        J.plan(("gather", 0), 1), J.plan(("gather", 1), 3)
        J.plan("PT", 7)
        for i in range(4):
            J.plan(("sc", i), 7 - i % 2)
        USES = list(J.count)
        BASE = list(dense_uses)
        BASE[1] += 1
        BASE[3] += 1

        def tile_finished(eng, tile, job):
            eng.wait_ge(w_used, job * 4 * NE + (SPLITS + 4 * EXPERT[tile] + 4))

        def job_ready(eng, name, job):
            b = J.at[name][0]
            alone = [n for n, (bb, _) in J.at.items() if bb == b and n[0] != "g"]
            eng.wait_ge(full[b], job * len(alone) + (BASE[b] + alone.index(name) + 1))

        def job_claim(eng, name, job):
            b, k = J.at[name]
            eng.wait_ge(free[b], job * USES[b] + (BASE[b] + k))

        def job_released(eng, name, job):
            b, k = J.at[name]
            eng.wait_ge(free[b], job * USES[b] + (BASE[b] + k + 1))

        def job_gathered(eng, job):
            for b in (1, 3):
                eng.wait_ge(free[b], job * USES[b] + BASE[b])

        landed = [sem(f"landed{s}") for s in range(RING)]
        down_done = sem("down_done")
        in_x, in_const, in_rows, in_misc, in_lam = (sem(n) for n in ("in_x", "in_const", "in_rows", "in_misc", "in_lam"))
        in_hankel, in_scratch, in_dt, in_router = sem("in_hankel"), sem("in_scratch"), sem("in_dt"), sem("in_router")
        out_done = sem("out_done")
        dve_step, act_step = sem("dve_step"), sem("act_step")
        relb_set = sem("relb_set")
        sq_ready = sem("sq_ready")
        rstd_ready = sem("rstd_ready")
        h_ready = sem("h_ready")
        gains_ready = sem("gains_ready")
        qk_sq, qk_rstd = sem("qk_sq"), sem("qk_rstd")
        lam_dot, lam_exp, lam_ready = sem("lam_dot"), sem("lam_exp"), sem("lam_ready")
        logit_ready, p_ready, attn_ready = sem("logit_ready"), sem("p_ready"), sem("attn_ready")
        o_sq, o_rstd = sem("o_sq"), sem("o_rstd")
        sp_abs, sp_ln, a_exp, da_ready, w0_arg, w0_ready = (sem(n) for n in (
            "sp_abs", "sp_ln", "a_exp", "da_ready", "w0_arg", "w0_ready"))
        conv_first, conv_sum, conv_out = sem("conv_first"), sem("conv_sum"), sem("conv_out")
        xw_ready, arg1_ready, dec_ready, m_ready, ce_ready = (sem(n) for n in (
            "xw_ready", "arg1_ready", "dec_ready", "m_ready", "ce_ready"))
        cbm_ready = sem("cbm_ready")
        z_silu, gated, y_sq, y_rstd, y_ready = (sem(n) for n in ("z_silu", "gated", "y_sq", "y_rstd", "y_ready"))
        top_diff, top_exp, sel_ready, flag_ready = (sem(n) for n in ("top_diff", "top_exp", "sel_ready", "flag_ready"))
        place_ready = sem("place_ready")
        w_hi, w_lo = sem("w_hi"), sem("w_lo")
        w_used = sem("w_used")
        hg_hi = sem("hg_hi")
        hid_hi = sem("hid_hi")
        hid_ready = sem("hid_ready")
        y_ready_e = sem("y_ready_e")
        moe_done = sem("moe_done")

        def cols(w, c0):
            return w[:, c0:c0 + 512].rearrange("(k p) n -> p k n", p=P)

        def rws(w, t):
            return w[512 * t:512 * (t + 1), :].rearrange("(k p) n -> p k n", p=P)

        W_IN = ssd_w_in[0]
        SOURCE = {
            "attn_q": lambda t: cols(attn_w_in[0], 512 * t), "attn_k": lambda t: cols(attn_w_in[0], D + 512 * t),
            "attn_v": lambda t: cols(attn_w_in[0], 2 * D + 512 * t), "attn_out": lambda t: rws(attn_w_out[0], t),
            "ffn_gate": lambda t: cols(ffn_w_gate[0], 512 * t), "ffn_up": lambda t: cols(ffn_w_up[0], 512 * t),
            "ffn_down": lambda t: rws(ffn_w_down[0], t),
            "ssd_z": lambda t: cols(W_IN, 512 * t), "ssd_x": lambda t: cols(W_IN, DI + 512 * t),
            "ssd_b": lambda t: cols(W_IN, 2 * DI), "ssd_c": lambda t: cols(W_IN, 2 * DI + 512),
            "ssd_out": lambda t: rws(ssd_w_out[0], t),
        }

        def view(kind, s):
            by_rows = kind.endswith("out") or kind.endswith("down")
            return slot_mem(s).rearrange("p (k n) -> p k n", k=4 if by_rows else KD)

        def expert_source(kind, c, e):
            if kind == "down":
                w = moe_w_down.rearrange("o e (c k p) n -> (o e) c p k n", k=4, p=P)
                return w[bass.ds(e, 1), c].rearrange("a p k n -> (a p) k n")
            w = (moe_w_gate if kind == "gate" else moe_w_up).rearrange("o e (k p) n -> (o e) p k n", p=P)
            return w[bass.ds(e, 1), :, :, 512 * c:512 * (c + 1)].rearrange("a p k n -> (a p) k n")

        block = ctx.enter_context(nc.Block())

        def dense_tile_used(eng, tile):
            kind, t = tile
            if kind in ("attn_q", "attn_k"):
                B.ready(eng, ("qk", 4 * t + 2 * (kind == "attn_k") + 1))
            elif kind == "attn_v":
                B.ready(eng, ("v", 2 * t + 1))
            elif kind in ("ffn_gate", "ffn_up"):
                B.ready(eng, (kind[4], t, 1))
            elif kind in ("ssd_b", "ssd_c", "ssd_x"):
                B.ready(eng, ("conv", 2 * {"ssd_b": 0, "ssd_c": 1, "ssd_x": 2 + t}[kind] + 1))
            elif kind == "ssd_z":
                B.ready(eng, ("z", t, 1))
            else:
                base, layer, last_t = {"attn_out": (0, "attn_acc", 1), "ffn_down": (1, "ffn_acc", NC_F - 1),
                                       "ssd_out": (NC_F, "ssd_acc", 3)}[kind]
                if t == last_t:
                    B.ready(eng, (layer, 3))
                else:
                    eng.wait_ge(down_done, base + t + 1)

        @block.sync
        def _(sp):
            sp.dma_start(xin[:, :, :], x[0].rearrange("(a p) n -> p a n", p=P)).then_inc(in_x, 16)
            for n, (kind, t) in enumerate(DT):
                slot = DENSE_SLOT[n % DENSE_RING]
                if n >= DENSE_RING:
                    dense_tile_used(sp, DT[n - DENSE_RING])
                sp.dma_start(view(kind, slot), SOURCE[kind](t)).then_inc(landed[slot], 16)

            def job_tiles(e, job, first):
                for m, (kind, c) in enumerate(ET):
                    slot = EXPERT_SLOT[m % RING]
                    if not first or m >= RING:
                        sp.wait_ge(w_lo, job * 4 * NE + 4 * (m - RING + 1))
                    elif slot == 3:
                        B.ready(sp, ("y_ms", GROUPS - 1))
                    elif slot < 3:
                        sp.wait_ge(y_ready, GROUPS)
                    else:
                        dense_tile_used(sp, DT[max(n for n in range(ND) if DENSE_SLOT[n % DENSE_RING] == slot)])
                    sp.dma_start(view(kind, slot), expert_source(kind, c, e)).then_inc(landed[slot], 16)

            job_tiles(0, 0, True)
            with sp.Fori(1, E) as e:
                job_tiles(e, e, False)
            sp.wait_ge(flag_ready, 1)
            more = sp.value_load(flag[0:1, 0:1], min_val=0, max_val=1)
            with sp.If(more > 0):
                with sp.Fori(1, PASSES) as p:
                    with sp.Fori(0, E) as e:
                        job_tiles(e, p * E + e, False)
            sp.wait_ge(moe_done, 1)
            sp.dma_start(out[0].rearrange("(a p) n -> p a n", p=P), xnat[:, :, :]).then_inc(out_done, 16)
            sp.wait_ge(out_done, 16)

        @block.gpsimd
        def _(pool):
            B.released(pool, "ubias")
            pool.dma_start(scratch[:, 0:NDIST], ubias[:, :]).then_inc(in_scratch, 16)
            pool.wait_ge(in_scratch, 16)
            pool.dma_start(hankel[:, :, :],
                           bass.AP(scratch.tensor, 0, [[1, P], [512, HEADS], [1, T]])).then_inc(in_hankel, 16)

            B.released(pool, ("ffn_acc", 3))
            pool.dma_start(wdt[:, :, :], W_IN[:, 2 * DI + 2 * GROUPS * NSTATE:]
                           .rearrange("(k p) n -> p k n", p=P)).then_inc(in_dt, 16)
            pool.dma_start(alog[:, 0, :], ssd_a_log[0:1, :].broadcast_to([P, SH])).then_inc(in_dt, 16)
            pool.dma_start(alog[:, 1, :], ssd_dt_bias[0:1, :].broadcast_to([P, SH])).then_inc(in_dt, 16)
            pool.wait_ge(w0_ready, 1)
            for g in range(GROUPS):
                B.released(pool, ("xn", g, 0))
                if g >= 2:
                    B.ready(pool, ("state", g - 2))
                nc.gpsimd.tensor_tensor(xw[:, g % 2, :].rearrange("p (h d) -> p h d", d=HD),
                                        xd[:, g % 2, 0:512].rearrange("p (h d) -> p h d", d=HD),
                                        w0[:, g * HPG:(g + 1) * HPG].unsqueeze(2).broadcast_to([P, HPG, HD]),
                                        ALU.mult).then_inc(xw_ready, 1)
                for half in range(2):
                    B.released(pool, ("ab", g, half, 1))
                    nc.gpsimd.tensor_tensor(eC[:, half, :].rearrange("p (h l) -> p h l", l=P),
                                            eC[:, half, :].rearrange("p (h l) -> p h l", l=P),
                                            CT[:, g, P:T].unsqueeze(1).broadcast_to([P, 4, P]),
                                            ALU.mult).then_inc(ce_ready, 1)
            B.released(pool, ("ssd_acc", 3))
            pool.dma_start(router[:, :, :], moe_router[0].rearrange("(k p) n -> p k n", p=P)).then_inc(in_router, 16)

        @block.tensor
        def _(pe):
            def mm(o, lhsT, rhs, start, stop, shared=False):
                return nc.tensor.matmul(o, lhsT, rhs, start=start, stop=stop, skip_group_check=shared)

            def arrive(tile):
                n = DENSE[tile]
                slot = DENSE_SLOT[n % DENSE_RING]
                pe.wait_ge(landed[slot], 16 * (n // DENSE_RING + 1))
                return view(tile[0], slot)

            pe.wait_ge(in_const, 16)
            pe.wait_ge(in_rows, 16 * N_ROWS)
            B.finish(nc.tensor.transpose(bank[4][:, 0:96], rows[0:96, 0, :], cst[0:96, 0:96]), "rowsA")
            B.finish(nc.tensor.transpose(bank[5][:, 0:ROWS_B], rows[0:ROWS_B, 1, :], cst[0:ROWS_B, 0:ROWS_B]), "rowsB")
            pe.wait_ge(in_misc, 16 * N_MISC)
            pe.wait_ge(relb_set, 2)
            B.finish(mm(bank[6][:, 0:16], C("odd_even", SH), small[0:SH, 0:16], True, True), "dcol")
            B.finish(mm(bank[7][0:HEADS, 0:NDIST], relb[:, :], onehot[:, :], True, True), "ubias")

            pe.wait_ge(in_x, 16)
            for i in range(4):
                B.claim(pe, ("x", i))
                for j in range(2):
                    for tt in range(TT):
                        last = nc.tensor.transpose(bank[4 + i][:, j * T + tt * P:j * T + (tt + 1) * P],
                                                   xin[:, tt, (2 * i + j) * P:(2 * i + j + 1) * P], C("ident"))
                B.finish(last, ("x", i))

            def mean_square(n):
                B.claim(pe, ("ms", n))
                for k in range(KD):
                    if k % 2 == 0:
                        pe.wait_ge(sq_ready, 4 * n + k // 2 + 1)
                    last = mm(bank[4][:, 0:T], C("mean_d"), hT[:, k, :], k == 0, k == KD - 1)
                    if n == 3 and k == 0:
                        last.then_inc(w_used, SPLITS)
                B.finish(last, ("ms", n))

            def project(o, w, col, fresh=None):
                for j in range(2):
                    for k in range(KD):
                        if fresh is not None and j == 0:
                            pe.wait_ge(h_ready, KD * fresh + k + 1)
                        last = mm(o[:, j * T:(j + 1) * T], w[:, k, col + j * P:col + (j + 1) * P], hT[:, k, :],
                                  k == 0, k == KD - 1)
                return last

            def down(acc, w, act, first, last_tile):
                for m in range(KD):
                    b = m // 2
                    if first and m % 2 == 0:
                        B.claim(pe, (acc, b))
                    for r in range(4):
                        last = mm(bank[b][:, (m % 2) * T:(m % 2 + 1) * T], w[:, r, m * P:(m + 1) * P], act(r),
                                  first and m % 2 == 0 and r == 0, last_tile and m % 2 == 1 and r == 3, shared=True)
                    if last_tile and m % 2 == 1:
                        B.finish(last, (acc, b))
                if not last_tile:
                    last.then_inc(down_done, 1)

            mean_square(0)
            for i in range(9):
                if i < 8:
                    t, hf = i // 2, i % 2
                    w = arrive(("attn_q" if t % 2 == 0 else "attn_k", t // 2))
                    B.claim(pe, ("qk", i))
                    B.finish(project(bank[i % 4], w, 256 * hf, 0 if i == 0 else None), ("qk", i))
                if i:
                    B.claim(pe, ("qk_ms", i - 1))
                    pe.wait_ge(qk_sq, i)
                    last = mm(bank[4 + (i - 1) % 2][:, :], C("mean_hd"), sqb[:, (i - 1) % 2, :], True, True)
                    B.finish(last, ("qk_ms", i - 1))
            for i in range(4):
                t, tt = i // 2, i % 2
                w = arrive(("attn_v", t))
                B.claim(pe, ("v", i))
                for k in range(KD):
                    last = mm(bank[6 + i % 2][:, :], hT[:, k, tt * P:(tt + 1) * P], w[:, k, :], k == 0, k == KD - 1)
                B.finish(last, ("v", i))
            pe.wait_ge(in_hankel, 16)
            for i in range(4):
                B.claim(pe, ("bias", i))
                last = mm(bank[i][:, :], C("anti"), hankel[:, 2 * i:2 * i + 2, :], True, True)
                B.finish(last, ("bias", i))
            for i in range(8):
                B.released(pe, ("qk", i))
            for i in range(4):
                B.released(pe, ("v", i))
            for i in range(HEADS + 4):
                if i < HEADS:
                    for m in range(2):
                        B.claim(pe, ("s", i, m))
                        b = bank[2 * m + i % 2]
                        q, k = qT[HD * m:HD * (m + 1), i, :], kT[HD * m:HD * (m + 1), i, :]
                        mm(b[:, 0:P], q[:, 0:P], k[:, 0:P], True, True)
                        B.finish(mm(b[:, P:P + T], q[:, P:T], k[:, :], True, True), ("s", i, m))
                h = i - 2
                if 0 <= h < HEADS:
                    B.claim(pe, ("at", h))
                    pe.wait_ge(attn_ready, h + 1)
                    for j in range(3):
                        last = nc.tensor.transpose(bank[4][:, j * P:(j + 1) * P], A[:, h % 2, j * P:(j + 1) * P],
                                                   C("ident"))
                    B.finish(last, ("at", h))
                h = i - 3
                if 0 <= h < HEADS:
                    B.claim(pe, ("o", h))
                    B.released(pe, ("at", h))
                    b = bank[5 + h % 2]
                    mm(b[:, 0:T], V[:, 0, h * P:(h + 1) * P], AT[:, h % 2, 0:T], True, False)
                    B.finish(mm(b[:, P:T], V[:, 1, h * P:(h + 1) * P], AT[:, h % 2, T:T + P], False, True), ("o", h))
                h = i - 4
                if 0 <= h < HEADS:
                    B.claim(pe, ("o_ms", h))
                    pe.wait_ge(o_sq, h + 1)
                    B.finish(mm(bank[7][:, 0:T], C("mean_v"), sqo[:, h % 2, :], True, True), ("o_ms", h))
            for t in range(2):
                w = arrive(("attn_out", t))
                for h in range(4 * t, 4 * t + 4):
                    B.released(pe, ("o", h))
                down("attn_acc", w, lambda r, t=t: oT[:, 4 * t + r, :], t == 0, t == 1)

            mean_square(1)
            for c in range(NC_F + 1):
                if c < NC_F:
                    for hf in range(2):
                        for kind, b in (("gate", 4 + hf), ("up", 6 + hf)):
                            w = arrive(("ffn_" + kind, c))
                            B.claim(pe, (kind[0], c, hf))
                            fresh = 1 if c == 0 and hf == 0 and kind == "gate" else None
                            B.finish(project(bank[b], w, 256 * hf, fresh), (kind[0], c, hf))
                if c:
                    w = arrive(("ffn_down", c - 1))
                    for hf in range(2):
                        B.released(pe, ("u", c - 1, hf))
                    down("ffn_acc", w, lambda r, c=c: hid[:, (c - 1) % 2, r, :], c == 1, c == NC_F)

            mean_square(2)
            pe.wait_ge(in_dt, 48)
            B.claim(pe, "dt")
            for k in range(KD):
                pe.wait_ge(h_ready, KD * 2 + k + 1)
            for tt in range(TT):
                for k in range(KD):
                    last = mm(bank[5][:, tt * SH:(tt + 1) * SH], hT[:, k, tt * P:(tt + 1) * P], wdt[:, k, :],
                              k == 0, k == KD - 1)
            B.finish(last, "dt")
            for i in range(12):
                t, hf = i // 2, i % 2
                w = arrive([("ssd_b", 0), ("ssd_c", 0), ("ssd_x", 0), ("ssd_x", 1), ("ssd_x", 2), ("ssd_x", 3)][t])
                B.claim(pe, ("conv", i))
                B.finish(project(bank[4 + i % 4], w, 256 * hf), ("conv", i))
                if i == 1:
                    B.claim(pe, "acs")
                    pe.wait_ge(da_ready, 1)
                    for c in range(TT):
                        mm(bank[6][:, c * SH:(c + 1) * SH], C("upto"), da[:, c, :], True, True)
                    B.finish(mm(bank[6][:, 64:64 + SH], C("ones"), da[:, 0, :], True, True), "acs")

            def project_z(g, hf, b):
                w = arrive(("ssd_z", g))
                B.claim(pe, ("z", g, hf))
                B.finish(project(bank[b], w, 256 * hf), ("z", g, hf))

            for g in range(GROUPS):
                pe.wait_ge(conv_out, 4 + 2 * g + 2)
                for c in range(TT):
                    B.claim(pe, ("xn", g, c))
                    for b in range(4):
                        last = nc.tensor.transpose(bank[1 + c][:, b * P:(b + 1) * P],
                                                   xsT[:, 4 * g + b, c * P:(c + 1) * P], C("ident"))
                    B.finish(last, ("xn", g, c))
                    if c == 0:
                        B.claim(pe, ("cb", g))
                        for cc in range(TT):
                            mm(bank[0][:, cc * P:(cc + 1) * P], BT[:, g, cc * P:(cc + 1) * P],
                               CT[:, g, cc * P:(cc + 1) * P], True, True)
                        B.finish(nc.tensor.transpose(bank[0][:, T:T + P], BT[:, g, 0:P], C("ident")), ("cb", g))
                project_z(g, 0, 0)
                B.claim(pe, ("state", g))
                pe.wait_ge(xw_ready, g + 1)
                B.finish(mm(bank[3][:, :], Bn[:, g % 2, :], xw[:, g % 2, :], True, True), ("state", g))
                for half in range(2):
                    for c in range(TT):
                        B.claim(pe, ("ab", g, half, c))
                        for q in range(4):
                            h = g * HPG + 4 * half + q
                            last = mm(bank[4 + 2 * half + c][:, q * P:(q + 1) * P],
                                      da[:, c, h:h + 1].broadcast_to([P, P]), C("upto"), True, True)
                        B.finish(last, ("ab", g, half, c))
                project_z(g, 1, 3)
                B.released(pe, ("xn", g, 1))
                B.released(pe, ("state", g))
                for half in range(2):
                    B.claim(pe, ("y", g, half))
                    pe.wait_ge(m_ready, 4 * g + 2 * half + 2)
                    pe.wait_ge(ce_ready, 2 * g + half + 1)
                    for q in range(4):
                        o = bank[1 + half][HD * (q % 2):HD * (q % 2 + 1), (q // 2) * T:(q // 2 + 1) * T]
                        ch = (4 * half + q) * HD
                        mm(o[:, 0:P], xd[:, g % 2, ch:ch + HD], dec[:, 2 * half, q * P:(q + 1) * P], True, True)
                        mm(o[:, P:T], xd[:, g % 2, 512 + ch:512 + ch + HD], dec[:, 2 * half + 1, q * P:(q + 1) * P],
                           True, False)
                        last = mm(o[:, P:T], stS[:, g % 2, ch:ch + HD], eC[:, half, q * P:(q + 1) * P], False, True)
                    B.finish(last, ("y", g, half))
            for g in range(GROUPS):
                B.claim(pe, ("y_ms", g))
                pe.wait_ge(y_sq, g + 1)
                for b in range(4):
                    last = mm(bank[4 + g][:, 0:T], C("mean_g"), zr[:, 4 * g + b, :], b == 0, b == 3)
                B.finish(last, ("y_ms", g))
            for g in range(GROUPS):
                w = arrive(("ssd_out", g))
                pe.wait_ge(y_ready, g + 1)
                down("ssd_acc", w, lambda r, g=g: xsT[:, 4 * g + r, :], g == 0, g == 3)

            mean_square(3)
            for i in range(4):
                tt, half = i // 2, i % 2
                B.claim(pe, ("xnat", i))
                for b in range(4):
                    last = nc.tensor.transpose(bank[i][:, b * P:(b + 1) * P], xT[:, 4 * half + b, tt * P:(tt + 1) * P],
                                               C("ident"))
                B.finish(last, ("xnat", i))
            for k in range(KD):
                pe.wait_ge(h_ready, KD * 3 + k + 1)
            pe.wait_ge(in_router, 16)
            B.claim(pe, "logits")
            for tt in range(TT):
                for k in range(KD):
                    last = mm(bank[0][:, tt * E:(tt + 1) * E], hT[:, k, tt * P:(tt + 1) * P], router[:, k, :],
                              k == 0, k == KD - 1)
            B.finish(last, "logits")
            for i in range(4):
                tt, half = i // 2, i % 2
                B.claim(pe, ("hnat", i))
                for b in range(4):
                    last = nc.tensor.transpose(bank[4 + i][:, b * P:(b + 1) * P],
                                               hT[:, 4 * half + b, tt * P:(tt + 1) * P], C("ident"))
                B.finish(last, ("hnat", i))
            B.claim(pe, "rank")
            pe.wait_ge(sel_ready, 1)
            sel = oh[:, 2, :]
            mm(bank[1][:, 0:E], C("before"), sel[:, 0:E], True, True)
            mm(bank[1][:, E:2 * E], C("ones"), sel[:, 0:E], True, False)
            mm(bank[1][:, E:2 * E], C("before"), sel[:, E:2 * E], False, True)
            mm(bank[1][:, 2 * E:3 * E], C("ones"), sel[:, 0:E], True, False)
            B.finish(mm(bank[1][:, 2 * E:3 * E], C("ones"), sel[:, E:2 * E], False, True), "rank")

            def gather(job):
                pe.wait_ge(place_ready, job + 1)
                for half in range(2):
                    b = 1 + 2 * half
                    for q in range(4):
                        d = 4 * half + q
                        for tt in range(TT):
                            last = mm(bank[b][:, q * SLOTS:(q + 1) * SLOTS], hnat[:, tt, d * P:(d + 1) * P],
                                      Pm[:, tt, :], tt == 0, tt == 1)
                    last.then_inc(full[b], 1)

            for i in range(4):
                B.released(pe, ("hnat", i))
            gather(0)

            def job_body(job):
                def split_products(tile, act, o, first, last_one):
                    m = EXPERT[tile]
                    for q in range(4):
                        pe.wait_ge(w_lo, job * 4 * NE + (4 * m + q + 1))
                        buf = (4 * m + q) % SPLITS
                        for j in range(2):
                            w_h, w_l = (wsplit[:, buf, part, j * 512:(j + 1) * 512] for part in range(2))
                            mm(o(j), act(q, j, 0), w_h, first(q, j), False)
                            mm(o(j), act(q, j, 1), w_h, False, False)
                            last = mm(o(j), act(q, j, 0), w_l, False, last_one(q, j))
                        last.then_inc(w_used, 1)

                def projected(kind, c, b):
                    if kind == "gate":
                        job_claim(pe, ("g", c), job)
                    split_products((kind, c), lambda q, j, part: hTg[:, part, 2 * q + j, :],
                                   lambda j: bank[b][0:SLOTS, :],
                                   lambda q, j: q == 0 and j == 0, lambda q, j: q == 3 and j == 1)

                def down_chunk(c):
                    job_released(pe, ("hidT", c), job)
                    split_products(("down", c), lambda q, j, part: ehidT[:, c % 2, part, q, :],
                                   lambda j: bank[4 + j][0:SLOTS, :],
                                   lambda q, j: c == 0 and q == 0, lambda q, j: c == NC_F - 1 and q == 3)

                def turn_hidden(c):
                    job_claim(pe, ("hidT", c), job)
                    pe.wait_ge(hid_ready, job * NC_F + (c + 1))
                    for j in range(4):
                        last = nc.tensor.transpose(bank[6][:, j * SLOTS:(j + 1) * SLOTS], ehid[0:SLOTS, j * P:(j + 1) * P],
                                                   cst[0:SLOTS, 0:SLOTS])
                    last.then_inc(full[6], 1)

                job_gathered(pe, job)
                for c in range(NC_F):
                    projected("gate", c, c % 2)
                    if c:
                        turn_hidden(c - 1)
                    projected("up", c, 2 + c % 2)
                    if c:
                        down_chunk(c - 1)
                    else:
                        job_claim(pe, "PT", job)
                        for tt in range(TT):
                            last = nc.tensor.transpose(bank[7][0:SLOTS, tt * P:(tt + 1) * P], Pm[:, tt, :], C("ident"))
                        last.then_inc(full[7], 1)
                turn_hidden(NC_F - 1)
                job_claim(pe, ("gather", 0), job)
                job_claim(pe, ("gather", 1), job)
                gather(job + 1)
                down_chunk(NC_F - 1)
                job_released(pe, "PT", job)
                for i in range(4):
                    tt, half = i // 2, i % 2
                    job_claim(pe, ("sc", i), job)
                    pe.wait_ge(y_ready_e, job * 2 + (half + 1))
                    mm(bank[7 - i % 2][:, :], PT[0:SLOTS, tt, :], ynat[0:SLOTS, half * 512:(half + 1) * 512],
                       True, True).then_inc(full[7 - i % 2], 1)

            with pe.Fori(0, E) as job:
                job_body(job)
            pe.wait_ge(flag_ready, 1)
            more = pe.value_load(flag[0:1, 0:1], min_val=0, max_val=1)
            with pe.If(more > 0):
                with pe.Fori(E, JOBS) as job:
                    job_body(job)

        @block.scalar
        def _(act):
            chain = Chain(act, act_step)
            fn = nc.scalar.activation

            act.dma_start(cst[:, :], const).then_inc(in_const, 16)
            for src, part, r0, c0 in (
                    (ssd_conv_w[0].rearrange("j (b p) -> (j b) p", p=P), 0, 0, 0),
                    (norm_mix.rearrange("i (b p) -> (i b) p", p=P), 1, NORM_MIX, 0),
                    (norm_ffn.rearrange("i (b p) -> (i b) p", p=P), 1, NORM_FFN, 0),
                    (ssd_conv_b[0].rearrange("(b p) -> b p", p=P), 1, CONV_B, 0),
                    (ssd_norm[0].rearrange("(b p) -> b p", p=P), 1, SSD_NORM, 0),
                    (attn_subln, 1, SUBLN, 0),
                    (attn_q_gain, 1, Q_GAIN, 0), (attn_q_gain, 1, Q_GAIN, HD),
                    (attn_k_gain, 1, K_GAIN, 0), (attn_k_gain, 1, K_GAIN, HD)):
                n, wd = src.shape
                act.dma_start(rows[r0:r0 + n, part, c0:c0 + wd], src).then_inc(in_rows, 16)
            act.dma_start(small[0:SH, 16:17], ssd_d[0].rearrange("(n a) -> n a", a=1)).then_inc(in_misc, 16)
            act.dma_start(relb[0:BUCKETS, :], rel_bias).then_inc(in_misc, 16)
            act.dma_start(onehot[:, :], hot).then_inc(in_misc, 16)
            act.dma_start(lam_in, attn_lambda.rearrange("o a d -> o (a d)").broadcast_to([P, 4 * HD])).then_inc(in_lam, 16)

            B.ready(act, "rowsA")
            B.release(nc.scalar.copy(colA[:, :], bank[4][:, 0:96]), "rowsA")
            B.ready(act, "rowsB")
            B.release(nc.scalar.copy(colB[:, 0:ROWS_B], bank[5][:, 0:ROWS_B]), "rowsB")
            B.ready(act, "dcol")
            B.release(nc.scalar.copy(dcol[:, :], bank[6][:, 0:16]), "dcol")
            B.ready(act, "ubias")
            B.release(nc.scalar.copy(ubias[:, :], bank[7][0:HEADS, 0:NDIST]), "ubias")

            def norm(n):
                for b in range(4):
                    B.released(act, ((("x", "attn_acc", "ffn_acc", "ssd_acc")[n]), b))
                    fn(hT[:, 2 * b:2 * b + 2, :], xT[:, 2 * b:2 * b + 2, :], ACT.Square).then_inc(sq_ready, 1)
                B.ready(act, ("ms", n))
                B.release(fn(rstd[:, :], bank[4][:, 0:T], ACT.Ln, bias=C("eps")), ("ms", n))
                B.released(act, ("ms", n))
                fn(rstd[:, :], rstd[:, :], ACT.Exp, scale=-0.5).then_inc(rstd_ready, 1)

            norm(0)
            act.wait_ge(lam_dot, 2)
            fn(small[:, 22:24], small[:, 20:22], ACT.Exp).then_inc(lam_exp, 1)
            for i in range(9):
                if i < 8:
                    B.ready(act, ("qk", i))
                    if i >= 2:
                        B.ready(act, ("qk_ms", i - 2))
                    fn(sqb[:, i % 2, :], bank[i % 4][:, :], ACT.Square).then_inc(qk_sq, 1)
                if i:
                    k = i - 1
                    B.ready(act, ("qk_ms", k))
                    if k >= 2:
                        B.released(act, ("qk", k - 2))
                    B.release(fn(rq[:, k % 2, :], bank[4 + k % 2][:, :], ACT.Ln, bias=C("eps")), ("qk_ms", k))
                    B.released(act, ("qk_ms", k))
                    fn(rq[:, k % 2, :], rq[:, k % 2, :], ACT.Exp, scale=-0.5).then_inc(qk_rstd, 1)
            for i in range(4):
                t, tt = i // 2, i % 2
                B.ready(act, ("v", i))
                B.release(nc.scalar.copy(V[:, tt, t * 512:(t + 1) * 512], bank[6 + i % 2][:, :]), ("v", i))
            for i in range(4):
                B.ready(act, ("bias", i))
                B.release(nc.scalar.copy(bias[:, 2 * i:2 * i + 2, :], bank[i][:, :]), ("bias", i))
            for i in range(HEADS + 4):
                if i < HEADS:
                    act.wait_ge(logit_ready, i + 1)
                    for m in range(2):
                        for qb in range(2):
                            a, n = m * 384 + qb * P, P + qb * P
                            j = 2 * m + qb
                            last = fn(L[:, i % 2, a:a + n], L[:, i % 2, a:a + n], ACT.Exp,
                                      bias=st[:, i % 2, 4 + j:5 + j], accum_out=st[:, i % 2, 8 + j:9 + j])
                    last.then_inc(p_ready, 1)
                h = i - 2
                if 0 <= h < HEADS:
                    B.ready(act, ("at", h))
                    if h >= 2:
                        B.ready(act, ("o", h - 2))
                    B.release(nc.scalar.copy(AT[:, h % 2, :], bank[4][:, 0:384]), ("at", h))
                h = i - 3
                if 0 <= h < HEADS:
                    B.ready(act, ("o", h))
                    if h >= 2:
                        B.ready(act, ("o_ms", h - 2))
                    fn(sqo[:, h % 2, :], bank[5 + h % 2][:, 0:T], ACT.Square).then_inc(o_sq, 1)
                h = i - 4
                if 0 <= h < HEADS:
                    B.ready(act, ("o_ms", h))
                    if h >= 2:
                        B.released(act, ("o", h - 2))
                    B.release(fn(ro[:, h % 2, :], bank[7][:, 0:T], ACT.Ln, bias=C("eps")), ("o_ms", h))
                    B.released(act, ("o_ms", h))
                    fn(ro[:, h % 2, :], ro[:, h % 2, :], ACT.Exp, scale=-0.5).then_inc(o_rstd, 1)

            norm(1)
            units = [(c, hf) for c in range(NC_F) for hf in range(2)]
            for i, (c, hf) in enumerate(units):
                B.ready(act, ("g", c, hf))
                if i >= 4:
                    B.released(act, ("u",) + units[i - 4])
                B.release(fn(sg[:, i % 4, :], bank[4 + hf][:, :], ACT.Silu), ("g", c, hf))

            norm(2)
            act.wait_ge(in_dt, 48)
            fn(alog[:, 0, :], alog[:, 0, :], ACT.Exp).then_inc(a_exp, 1)
            act.wait_ge(sp_abs, 1)
            chain.link(fn(dta[:, :, :], dta[:, :, :], ACT.Exp, scale=-1.0))
            fn(dta[:, :, :], dta[:, :, :], ACT.Ln, bias=C("one")).then_inc(sp_ln, 1)
            act.wait_ge(w0_arg, 1)
            fn(w0, w0, ACT.Exp).then_inc(w0_ready, 1)
            for i in range(13):
                if i < 12:
                    B.ready(act, ("conv", i))
                    if i >= 2:
                        act.wait_ge(conv_out, i - 1)
                    for j in range(2):
                        blk = conv_block(i) + j
                        last = fn(cvb[:, i % 2, j * T:(j + 1) * T], bank[4 + i % 4][:, j * T:(j + 1) * T], ACT.Identity,
                                  bias=colB[:, CONV_B + blk:CONV_B + blk + 1], scale=colA[:, 72 + blk:73 + blk])
                    last.then_inc(conv_first, 1)
                if i:
                    k = i - 1
                    B.released(act, ("conv", k))
                    dest = BT if k < 2 else CT if k < 4 else xsT
                    r = 2 * k - (0 if k < 2 else 4 if k < 4 else 8)
                    fn(dest[:, r:r + 2, :], cvb[:, k % 2, :], ACT.Silu).then_inc(conv_out, 1)
            for g in range(GROUPS):
                B.ready(act, ("z", g, 0))
                B.release(nc.scalar.copy(zr[:, 4 * g:4 * g + 2, :], bank[0][:, :]), ("z", g, 0))
                B.ready(act, ("state", g))
                if g >= 2:
                    B.ready(act, ("y", g - 2, 1))
                B.release(nc.scalar.copy(stS[:, g % 2, :], bank[3][:, :]), ("state", g))
                for half in range(2):
                    for c in range(TT):
                        if c == 0:
                            B.released(act, ("ab", g, half, 0))
                        else:
                            act.wait_ge(arg1_ready, 2 * g + half + 1)
                        fn(dec[:, 2 * half + c, :], dec[:, 2 * half + c, :], ACT.Exp).then_inc(dec_ready, 1)
                    B.ready(act, ("ab", g, half, 1))
                    if g:
                        B.ready(act, ("y", g - 1, half))
                    B.release(fn(eC[:, half, :], bank[4 + 2 * half + 1][:, :], ACT.Exp), ("ab", g, half, 1))
                B.ready(act, ("z", g, 1))
                B.release(nc.scalar.copy(zr[:, 4 * g + 2:4 * g + 4, :], bank[3][:, :]), ("z", g, 1))
            for g in range(GROUPS):
                for hf in range(2):
                    B.released(act, ("z", g, hf))
                fn(zr[:, 4 * g:4 * g + 4, :], zr[:, 4 * g:4 * g + 4, :], ACT.Silu).then_inc(z_silu, 1)
            for g in range(GROUPS):
                act.wait_ge(gated, g + 1)
                fn(zr[:, 4 * g:4 * g + 4, :], xsT[:, 4 * g:4 * g + 4, :], ACT.Square).then_inc(y_sq, 1)
            for g in range(GROUPS):
                B.ready(act, ("y_ms", g))
                if g >= 2:
                    act.wait_ge(y_ready, g - 1)
                B.release(fn(rg[:, g % 2, :], bank[4 + g][:, 0:T], ACT.Ln, bias=C("eps")), ("y_ms", g))
                B.released(act, ("y_ms", g))
                fn(rg[:, g % 2, :], rg[:, g % 2, :], ACT.Exp, scale=-0.5).then_inc(y_rstd, 1)

            norm(3)
            for i in range(4):
                B.ready(act, ("xnat", i))
                B.release(nc.scalar.copy(xnat[:, i // 2, (i % 2) * 512:(i % 2 + 1) * 512], bank[i][:, :]), ("xnat", i))
            for i in range(4):
                B.ready(act, ("hnat", i))
                B.release(nc.scalar.copy(hnat[:, i // 2, (i % 2) * 512:(i % 2 + 1) * 512], bank[4 + i][:, :]), ("hnat", i))
            act.wait_ge(top_diff, 1)
            fn(tw[:, 1, 0:TT], tw[:, 0, 0:TT], ACT.Exp).then_inc(top_exp, 1)

            def gathered(ready):
                for half in range(2):
                    ready(act, half)
                    nc.scalar.copy(hTg[:, 0, 4 * half:4 * half + 4, :], bank[1 + 2 * half][:, 0:4 * SLOTS])\
                        .then_inc(hg_hi, 1)

            def first_gather(eng, half):
                b = 1 + 2 * half
                eng.wait_ge(full[b], dense_uses[b] + 1)

            gathered(first_gather)

            def job_body(job):
                def split(tile):
                    w = expert_landed(act, tile, job)
                    for q in range(4):
                        n = 4 * EXPERT[tile] + q
                        act.wait_ge(w_used, job * 4 * NE + (n + 1))
                        nc.scalar.copy(wsplit[:, n % SPLITS, 0, :].rearrange("p (k n) -> p k n", n=w.shape[2]),
                                       quarter(w, q)).then_inc(w_hi, 1)

                def hidden_hi(c):
                    job_ready(act, ("hidT", c), job)
                    nc.scalar.copy(ehidT[:, c % 2, 0, :, :], bank[6][:, 0:4 * SLOTS]).then_inc(hid_hi, 1)

                for tile in ET:
                    kind, c = tile
                    split(tile)
                    if kind == "up":
                        if c:
                            hidden_hi(c - 1)
                        tile_finished(act, ("gate", c), job)
                        fn(esg[0:SLOTS, c % 2, :], bank[c % 2][0:SLOTS, :], ACT.Silu).then_inc(free[c % 2], 1)
                    if tile == ("gate", 1):
                        job_ready(act, "PT", job)
                        nc.scalar.copy(PT[0:SLOTS, :, :], bank[7][0:SLOTS, 0:T]).then_inc(free[7], 1)
                hidden_hi(NC_F - 1)
                gathered(lambda eng, half: job_ready(eng, ("gather", half), job))
                tile_finished(act, ("down", NC_F - 1), job)
                for half in range(2):
                    nc.scalar.copy(ynat[0:SLOTS, half * 512:(half + 1) * 512], bank[4 + half][0:SLOTS, :])\
                        .then_inc(y_ready_e, 1)

            with act.Fori(0, E) as job:
                job_body(job)
            act.wait_ge(flag_ready, 1)
            more = act.value_load(flag[0:1, 0:1], min_val=0, max_val=1)
            with act.If(more > 0):
                with act.Fori(E, JOBS) as job:
                    job_body(job)

        @block.vector
        def _(dve):
            chain = Chain(dve, dve_step)
            link = chain.link
            V_ = nc.vector
            tt_, ts_, stt = V_.tensor_tensor, V_.tensor_scalar, V_.scalar_tensor_tensor

            dve.wait_ge(in_const, 16)
            dve.wait_ge(in_misc, 16 * N_MISC)
            V_.memset(relb[BUCKETS:BUCKETS + 1, :], MASKED).then_inc(relb_set, 1)
            ts_(small[0:SH, 0:16], C("pair_of", SH), small[0:SH, 16:17], None, ALU.mult).then_inc(relb_set, 1)
            dve.wait_ge(in_lam, 16)
            for j in range(2):
                V_.tensor_tensor_reduce(lam_in[:, 2 * j * HD:(2 * j + 1) * HD], lam_in[:, 2 * j * HD:(2 * j + 1) * HD],
                                        lam_in[:, (2 * j + 1) * HD:(2 * j + 2) * HD], 1.0, 0.0, ALU.mult, ALU.add,
                                        small[:, 20 + j:21 + j]).then_inc(lam_dot, 1)
            B.released(dve, "rowsB")
            link(ts_(small[:, 25:26], colB[:, Q_GAIN:Q_GAIN + 1], HD ** -0.5, None, ALU.mult))
            link(ts_(small[:, 26:27], colB[:, SUBLN:SUBLN + 1], 1.0 - LAMBDA_INIT, None, ALU.mult))
            for i in range(4):
                B.ready(dve, ("x", i))
                B.release(V_.tensor_copy(xT[:, 2 * i:2 * i + 2, :], bank[4 + i][:, :]), ("x", i))

            def norm(n):
                col = (NORM_MIX, NORM_FFN)[n % 2] + KD * (n // 2)
                dve.wait_ge(rstd_ready, n + 1)
                for k in range(KD):
                    stt(out=hT[:, k, :], in0=xT[:, k, :], scalar=colB[:, col + k:col + k + 1], in1=rstd[:, :],
                        op0=ALU.mult, op1=ALU.mult).then_inc(h_ready, 1)

            def residual(acc):
                for b in range(4):
                    B.ready(dve, (acc, b))
                    B.release(tt_(xT[:, 2 * b:2 * b + 2, :], xT[:, 2 * b:2 * b + 2, :],
                                  bank[b][:, :].rearrange("p (a t) -> p a t", a=2), ALU.add), (acc, b))

            norm(0)
            dve.wait_ge(lam_exp, 1)
            link(tt_(small[:, 24:25], small[:, 23:24], small[:, 22:23], ALU.subtract))
            ts_(small[:, 24:25], small[:, 24:25], -LAMBDA_INIT, None, ALU.add).then_inc(lam_ready, 1)
            for i in range(8):
                t, hf = i // 2, i % 2
                dest, gain = (qT, small[:, 25:26]) if t % 2 == 0 else (kT, colB[:, K_GAIN:K_GAIN + 1])
                h = 4 * (t // 2) + 2 * hf
                dve.wait_ge(qk_rstd, i + 1)
                B.ready(dve, ("qk", i))
                B.release(stt(out=dest[:, h:h + 2, :], in0=bank[i % 4][:, :].rearrange("p (a t) -> p a t", a=2),
                              scalar=gain, in1=rq[:, i % 2, :].rearrange("p (a t) -> p a t", a=2),
                              op0=ALU.mult, op1=ALU.mult), ("qk", i))
            for i in range(4):
                B.released(dve, ("bias", i))
            dve.wait_ge(lam_ready, 1)
            for i in range(HEADS + 4):
                if i < HEADS:
                    s = st[:, i % 2, :]
                    if i >= 2:
                        dve.wait_ge(attn_ready, i - 1)
                    for m in range(2):
                        B.ready(dve, ("s", i, m))
                        b = bank[2 * m + i % 2]
                        for qb in range(2):
                            a, n = qb * P, P + qb * P
                            j = 2 * m + qb
                            last = V_.tensor_tensor_reduce(L[:, i % 2, m * 384 + a:m * 384 + a + n], b[:, a:a + n],
                                                           bias[:, i, T - n:T], 1.0, -3e38, ALU.add, ALU.max,
                                                           s[:, j:j + 1])
                        B.release(last, ("s", i, m))
                    for m in range(2):
                        B.released(dve, ("s", i, m))
                    ts_(s[:, 4:8], s[:, 0:4], -1.0, None, ALU.mult).then_inc(logit_ready, 1)
                h = i - 1
                if 0 <= h < HEADS:
                    s = st[:, h % 2, :]
                    dve.wait_ge(p_ready, h + 1)
                    if h >= 2:
                        B.ready(dve, ("at", h - 2))
                    link(V_.reciprocal(s[:, 8:12], s[:, 8:12]))
                    link(ts_(s[:, 12:14], s[:, 10:12], small[:, 24:25], None, ALU.mult))
                    for qb in range(2):
                        a, n = qb * P, P + qb * P
                        last = ts_(A[:, h % 2, a:a + n], L[:, h % 2, a:a + n], s[:, 8 + qb:9 + qb], None, ALU.mult)
                    link(last)
                    for qb in range(2):
                        a, n = qb * P, P + qb * P
                        last = stt(out=A[:, h % 2, a:a + n], in0=L[:, h % 2, 384 + a:384 + a + n],
                                   scalar=s[:, 12 + qb:13 + qb], in1=A[:, h % 2, a:a + n], op0=ALU.mult, op1=ALU.add)
                    last.then_inc(attn_ready, 1)
                h = i - 4
                if 0 <= h < HEADS:
                    dve.wait_ge(o_rstd, h + 1)
                    B.release(stt(out=oT[:, h, :], in0=bank[5 + h % 2][:, 0:T], scalar=small[:, 26:27],
                                  in1=ro[:, h % 2, :], op0=ALU.mult, op1=ALU.mult), ("o", h))
            residual("attn_acc")

            norm(1)
            for i, (c, hf) in enumerate((c, hf) for c in range(NC_F) for hf in range(2)):
                B.released(dve, ("g", c, hf))
                B.ready(dve, ("u", c, hf))
                B.release(tt_(hid[:, c % 2, 2 * hf:2 * hf + 2, :], sg[:, i % 4, :].rearrange("p (a t) -> p a t", a=2),
                              bank[6 + hf][:, :].rearrange("p (a t) -> p a t", a=2), ALU.mult), ("u", c, hf))
            residual("ffn_acc")

            norm(2)
            dve.wait_ge(in_dt, 48)
            B.ready(dve, "dt")
            B.release(tt_(dtv[:, :, :], bank[5][:, 0:TT * SH].rearrange("p (c h) -> p c h", c=TT),
                          alog[:, 1, :].unsqueeze(1).broadcast_to([P, TT, SH]), ALU.add), "dt")
            B.released(dve, "dt")
            stt(out=dta[:, :, :], in0=dtv[:, :, :], scalar=-1.0, in1=dtv[:, :, :], op0=ALU.mult,
                op1=ALU.max).then_inc(sp_abs, 1)
            dve.wait_ge(sp_ln, 1)
            link(stt(out=dtv[:, :, :], in0=dtv[:, :, :], scalar=0.0, in1=dta[:, :, :], op0=ALU.max, op1=ALU.add))
            dve.wait_ge(a_exp, 1)
            stt(out=da[:, :, :], in0=dtv[:, :, :], scalar=-1.0,
                in1=alog[:, 0, :].unsqueeze(1).broadcast_to([P, TT, SH]), op0=ALU.mult, op1=ALU.mult).then_inc(da_ready, 1)
            B.ready(dve, "acs")
            link(V_.tensor_copy(acs[:, :, :], bank[6][:, 0:TT * SH].rearrange("p (c h) -> p c h", c=TT)))
            link(tt_(w0, bank[6][:, 64:64 + SH], acs[:, 0, :], ALU.subtract))
            B.release(V_.tensor_copy(small[:, 30:31], small[:, 24:25]), "acs")
            V_.tensor_copy(small[:, 31:32], small[:, 24:25]).then_inc(w0_arg, 1)
            for i in range(12):
                dve.wait_ge(conv_first, i + 1)
                for tap in range(3):
                    sh = 3 - tap
                    for j in range(2):
                        blk = conv_block(i) + j
                        o = cvb[:, i % 2, j * T + sh:(j + 1) * T]
                        last = stt(out=o, in0=bank[4 + i % 4][:, j * T:(j + 1) * T - sh],
                                   scalar=colA[:, 24 * tap + blk:24 * tap + blk + 1], in1=o, op0=ALU.mult, op1=ALU.add)
                    if tap < 2:
                        link(last)
                B.release(last, ("conv", i))
            for g in range(GROUPS):
                for c in range(TT):
                    B.ready(dve, ("xn", g, c))
                    if g >= 2 and c == 0:
                        B.ready(dve, ("y", g - 2, 1))
                    B.release(tt_(xd[:, g % 2, c * 512:(c + 1) * 512].rearrange("p (h d) -> p h d", d=HD),
                                  bank[1 + c][:, :].rearrange("p (h d) -> p h d", d=HD),
                                  dtv[:, c, g * HPG:(g + 1) * HPG].unsqueeze(2).broadcast_to([P, HPG, HD]), ALU.mult),
                              ("xn", g, c))
                    if c == 0:
                        B.ready(dve, ("cb", g))
                        if g >= 2:
                            B.ready(dve, ("state", g - 2))
                        tt_(cbm[:, g % 2, :].rearrange("p (c l) -> p c l", l=P),
                            bank[0][:, 0:T].rearrange("p (c l) -> p c l", l=P),
                            C("upto").unsqueeze(1).broadcast_to([P, TT, P]), ALU.mult).then_inc(cbm_ready, 1)
                        B.release(V_.tensor_copy(Bn[:, g % 2, :], bank[0][:, T:T + P]), ("cb", g))
                for half in range(2):
                    for c in range(TT):
                        B.ready(dve, ("ab", g, half, c))
                        if g and c == 0:
                            B.ready(dve, ("y", g - 1, half))
                        for q in range(4):
                            h = g * HPG + 4 * half + q
                            last = ts_(dec[:, 2 * half + c, q * P:(q + 1) * P],
                                       bank[4 + 2 * half + c][:, q * P:(q + 1) * P], acs[:, c, h:h + 1], 0.0,
                                       ALU.subtract, ALU.min)
                        if c == 0:
                            B.release(last, ("ab", g, half, 0))
                        else:
                            last.then_inc(arg1_ready, 1)
                dve.wait_ge(cbm_ready, g + 1)
                for half in range(2):
                    for c in range(TT):
                        dve.wait_ge(dec_ready, 4 * g + 2 * half + c + 1)
                        o = dec[:, 2 * half + c, :].rearrange("p (h l) -> p h l", l=P)
                        tt_(o, o, cbm[:, g % 2, c * P:(c + 1) * P].unsqueeze(1).broadcast_to([P, 4, P]),
                            ALU.mult).then_inc(m_ready, 1)
                for half in range(2):
                    B.ready(dve, ("y", g, half))
                    for j in range(2):
                        blk = 4 * g + 2 * half + j
                        last = stt(out=xsT[:, blk, :], in0=xsT[:, blk, :], scalar=dcol[:, blk:blk + 1],
                                   in1=bank[1 + half][:, j * T:(j + 1) * T], op0=ALU.mult, op1=ALU.add)
                    B.release(last, ("y", g, half))
            for g in range(GROUPS):
                dve.wait_ge(z_silu, g + 1)
                B.released(dve, ("y", g, 1))
                tt_(xsT[:, 4 * g:4 * g + 4, :], xsT[:, 4 * g:4 * g + 4, :], zr[:, 4 * g:4 * g + 4, :],
                    ALU.mult).then_inc(gated, 1)
            for g in range(GROUPS):
                dve.wait_ge(y_rstd, g + 1)
                for b in range(4):
                    blk = 4 * g + b
                    last = stt(out=xsT[:, blk, :], in0=xsT[:, blk, :], scalar=colB[:, SSD_NORM + blk:SSD_NORM + blk + 1],
                               in1=rg[:, g % 2, :], op0=ALU.mult, op1=ALU.mult)
                last.then_inc(y_ready, 1)
            residual("ssd_acc")

            norm(3)
            def per_expert(v):
                return v.rearrange("p (t e) -> p t e", e=E)

            B.ready(dve, "logits")
            lg_ = lg[:, :, :]
            B.release(V_.tensor_copy(lg_, bank[0][:, 0:TT * E].rearrange("p (t e) -> p t e", e=E)), "logits")
            B.released(dve, "logits")
            order = C("rank_of").unsqueeze(1).broadcast_to([P, TT, E])
            tmp = per_expert(tw[:, 2, :])

            def best(v, oh_k, m_k, s_k):
                link(V_.tensor_reduce(m_k, v, AX_X, ALU.max))
                link(tt_(tmp, v, m_k.unsqueeze(2).broadcast_to([P, TT, E]), ALU.is_ge))
                link(tt_(tmp, tmp, order, ALU.mult))
                link(V_.tensor_reduce(s_k, tmp, AX_X, ALU.max))
                link(tt_(oh_k, order, s_k.unsqueeze(2).broadcast_to([P, TT, E]), ALU.is_equal))

            oh1, oh2, sel, comb = (per_expert(oh[:, j, :]) for j in range(4))
            m1, m2, s1, s2 = (tw[:, 3 + j, 0:TT] for j in range(4))
            best(lg_, oh1, m1, s1)
            lg2 = per_expert(tw[:, 7, :])
            link(stt(out=lg2, in0=oh1, scalar=-3e38, in1=lg_, op0=ALU.mult, op1=ALU.add))
            best(lg2, oh2, m2, s2)
            tt_(tw[:, 0, 0:TT], m2, m1, ALU.subtract).then_inc(top_diff, 1)
            tt_(sel, oh1, oh2, ALU.add).then_inc(sel_ready, 1)
            dve.wait_ge(top_exp, 1)
            w1, w2, den = tw[:, 8, 0:TT], tw[:, 9, 0:TT], tw[:, 10, 0:TT]
            link(ts_(den, tw[:, 1, 0:TT], 1.0, None, ALU.add))
            link(V_.reciprocal(w1, den))
            link(tt_(w2, w1, tw[:, 1, 0:TT], ALU.mult))
            link(tt_(comb, oh1, w1.unsqueeze(2).broadcast_to([P, TT, E]), ALU.mult))
            link(tt_(tmp, oh2, w2.unsqueeze(2).broadcast_to([P, TT, E]), ALU.mult))
            link(tt_(comb, comb, tmp, ALU.add))
            for p in range(PASSES):
                link(V_.tensor_copy(cj[:, :, p * E:(p + 1) * E], comb))
            B.ready(dve, "rank")
            dve.wait_ge(sel_ready, 1)
            rank = per_expert(tw[:, 11, :])
            link(stt(out=rank, in0=bank[1][:, 0:2 * E].rearrange("p (t e) -> p t e", e=E), scalar=1.0, in1=sel,
                     op0=ALU.add, op1=ALU.mult))
            for p in range(PASSES):
                link(ts_(rj[:, :, p * E:(p + 1) * E], rank, -1.0 - p * SLOTS, None, ALU.add))
            link(V_.memset(rj[:, :, JOBS:JOBS + 1], -1.0))
            link(V_.tensor_reduce(tw[:, 0, 0:1], bank[1][:, 2 * E:3 * E], AX_X, ALU.max))
            B.release(ts_(flag[:, 0:1], tw[:, 0, 0:1], float(SLOTS), None, ALU.is_gt), "rank")
            B.released(dve, "rank")
            V_.tensor_copy(flag[:, 1:2], flag[:, 0:1]).then_inc(flag_ready, 1)

            def places(job):
                for tt in range(TT):
                    last = ts_(Pm[:, tt, :], C("slot_no"), rj[:, tt, bass.ds(job, 1)], None, ALU.is_equal)
                last.then_inc(place_ready, 1)

            for i in range(4):
                B.released(dve, ("hnat", i))
            places(0)
            for i in range(4):
                B.released(dve, ("xnat", i))

            def gathered(job, ready):
                for half in range(2):
                    ready(dve, half)
                    dve.wait_ge(hg_hi, job * 2 + (half + 1))
                    b = 1 + 2 * half
                    o = hTg[:, :, 4 * half:4 * half + 4, :]
                    tt_(o[:, 1], bank[b][:, 0:4 * SLOTS].rearrange("p (k n) -> p k n", k=4), o[:, 0].bitcast(F32),
                        ALU.subtract).then_inc(free[b], 1)

            gathered(0, lambda eng, half: eng.wait_ge(full[1 + 2 * half], dense_uses[1 + 2 * half] + 1))

            def job_body(job):
                def split(tile):
                    w = expert_landed(dve, tile, job)
                    for q in range(4):
                        n = 4 * EXPERT[tile] + q
                        dve.wait_ge(w_hi, job * 4 * NE + (n + 1))
                        hi, lo = (wsplit[:, n % SPLITS, part, :].rearrange("p (k n) -> p k n", n=w.shape[2])
                                  for part in range(2))
                        tt_(lo, quarter(w, q), hi.bitcast(F32), ALU.subtract).then_inc(w_lo, 1)

                def hidden(c):
                    job_released(dve, ("g", c), job)
                    tile_finished(dve, ("up", c), job)
                    if c:
                        job_ready(dve, ("hidT", c - 1), job)
                    tt_(ehid[0:SLOTS, :], esg[0:SLOTS, c % 2, :], bank[2 + c % 2][0:SLOTS, :], ALU.mult)\
                        .then_inc(hid_ready, 1)

                def hidden_lo(c):
                    dve.wait_ge(hid_hi, job * NC_F + (c + 1))
                    tt_(ehidT[:, c % 2, 1, :, :], bank[6][:, 0:4 * SLOTS].rearrange("p (k n) -> p k n", k=4),
                        ehidT[:, c % 2, 0, :, :].bitcast(F32), ALU.subtract).then_inc(free[6], 1)

                for tile in ET:
                    kind, c = tile
                    split(tile)
                    if kind == "up" and c:
                        hidden_lo(c - 1)
                    if tile == ("gate", 1):
                        hidden(0)
                    elif kind == "down" and c < NC_F - 1:
                        hidden(c + 1)
                    if tile == ("gate", 2):
                        job_ready(dve, "PT", job)
                        places(job + 1)
                hidden_lo(NC_F - 1)
                gathered(job + 1, lambda eng, half: job_ready(eng, ("gather", half), job))
                for i in range(4):
                    tt, half = i // 2, i % 2
                    job_ready(dve, ("sc", i), job)
                    o = xnat[:, tt, half * 512:(half + 1) * 512]
                    stt(out=o, in0=bank[7 - i % 2][:, :], scalar=cj[:, tt, bass.ds(job, 1)], in1=o,
                        op0=ALU.mult, op1=ALU.add).then_inc(free[7 - i % 2], 1)
                for i in (2, 3):
                    job_released(dve, ("sc", i), job)

            with dve.Fori(0, E) as job:
                job_body(job)
            more = dve.value_load(flag[0:1, 0:1], min_val=0, max_val=1)
            with dve.If(more > 0):
                with dve.Fori(E, JOBS) as job:
                    job_body(job)
            V_.memset(small[:, 40:41], 0.0).then_inc(moe_done, 1)


INPUTS = ["x", "rel_bias", "norm_mix", "norm_ffn", "attn_w_in", "attn_q_gain", "attn_k_gain", "attn_lambda",
          "attn_subln", "attn_w_out", "ffn_w_gate", "ffn_w_up", "ffn_w_down", "ssd_w_in", "ssd_conv_w",
          "ssd_conv_b", "ssd_dt_bias", "ssd_a_log", "ssd_d", "ssd_norm", "ssd_w_out", "moe_router",
          "moe_w_gate", "moe_w_up", "moe_w_down"]


def kernel(**inputs):
    import concourse.bacc as bacc
    from concourse.bass_utils import run_bass_kernel_spmd

    nc = bacc.Bacc("TRN2", target_bir_lowering=False, num_devices=1)
    const, hot = constants()
    arrays = {name: np.ascontiguousarray(inputs[name]) for name in INPUTS}
    arrays["const"], arrays["hot"] = const, hot
    args = [nc.dram_tensor(name, a.shape, mybir.dt.from_np(a.dtype), kind="ExternalInput").ap()
            for name, a in arrays.items()]
    args.append(nc.dram_tensor("out", (1, T, D), F32, kind="ExternalOutput").ap())
    hybrid_trunk(nc, *args)
    result = run_bass_kernel_spmd(nc, [arrays], core_ids=[0])
    return result.results[0]["out"]
```

```python
import math
from contextlib import ExitStack

import numpy as np

import concourse.bass as bass
from concourse import mybir

F32 = mybir.dt.float32
F32R = mybir.dt.float32r
I32 = mybir.dt.int32
ALU = mybir.AluOpType
ACT = mybir.ActivationFunctionType
AX_X = mybir.AxisListType.X

P = 128
D = 1024
KD = D // P
T = 256
TT = T // P
HEADS = 8
HD = 64
F = 3584
NC_F = F // 512
DI = 2048
GROUPS = 4
NSTATE = 128
SH = 32
HPG = SH // GROUPS
E = 8
SLOTS = 96
PASSES = 3
JOBS = E * PASSES
LAMBDA_INIT = 0.8 - 0.6 * math.exp(0.0)
EPS = 1e-6
MASKED = -1e30
BUCKETS = 32
DENSE_RING = 3
RING = 7
SPLITS = 3
EXPERT_SPLITS = 4
QUARTER = 1024
SLOT = 4096

CONSTS = {}
_at = 0
for _name, _n in (("ident", 128), ("anti", 128), ("mean_d", 128), ("mean_hd", 128), ("mean_v", 128),
                  ("mean_g", 128), ("upto", 128), ("before", 128), ("ones", 128), ("slot_no", SLOTS),
                  ("rank_of", E), ("eps", 1), ("one", 1), ("odd_even", 128), ("pair_of", 16)):
    CONSTS[_name] = (_at, _at + _n)
    _at += _n
NCONST = _at
NORM_MIX, NORM_FFN, CONV_B, SSD_NORM, SUBLN, Q_GAIN, K_GAIN = 0, 16, 32, 56, 72, 73, 74
ROWS_B = 75
NDIST = 2 * P + P - 1


def constants():
    c = np.zeros((P, NCONST), np.float32)
    i = np.arange(P)

    def put(name, v):
        a, b = CONSTS[name]
        c[:, a:b] = v

    put("ident", np.eye(P))
    put("anti", np.eye(P)[::-1])
    put("mean_d", 1.0 / D)
    put("mean_hd", (i[:, None] // HD == i[None, :] // HD) / HD)
    put("mean_v", 1.0 / P)
    put("mean_g", 1.0 / (DI // GROUPS))
    put("upto", i[:, None] <= i[None, :])
    put("before", i[:, None] < i[None, :])
    put("ones", 1.0)
    put("slot_no", np.arange(SLOTS)[None, :])
    put("rank_of", (E - np.arange(E))[None, :])
    put("eps", EPS)
    put("one", 1.0)
    put("odd_even", i[:, None] % 2 == i[None, :] // HD)
    put("pair_of", i[:, None] // 2 == np.arange(16)[None, :])
    dist = 255 - np.arange(NDIST)
    n = np.maximum(dist, 0)
    exact = BUCKETS // 2
    large = exact + (np.log(np.maximum(n, 1).astype(np.float32) / np.float32(exact)) / np.float32(math.log(128 / exact))
                     * np.float32(BUCKETS - exact)).astype(np.int32)
    bucket = np.where(n < exact, n, np.minimum(large, BUCKETS - 1))
    hot = np.zeros((BUCKETS + 1, NDIST), np.float32)
    for j in range(NDIST):
        hot[BUCKETS if dist[j] < 0 else bucket[j], j] = 1.0
    return c, hot


N_ROWS, N_MISC = 10, 3


def conv_block(i):
    return 16 + 2 * i if i < 4 else 2 * i - 8


class Chain:

    def __init__(self, eng, sem):
        self.eng, self.sem, self.n = eng, sem, 0

    def link(self, ins):
        self.n += 1
        ins.then_inc(self.sem, 1)
        self.eng.wait_ge(self.sem, self.n)


class Banks:

    def __init__(self, full, free, tile_end):
        self.full, self.free, self.tile_end = full, free, tile_end
        self.count, self.fulls = [0] * 8, [0] * 8
        self.at = {}

    def plan(self, name, bank, tile=None):
        self.at[name] = (bank, self.count[bank], self.fulls[bank], tile)
        self.count[bank] += 1
        self.fulls[bank] += tile is None

    def claim(self, pe, name):
        b, k = self.at[name][:2]
        if k:
            pe.wait_ge(self.free[b], k)

    def finish(self, ins, name):
        assert self.at[name][3] is None
        ins.then_inc(self.full[self.at[name][0]], 1)

    def ready(self, eng, name):
        b, _, k, tile = self.at[name]
        if tile:
            self.tile_end(eng, tile)
        else:
            eng.wait_ge(self.full[b], k + 1)

    def release(self, ins, name):
        ins.then_inc(self.free[self.at[name][0]], 1)

    def released(self, eng, name):
        b, k = self.at[name][:2]
        eng.wait_ge(self.free[b], k + 1)


def dense_tiles():
    tiles = []
    for t in range(2):
        tiles += [("attn_q", t), ("attn_k", t)]
    tiles += [("attn_v", 0), ("attn_v", 1), ("attn_out", 0), ("attn_out", 1)]
    for c in range(NC_F):
        tiles += [("ffn_gate", c), ("ffn_up", c)]
        if c:
            tiles.append(("ffn_down", c - 1))
    tiles.append(("ffn_down", NC_F - 1))
    tiles += [("ssd_b", 0), ("ssd_c", 0)] + [("ssd_x", t) for t in range(4)] + [("ssd_z", t) for t in range(4)]
    tiles += [("ssd_out", t) for t in range(4)]
    return tiles


def expert_tiles():
    tiles = []
    for c in range(NC_F):
        tiles += [("gate", c), ("up", c)]
        if c:
            tiles.append(("down", c - 1))
    tiles.append(("down", NC_F - 1))
    return tiles


def hybrid_trunk(nc, x, rel_bias, norm_mix, norm_ffn, attn_w_in, attn_q_gain, attn_k_gain, attn_lambda,
                 attn_subln, attn_w_out, ffn_w_gate, ffn_w_up, ffn_w_down, ssd_w_in, ssd_conv_w, ssd_conv_b,
                 ssd_dt_bias, ssd_a_log, ssd_d, ssd_norm, ssd_w_out, moe_router, moe_w_gate, moe_w_up,
                 moe_w_down, const, hot, out):
    DT = dense_tiles()
    DENSE = {name: n for n, name in enumerate(DT)}
    ND = len(DT)
    ET = expert_tiles()
    EXPERT = {name: m for m, name in enumerate(ET)}
    NE = len(ET)
    assert NE % RING == 0

    with ExitStack() as ctx:
        def sb(name, shape, dt=F32):
            return ctx.enter_context(nc.sbuf_tensor(name, shape, dt))

        def sem(name):
            return ctx.enter_context(nc.semaphore(name))

        cst = sb("cst", [P, NCONST])
        colA = sb("colA", [P, 96])
        colB = sb("colB", [P, 80])
        rows = sb("rows", [P, 2, P])
        dcol = sb("dcol", [P, 16])
        small = sb("small", [P, 64])
        rstd = sb("rstd", [P, T])
        relb = sb("relb", [BUCKETS + 1, HEADS])
        flag = sb("flag", [P, 2], I32)
        tables = sb("tables", [P, 768])
        split_mem = sb("split_mem", [P, SPLITS * 2 * QUARTER + 3 * 2048], F32R)
        wsplit = split_mem[:, 0:EXPERT_SPLITS * 2 * QUARTER].rearrange("p (s a b) -> p s a b", s=EXPERT_SPLITS, a=2)

        def act_parts(at, *shape):
            names = " ".join("abcd"[:len(shape)])
            at += SPLITS * 2 * QUARTER
            return split_mem[:, at:at + int(np.prod(shape))].rearrange(
                f"p ({names}) -> p {names}", **{"abcd"[i]: n for i, n in enumerate(shape)})

        h2 = act_parts(0, 2, KD, T)
        in2 = [act_parts(at, 2, 4, T) for at in (4096, 0, 2048)]
        hTg = act_parts(2048, 2, KD, SLOTS)
        ehidT = act_parts(2048 + 1536, 2, 2, 4, SLOTS)
        HEAD = KD * T
        SLOT_AT = 4 * HEAD
        mem = sb("mem", [P, SLOT_AT + RING * SLOT])
        xT = mem[:, 0:HEAD].rearrange("p (k t) -> p k t", k=KD)
        hT = mem[:, HEAD:2 * HEAD].rearrange("p (k t) -> p k t", k=KD)

        def slot_mem(s):
            return mem[:, SLOT_AT + s * SLOT:SLOT_AT + (s + 1) * SLOT]

        DENSE_SLOT = [4, 5, 6]
        EXPERT_SLOT = [3, 0, 1, 2, 4, 5, 6]

        def carve(spec, region, at, end):
            got = []
            for shape in spec:
                n = int(np.prod(shape))
                v = region[:, at:at + n]
                if len(shape) > 1:
                    names = " ".join("abc"[:len(shape)])
                    v = v.rearrange(f"p ({names}) -> p {names}", **{"abc"[i]: s for i, s in enumerate(shape)})
                got.append(v)
                at += n
            assert at <= end, (at, end)
            return got

        LAYER = (mem, 2 * HEAD, SLOT_AT + 3 * SLOT)
        spec = [(HEADS, T), (HEADS, T), (TT, D), (HEADS, T), (HEADS, T), (2, 384), (2, 384), (4 * HD,), (2, 16)]
        qT, kT, V, oT, bias, A, AT, lam_in, st, sqb, rq = carve(spec + [(2, 512), (2, 512)], *LAYER)
        L = carve(spec + [(2, 2 * 384)], *LAYER)[-1]
        hid, sg = carve([(2, 4 * T), (4, 512)], *LAYER)
        hid = hid.rearrange("p b (f t) -> p b f t", f=4)
        (xsT, BT, CT, xd, xw, Bn, cbm, stS, dec, eC, cvb, wdt, dtv, dta, da, acs, w0, alog, rg) = carve(
            [(16, T), (4, T), (4, T), (2, 2 * 512), (2, 512), (2, P), (2, 2 * P), (2, 512), (4, 512), (2, 512),
             (2, 512), (KD, SH), (TT, SH), (TT, SH), (TT, SH), (TT, SH), (SH,), (2, SH), (2, T)], *LAYER)
        zr = slot_mem(3).rearrange("p (b t) -> p b t", b=16)
        xin = slot_mem(3)[:, 0:TT * D].rearrange("p (a b) -> p a b", a=TT)
        hankel = slot_mem(3)[:, TT * D:SLOT].rearrange("p (h t) -> p h t", h=HEADS)
        onehot, ubias = tables[0:BUCKETS + 1, 0:NDIST], tables[0:HEADS, 384:384 + NDIST]
        scratch = nc.dram_tensor("bias_by_distance", (HEADS, 512), F32).ap()
        xnat, hnat = carve([(TT, D), (TT, D)], mem, 2 * HEAD, SLOT_AT)
        ehid, esg, Pm, PT, ynat = carve([(512,), (2, 512), (TT, SLOTS), (TT, P), (D,)], mem, 0, 2 * HEAD)
        lg, oh, tw, rj, cj, router = carve(
            [(TT, E), (4, TT * E), (12, TT * E), (TT, JOBS + 1), (TT, JOBS + 1), (KD, E)], tables, 0, 768)

        dense_in_slot = [sum(1 for n in range(ND) if DENSE_SLOT[n % DENSE_RING] == s) for s in range(RING)]

        def expert_landed(eng, tile, job):
            m = EXPERT[tile]
            s = EXPERT_SLOT[m % RING]
            eng.wait_ge(landed[s], job * (16 * NE // RING) + 16 * (dense_in_slot[s] + m // RING + 1))
            return view(tile[0], s)

        def quarter(w, q):
            n = w.shape[1] // 4
            return w[:, n * q:n * (q + 1), :]

        def C(name, n=P):
            a, b = CONSTS[name]
            return cst[0:n, a:b]

        bank = [ctx.enter_context(nc.psum_tensor(f"bank{b}", [P, 512], F32)) for b in range(8)]
        full = [sem(f"full{b}") for b in range(8)]
        free = [sem(f"free{b}") for b in range(8)]
        w_hi, w_lo = sem("w_hi"), sem("w_lo")
        w_used = sem("w_used")

        def dense_tile_end(eng, tile):
            eng.wait_ge(w_used, 4 * DENSE[tile] + 4)

        B = Banks(full, free, dense_tile_end)
        CONV_TILES = [("ssd_b", 0), ("ssd_c", 0)] + [("ssd_x", t) for t in range(4)]

        PAIR_AT = {2 * b + 5: b for b in range(4)}
        B.plan("rowsA", 0), B.plan("rowsB", 1), B.plan("dcol", 2), B.plan("ubias", 3)
        for i in range(4):
            B.plan(("x", i), 4 + i)
        B.plan(("ms", 0), 4)
        for t in range(5):
            for hf in range(2):
                if t < 4:
                    B.plan(("qk", 2 * t + hf), (2 * t + hf) % 4, ("attn_k" if t % 2 else "attn_q", t // 2))
            for hf in range(2):
                if t:
                    B.plan(("qk_ms", 2 * t - 2 + hf), 4 + hf)
        for i in range(4):
            B.plan(("v", i), 6 + i % 2, ("attn_v", i // 2))
        for i in range(4):
            B.plan(("bias", i), i)
        for i in range(HEADS + 4):
            if i < HEADS:
                B.plan(("s", i, 0), i % 2), B.plan(("s", i, 1), 2 + i % 2)
            if 0 <= i - 2 < HEADS:
                B.plan(("at", i - 2), 4)
            if 0 <= i - 3 < HEADS:
                B.plan(("o", i - 3), 5 + (i - 3) % 2)
            if i in PAIR_AT:
                B.plan(("o_ms", PAIR_AT[i]), 7)
        for b in range(4):
            B.plan(("attn_acc", b), b, ("attn_out", 1))
        B.plan(("ms", 1), 4)
        for c in range(NC_F):
            for hf in range(2):
                B.plan(("g", c, hf), 4 + hf, ("ffn_gate", c)), B.plan(("u", c, hf), 6 + hf, ("ffn_up", c))
        for b in range(4):
            B.plan(("ffn_acc", b), b, ("ffn_down", NC_F - 1))
        B.plan(("ms", 2), 4), B.plan("dt", 5), B.plan("acs", 6)
        for i in range(12):
            B.plan(("conv", i), 4 + i % 4, CONV_TILES[i // 2])
        for g in range(GROUPS):
            B.plan(("xn", g, 0), 1), B.plan(("cb", g), 0), B.plan(("xn", g, 1), 2)
            B.plan(("z", g, 0), 0, ("ssd_z", g)), B.plan(("z", g, 1), 3, ("ssd_z", g))
            B.plan(("state", g), 1)
            for half in range(2):
                for c in range(TT):
                    B.plan(("ab", g, half, c), 4 + 2 * half + c)
            for half in range(2):
                B.plan(("y", g, half), 1 + half)
        for g in range(GROUPS):
            B.plan(("y_ms", g), 4 + g)
        for b in range(4):
            B.plan(("ssd_acc", b), b, ("ssd_out", 3))
        B.plan(("ms", 3), 4)
        for i in range(4):
            B.plan(("xnat", i), i)
        for i in range(4):
            B.plan(("hnat", i), 4 + i)
        B.plan("logits", 0), B.plan("rank", 1)
        dense_uses = list(B.count)

        SCATTER_BANK = [7, 6, 4, 5]

        J = Banks(full, free, None)
        for i in range(4):
            J.plan(("sc", i), SCATTER_BANK[i])
        for c in range(NC_F):
            J.plan(("g", c), c % 2), J.plan(("hidT", c), 6)
        J.plan(("gather", 0), 1), J.plan(("gather", 1), 3)
        J.plan("PT", 7)
        USES = list(J.count)
        BASE = list(dense_uses)
        FULL_BASE = list(B.fulls)
        for b in (1, 3):
            BASE[b] += 1
            FULL_BASE[b] += 1
        WQ = 4 * ND
        EXPERT_BUFFER = [SPLITS] + [(WQ - SPLITS + i) % SPLITS for i in range(SPLITS)]

        def tile_finished(eng, tile, job):
            eng.wait_ge(w_used, job * 4 * NE + (WQ + 4 * EXPERT[tile] + 4))

        def job_ready(eng, name, job):
            b = J.at[name][0]
            alone = [n for n, (bb, *_) in J.at.items() if bb == b and n[0] != "g"]
            eng.wait_ge(full[b], job * len(alone) + (FULL_BASE[b] + alone.index(name) + 1))

        def job_claim(eng, name, job):
            b, k = J.at[name][:2]
            eng.wait_ge(free[b], job * USES[b] + (BASE[b] + k))

        def job_released(eng, name, job):
            b, k = J.at[name][:2]
            eng.wait_ge(free[b], job * USES[b] + (BASE[b] + k + 1))

        def gather_ready(eng, half, job):
            b = 1 + 2 * half
            assert USES[3] == 1 and FULL_BASE[b]
            eng.wait_ge(full[b], job + FULL_BASE[b])

        def job_gathered(eng, job):
            for b in (1, 3):
                eng.wait_ge(free[b], job * USES[b] + BASE[b])

        landed = [sem(f"landed{s}") for s in range(RING)]
        h_hi, h_lo = sem("h_hi"), sem("h_lo")
        in_hi, in_lo = sem("in_hi"), sem("in_lo")
        in_x, in_const, in_rows, in_misc, in_lam = (sem(n) for n in ("in_x", "in_const", "in_rows", "in_misc", "in_lam"))
        in_hankel, in_scratch, in_dt, in_router = sem("in_hankel"), sem("in_scratch"), sem("in_dt"), sem("in_router")
        out_done = sem("out_done")
        dve_step, act_step = sem("dve_step"), sem("act_step")
        relb_set = sem("relb_set")
        sq_ready = sem("sq_ready")
        rstd_ready = sem("rstd_ready")
        h_ready = sem("h_ready")
        qk_sq, qk_rstd = sem("qk_sq"), sem("qk_rstd")
        lam_dot, lam_exp, lam_ready = sem("lam_dot"), sem("lam_exp"), sem("lam_ready")
        logit_ready, p_ready, attn_ready = sem("logit_ready"), sem("p_ready"), sem("attn_ready")
        o_sq, o_rstd, o_ready = sem("o_sq"), sem("o_rstd"), sem("o_ready")
        sp_abs, sp_ln, a_exp, da_ready, w0_arg, w0_ready = (sem(n) for n in (
            "sp_abs", "sp_ln", "a_exp", "da_ready", "w0_arg", "w0_ready"))
        conv_first, conv_out = sem("conv_first"), sem("conv_out")
        xw_ready, arg1_ready, dec_ready, m_ready, ce_ready = (sem(n) for n in (
            "xw_ready", "arg1_ready", "dec_ready", "m_ready", "ce_ready"))
        cbm_ready = sem("cbm_ready")
        z_silu, gated, y_sq, y_rstd, y_ready = (sem(n) for n in ("z_silu", "gated", "y_sq", "y_rstd", "y_ready"))
        top_diff, top_exp, sel_ready, flag_ready = (sem(n) for n in ("top_diff", "top_exp", "sel_ready", "flag_ready"))
        place_ready = sem("place_ready")
        hg_hi = sem("hg_hi")
        hid_hi = sem("hid_hi")
        hid_ready = sem("hid_ready")
        y_ready_e = sem("y_ready_e")
        no_result = sem("no_result")
        moe_done = sem("moe_done")

        def cols(w, c0):
            return w[:, c0:c0 + 512].rearrange("(k p) n -> p k n", p=P)

        def rws(w, t):
            return w[512 * t:512 * (t + 1), :].rearrange("(k p) n -> p k n", p=P)

        W_IN = ssd_w_in[0]
        SOURCE = {
            "attn_q": lambda t: cols(attn_w_in[0], 512 * t), "attn_k": lambda t: cols(attn_w_in[0], D + 512 * t),
            "attn_v": lambda t: cols(attn_w_in[0], 2 * D + 512 * t), "attn_out": lambda t: rws(attn_w_out[0], t),
            "ffn_gate": lambda t: cols(ffn_w_gate[0], 512 * t), "ffn_up": lambda t: cols(ffn_w_up[0], 512 * t),
            "ffn_down": lambda t: rws(ffn_w_down[0], t),
            "ssd_z": lambda t: cols(W_IN, 512 * t), "ssd_x": lambda t: cols(W_IN, DI + 512 * t),
            "ssd_b": lambda t: cols(W_IN, 2 * DI), "ssd_c": lambda t: cols(W_IN, 2 * DI + 512),
            "ssd_out": lambda t: rws(ssd_w_out[0], t),
        }

        def view(kind, s):
            by_rows = kind.endswith("out") or kind.endswith("down")
            return slot_mem(s).rearrange("p (k n) -> p k n", k=4 if by_rows else KD)

        def expert_source(kind, c, e):
            if kind == "down":
                w = moe_w_down.rearrange("o e (c k p) n -> (o e) c p k n", k=4, p=P)
                return w[bass.ds(e, 1), c].rearrange("a p k n -> (a p) k n")
            w = (moe_w_gate if kind == "gate" else moe_w_up).rearrange("o e (k p) n -> (o e) p k n", p=P)
            return w[bass.ds(e, 1), :, :, 512 * c:512 * (c + 1)].rearrange("a p k n -> (a p) k n")

        block = ctx.enter_context(nc.Block())

        def row_input(tile):
            kind, t = tile
            if kind == "attn_out":
                return in2[t], t
            if kind == "ffn_down":
                return in2[0 if t < NC_F - 1 else 1], 2 + t
            return in2[t % 3], 2 + NC_F + t

        @block.sync
        def _(sp):
            sp.dma_start(xin[:, :, :], x[0].rearrange("(a p) n -> p a n", p=P)).then_inc(in_x, 16)
            for n, (kind, t) in enumerate(DT):
                slot = DENSE_SLOT[n % DENSE_RING]
                if n == 1:
                    sp.wait_ge(in_lam, 16)
                if n >= DENSE_RING:
                    sp.wait_ge(w_lo, 4 * (n - DENSE_RING + 1))
                sp.dma_start(view(kind, slot), SOURCE[kind](t)).then_inc(landed[slot], 16)

            def job_tiles(e, job, first):
                for m, (kind, c) in enumerate(ET):
                    slot = EXPERT_SLOT[m % RING]
                    if not first or m >= RING:
                        sp.wait_ge(w_lo, job * 4 * NE + (WQ + 4 * (m - RING + 1)))
                    elif slot == 3:
                        B.ready(sp, ("y_ms", GROUPS - 1))
                    elif slot < 3:
                        sp.wait_ge(y_ready, GROUPS)
                    else:
                        sp.wait_ge(w_lo, 4 * (max(n for n in range(ND) if DENSE_SLOT[n % DENSE_RING] == slot) + 1))
                    sp.dma_start(view(kind, slot), expert_source(kind, c, e)).then_inc(landed[slot], 16)

            job_tiles(0, 0, True)
            with sp.Fori(1, E) as e:
                job_tiles(e, e, False)
            sp.wait_ge(flag_ready, 1)
            more = sp.value_load(flag[0:1, 0:1], min_val=0, max_val=1)
            with sp.If(more > 0):
                with sp.Fori(1, PASSES) as p:
                    with sp.Fori(0, E) as e:
                        job_tiles(e, p * E + e, False)
            sp.wait_ge(moe_done, 1)
            sp.dma_start(out[0].rearrange("(a p) n -> p a n", p=P), xnat[:, :, :]).then_inc(out_done, 16)
            sp.wait_ge(out_done, 16)

        @block.gpsimd
        def _(pool):
            B.released(pool, "ubias")
            pool.dma_start(scratch[:, 0:NDIST], ubias[:, :]).then_inc(in_scratch, 16)
            pool.wait_ge(in_scratch, 16)
            pool.dma_start(hankel[:, :, :],
                           bass.AP(scratch.tensor, 0, [[1, P], [512, HEADS], [1, T]])).then_inc(in_hankel, 16)

            B.released(pool, ("attn_acc", 3))
            pool.dma_start(wdt[:, :, :], W_IN[:, 2 * DI + 2 * GROUPS * NSTATE:]
                           .rearrange("(k p) n -> p k n", p=P)).then_inc(in_dt, 16)
            pool.dma_start(alog[:, 0, :], ssd_a_log[0:1, :].broadcast_to([P, SH])).then_inc(in_dt, 16)
            pool.dma_start(alog[:, 1, :], ssd_dt_bias[0:1, :].broadcast_to([P, SH])).then_inc(in_dt, 16)
            pool.dma_start(router[:, :, :], moe_router[0].rearrange("(k p) n -> p k n", p=P)).then_inc(in_router, 16)
            pool.wait_ge(w0_ready, 1)
            for g in range(GROUPS):
                B.released(pool, ("xn", g, 0))
                if g >= 2:
                    B.ready(pool, ("state", g - 2))
                nc.gpsimd.tensor_tensor(xw[:, g % 2, :].rearrange("p (h d) -> p h d", d=HD),
                                        xd[:, g % 2, 0:512].rearrange("p (h d) -> p h d", d=HD),
                                        w0[:, g * HPG:(g + 1) * HPG].unsqueeze(2).broadcast_to([P, HPG, HD]),
                                        ALU.mult).then_inc(xw_ready, 1)
                for half in range(2):
                    B.released(pool, ("ab", g, half, 1))
                    nc.gpsimd.tensor_tensor(eC[:, half, :].rearrange("p (h l) -> p h l", l=P),
                                            eC[:, half, :].rearrange("p (h l) -> p h l", l=P),
                                            CT[:, g, P:T].unsqueeze(1).broadcast_to([P, 4, P]),
                                            ALU.mult).then_inc(ce_ready, 1)

        @block.tensor
        def _(pe):
            def mm(o, lhsT, rhs, start, stop, shared=False):
                return nc.tensor.matmul(o, lhsT, rhs, start=start, stop=stop, skip_group_check=shared)

            def parts(tile, q, k):
                n = 4 * DENSE[tile] + q
                pe.wait_ge(w_lo, n + 1)
                wd = 1024 if tile[0].endswith("out") or tile[0].endswith("down") else 512
                return [wsplit[:, n % SPLITS, part, k * wd:(k + 1) * wd] for part in range(2)]

            def three(o, w, a, start, stop, shared=True):
                (w_h, w_l), (a_h, a_l) = w, a
                mm(o, w_h, a_h, start, False, shared)
                mm(o, w_h, a_l, False, False, shared)
                return mm(o, w_l, a_h, False, stop, shared)

            pe.wait_ge(in_const, 16)
            pe.wait_ge(in_x, 16)
            for i in range(4):
                B.claim(pe, ("x", i))
                for j in range(2):
                    for tt in range(TT):
                        last = nc.tensor.transpose(bank[4 + i][:, j * T + tt * P:j * T + (tt + 1) * P],
                                                   xin[:, tt, (2 * i + j) * P:(2 * i + j + 1) * P], C("ident"))
                B.finish(last, ("x", i))

            def mean_square(n):
                B.claim(pe, ("ms", n))
                for k in range(KD):
                    if k % 2 == 0:
                        pe.wait_ge(sq_ready, 4 * n + k // 2 + 1)
                    last = mm(bank[4][:, 0:T], C("mean_d"), hT[:, k, :], k == 0, k == KD - 1)
                B.finish(last, ("ms", n))

            def project(tile, banks, q, fresh=None):
                if fresh is not None:
                    pe.wait_ge(h_lo, 4 * fresh + q + 1)
                for j in range(2):
                    w = parts(tile, q, j)
                    k = 2 * q + j
                    for m in range(4):
                        last = three(bank[banks[m // 2]][:, (m % 2) * T:(m % 2 + 1) * T],
                                     [p[:, m * P:(m + 1) * P] for p in w], [h2[:, part, k, :] for part in range(2)],
                                     k == 0 and m % 2 == 0, k == KD - 1 and m % 2 == 1)
                last.then_inc(w_used, 1)

            def down(acc, tile, first, last_tile):
                act, n = row_input(tile)
                pe.wait_ge(in_lo, n + 1)
                for q in range(4):
                    w = parts(tile, q, 0)
                    for m in range(KD):
                        b = m // 2
                        if first and q == 0 and m % 2 == 0:
                            B.claim(pe, (acc, b))
                        last = three(bank[b][:, (m % 2) * T:(m % 2 + 1) * T], [p[:, m * P:(m + 1) * P] for p in w],
                                     [act[:, part, q, :] for part in range(2)],
                                     first and q == 0 and m % 2 == 0, last_tile and q == 3 and m % 2 == 1)
                    last.then_inc(w_used, 1)

            mean_square(0)
            pe.wait_ge(in_rows, 16 * N_ROWS)
            B.finish(nc.tensor.transpose(bank[1][:, 0:ROWS_B], rows[0:ROWS_B, 1, :], cst[0:ROWS_B, 0:ROWS_B]), "rowsB")
            B.finish(nc.tensor.transpose(bank[0][:, 0:96], rows[0:96, 0, :], cst[0:96, 0:96]), "rowsA")
            pe.wait_ge(in_misc, 16 * N_MISC)
            pe.wait_ge(relb_set, 2)
            B.finish(mm(bank[2][:, 0:16], C("odd_even", SH), small[0:SH, 0:16], True, True), "dcol")
            B.finish(mm(bank[3][0:HEADS, 0:NDIST], relb[:, :], onehot[:, :], True, True), "ubias")
            for t in range(6):
                tile = DT[t]
                for q in range(4):
                    if q == 0:
                        for i in (2 * t, 2 * t + 1):
                            B.claim(pe, ("qk", i) if t < 4 else ("v", i - 8))
                    if t < 4:
                        project(tile, ((2 * t) % 4, (2 * t + 1) % 4), q, 0 if t == 0 else None)
                    else:
                        for j in range(2):
                            w = parts(tile, q, j)
                            k = 2 * q + j
                            for tt in range(TT):
                                a_h, a_l = (h2[:, part, k, tt * P:(tt + 1) * P] for part in range(2))
                                o = bank[6 + tt][:, :]
                                mm(o, a_h, w[0], k == 0, False)
                                mm(o, a_l, w[0], False, False)
                                last = mm(o, a_h, w[1], False, k == KD - 1)
                        last.then_inc(w_used, 1)
                    if q == 1 and 1 <= t <= 4:
                        for hf in range(2):
                            i = 2 * t - 2 + hf
                            B.claim(pe, ("qk_ms", i))
                            pe.wait_ge(qk_sq, i + 1)
                            B.finish(mm(bank[4 + hf][:, :], C("mean_hd"), sqb[:, hf, :], True, True), ("qk_ms", i))
            pe.wait_ge(in_hankel, 16)
            for i in range(4):
                B.claim(pe, ("bias", i))
                last = mm(bank[i][:, :], C("anti"), hankel[:, 2 * i:2 * i + 2, :], True, True)
                B.finish(last, ("bias", i))
            for i in range(8):
                B.released(pe, ("qk", i))
            for i in range(4):
                B.released(pe, ("v", i))
            for i in range(HEADS + 4):
                if i < HEADS:
                    for m in range(2):
                        B.claim(pe, ("s", i, m))
                        b = bank[2 * m + i % 2]
                        q, k = qT[HD * m:HD * (m + 1), i, :], kT[HD * m:HD * (m + 1), i, :]
                        mm(b[:, 0:P], q[:, 0:P], k[:, 0:P], True, True)
                        B.finish(mm(b[:, P:P + T], q[:, P:T], k[:, :], True, True), ("s", i, m))
                h = i - 2
                if 0 <= h < HEADS:
                    B.claim(pe, ("at", h))
                    pe.wait_ge(attn_ready, h + 1)
                    for j in range(3):
                        last = nc.tensor.transpose(bank[4][:, j * P:(j + 1) * P], A[:, h % 2, j * P:(j + 1) * P],
                                                   C("ident"))
                    B.finish(last, ("at", h))
                h = i - 3
                if 0 <= h < HEADS:
                    B.claim(pe, ("o", h))
                    B.released(pe, ("at", h))
                    b = bank[5 + h % 2]
                    mm(b[:, 0:T], V[:, 0, h * P:(h + 1) * P], AT[:, h % 2, 0:T], True, False)
                    B.finish(mm(b[:, P:T], V[:, 1, h * P:(h + 1) * P], AT[:, h % 2, T:T + P], False, True), ("o", h))
                if i in PAIR_AT:
                    b = PAIR_AT[i]
                    B.claim(pe, ("o_ms", b))
                    pe.wait_ge(o_sq, 2 * b + 2)
                    B.finish(mm(bank[7][:, :], C("mean_v"), hT[:, 2 * b:2 * b + 2, :], True, True), ("o_ms", b))
            for t in range(2):
                down("attn_acc", ("attn_out", t), t == 0, t == 1)

            mean_square(1)
            for tile in DT[DENSE[("ffn_gate", 0)]:DENSE[("ffn_down", NC_F - 1)] + 1]:
                kind, c = tile
                if kind == "ffn_down":
                    down("ffn_acc", tile, c == 0, c == NC_F - 1)
                else:
                    b0 = 4 if kind == "ffn_gate" else 6
                    for hf in range(2):
                        B.claim(pe, (kind[4], c, hf))
                    for q in range(4):
                        project(tile, (b0, b0 + 1), q, 1 if c == 0 and kind == "ffn_gate" else None)

            mean_square(2)
            pe.wait_ge(in_dt, 48)
            B.claim(pe, "dt")
            for k in range(KD):
                pe.wait_ge(h_ready, KD * 2 + k + 1)
            for tt in range(TT):
                for k in range(KD):
                    last = mm(bank[5][:, tt * SH:(tt + 1) * SH], hT[:, k, tt * P:(tt + 1) * P], wdt[:, k, :],
                              k == 0, k == KD - 1)
            B.finish(last, "dt")
            def group_inputs(g):
                pe.wait_ge(conv_out, 4 + 2 * g + 2)
                for c in range(TT):
                    B.claim(pe, ("xn", g, c))
                    for b in range(4):
                        last = nc.tensor.transpose(bank[1 + c][:, b * P:(b + 1) * P],
                                                   xsT[:, 4 * g + b, c * P:(c + 1) * P], C("ident"))
                    B.finish(last, ("xn", g, c))
                    if c == 0:
                        B.claim(pe, ("cb", g))
                        for cc in range(TT):
                            mm(bank[0][:, cc * P:(cc + 1) * P], BT[:, g, cc * P:(cc + 1) * P],
                               CT[:, g, cc * P:(cc + 1) * P], True, True)
                        B.finish(nc.tensor.transpose(bank[0][:, T:T + P], BT[:, g, 0:P], C("ident")), ("cb", g))

            for t, tile in enumerate(CONV_TILES):
                if tile == CONV_TILES[-1]:
                    group_inputs(0)
                banks = (4 + (2 * t) % 4, 5 + (2 * t) % 4)
                for hf in range(2):
                    B.claim(pe, ("conv", 2 * t + hf))
                for q in range(4):
                    project(tile, banks, q, 2 if t == 0 else None)
                if t == 0:
                    B.claim(pe, "acs")
                    pe.wait_ge(da_ready, 1)
                    for c in range(TT):
                        mm(bank[6][:, c * SH:(c + 1) * SH], C("upto"), da[:, c, :], True, True)
                    B.finish(mm(bank[6][:, 64:64 + SH], C("ones"), da[:, 0, :], True, True), "acs")

            for g in range(GROUPS):
                if g:
                    group_inputs(g)
                for hf in range(2):
                    B.claim(pe, ("z", g, hf))
                for q in range(2):
                    project(("ssd_z", g), (0, 3), q)
                B.claim(pe, ("state", g))
                pe.wait_ge(xw_ready, g + 1)
                B.finish(mm(bank[1][:, :], Bn[:, g % 2, :], xw[:, g % 2, :], True, True), ("state", g))
                for half in range(2):
                    for c in range(TT):
                        B.claim(pe, ("ab", g, half, c))
                        for q in range(4):
                            h = g * HPG + 4 * half + q
                            last = mm(bank[4 + 2 * half + c][:, q * P:(q + 1) * P],
                                      da[:, c, h:h + 1].broadcast_to([P, P]), C("upto"), True, True)
                        B.finish(last, ("ab", g, half, c))
                for q in range(2, 4):
                    project(("ssd_z", g), (0, 3), q)
                B.released(pe, ("xn", g, 1))
                B.released(pe, ("state", g))
                for half in range(2):
                    B.claim(pe, ("y", g, half))
                    pe.wait_ge(m_ready, 4 * g + 2 * half + 2)
                    pe.wait_ge(ce_ready, 2 * g + half + 1)
                    for q in range(4):
                        o = bank[1 + half][HD * (q % 2):HD * (q % 2 + 1), (q // 2) * T:(q // 2 + 1) * T]
                        ch = (4 * half + q) * HD
                        mm(o[:, 0:P], xd[:, g % 2, ch:ch + HD], dec[:, 2 * half, q * P:(q + 1) * P], True, True)
                        mm(o[:, P:T], xd[:, g % 2, 512 + ch:512 + ch + HD], dec[:, 2 * half + 1, q * P:(q + 1) * P],
                           True, False)
                        last = mm(o[:, P:T], stS[:, g % 2, ch:ch + HD], eC[:, half, q * P:(q + 1) * P], False, True)
                    B.finish(last, ("y", g, half))
            for g in range(GROUPS):
                B.claim(pe, ("y_ms", g))
                pe.wait_ge(y_sq, g + 1)
                for b in range(4):
                    last = mm(bank[4 + g][:, 0:T], C("mean_g"), zr[:, 4 * g + b, :], b == 0, b == 3)
                B.finish(last, ("y_ms", g))
            for g in range(GROUPS):
                down("ssd_acc", ("ssd_out", g), g == 0, g == 3)

            mean_square(3)
            for i in range(4):
                tt, half = i // 2, i % 2
                B.claim(pe, ("xnat", i))
                for b in range(4):
                    last = nc.tensor.transpose(bank[i][:, b * P:(b + 1) * P], xT[:, 4 * half + b, tt * P:(tt + 1) * P],
                                               C("ident"))
                B.finish(last, ("xnat", i))
            pe.wait_ge(in_router, 16)
            B.claim(pe, "logits")
            for k in range(KD):
                pe.wait_ge(h_ready, KD * 3 + k + 1)
                for tt in range(TT):
                    last = mm(bank[0][:, tt * E:(tt + 1) * E], hT[:, k, tt * P:(tt + 1) * P], router[:, k, :],
                              k == 0 and tt == 0, k == KD - 1 and tt == TT - 1, True)
            B.finish(last, "logits")
            for i in range(4):
                tt, half = i // 2, i % 2
                B.claim(pe, ("hnat", i))
                for b in range(4):
                    last = nc.tensor.transpose(bank[4 + i][:, b * P:(b + 1) * P],
                                               hT[:, 4 * half + b, tt * P:(tt + 1) * P], C("ident"))
                B.finish(last, ("hnat", i))
            B.claim(pe, "rank")
            pe.wait_ge(sel_ready, 1)
            sel = oh[:, 2, :]
            mm(bank[1][:, 0:E], C("before"), sel[:, 0:E], True, True)
            mm(bank[1][:, E:2 * E], C("ones"), sel[:, 0:E], True, False)
            mm(bank[1][:, E:2 * E], C("before"), sel[:, E:2 * E], False, True)
            mm(bank[1][:, 2 * E:3 * E], C("ones"), sel[:, 0:E], True, False)
            B.finish(mm(bank[1][:, 2 * E:3 * E], C("ones"), sel[:, E:2 * E], False, True), "rank")

            def gather(job):
                pe.wait_ge(place_ready, job + 1)
                for half in range(2):
                    b = 1 + 2 * half
                    for q in range(4):
                        d = 4 * half + q
                        for tt in range(TT):
                            last = mm(bank[b][:, q * SLOTS:(q + 1) * SLOTS], hnat[:, tt, d * P:(d + 1) * P],
                                      Pm[:, tt, :], tt == 0, tt == 1)
                    last.then_inc(full[b], 1)

            for i in range(4):
                B.released(pe, ("hnat", i))
            gather(0)
            pe.wait_ge(no_result, 1)

            def scatter(job):
                pe.wait_ge(y_ready_e, job * 2 + 2)
                for i in range(4):
                    tt, half = i // 2, i % 2
                    job_claim(pe, ("sc", i), job)
                    mm(bank[SCATTER_BANK[i]][:, :], PT[0:SLOTS, tt, :], ynat[0:SLOTS, half * 512:(half + 1) * 512],
                       True, True).then_inc(full[SCATTER_BANK[i]], 1)

            def job_body(job):
                def split_products(tile, act, o, first, last_one):
                    m = EXPERT[tile]
                    for q in range(4):
                        pe.wait_ge(w_lo, job * 4 * NE + (WQ + 4 * m + q + 1))
                        buf = EXPERT_BUFFER[q % EXPERT_SPLITS]
                        for j in range(2):
                            w_h, w_l = (wsplit[:, buf, part, j * 512:(j + 1) * 512] for part in range(2))
                            mm(o(j), act(q, j, 0), w_h, first(q, j), False)
                            mm(o(j), act(q, j, 1), w_h, False, False)
                            last = mm(o(j), act(q, j, 0), w_l, False, last_one(q, j))
                        last.then_inc(w_used, 1)

                def projected(kind, c, b):
                    if kind == "gate":
                        job_claim(pe, ("g", c), job)
                    split_products((kind, c), lambda q, j, part: hTg[:, part, 2 * q + j, :],
                                   lambda j: bank[b][0:SLOTS, :],
                                   lambda q, j: q == 0 and j == 0, lambda q, j: q == 3 and j == 1)

                def down_chunk(c):
                    if c == 0:
                        for i in (2, 3):
                            job_released(pe, ("sc", i), job)
                    job_released(pe, ("hidT", c), job)
                    split_products(("down", c), lambda q, j, part: ehidT[:, c % 2, part, q, :],
                                   lambda j: bank[4 + j][0:SLOTS, :],
                                   lambda q, j: c == 0 and q == 0, lambda q, j: c == NC_F - 1 and q == 3)

                def turn_hidden(c):
                    job_claim(pe, ("hidT", c), job)
                    pe.wait_ge(hid_ready, job * NC_F + (c + 1))
                    for j in range(4):
                        last = nc.tensor.transpose(bank[6][:, j * SLOTS:(j + 1) * SLOTS], ehid[0:SLOTS, j * P:(j + 1) * P],
                                                   cst[0:SLOTS, 0:SLOTS])
                    last.then_inc(full[6], 1)

                job_gathered(pe, job)
                for c in range(NC_F):
                    projected("gate", c, c % 2)
                    if c:
                        turn_hidden(c - 1)
                    else:
                        scatter(job)
                    projected("up", c, 2 + c % 2)
                    if c == 1:
                        job_claim(pe, "PT", job)
                        for tt in range(TT):
                            last = nc.tensor.transpose(bank[7][0:SLOTS, tt * P:(tt + 1) * P], Pm[:, tt, :], C("ident"))
                        last.then_inc(full[7], 1)
                    if c:
                        down_chunk(c - 1)
                turn_hidden(NC_F - 1)
                job_claim(pe, ("gather", 0), job)
                job_claim(pe, ("gather", 1), job)
                gather(job + 1)
                down_chunk(NC_F - 1)
            with pe.Fori(0, E) as job:
                job_body(job)
            pe.wait_ge(flag_ready, 1)
            more = pe.value_load(flag[0:1, 0:1], min_val=0, max_val=1)
            with pe.If(more > 0):
                with pe.Fori(E, JOBS) as job:
                    job_body(job)
            scatter(more * (JOBS - E) + E)

        @block.scalar
        def _(act):
            chain = Chain(act, act_step)
            fn = nc.scalar.activation

            act.dma_start(cst[:, :], const).then_inc(in_const, 16)
            for src, part, r0, c0 in (
                    (ssd_conv_w[0].rearrange("j (b p) -> (j b) p", p=P), 0, 0, 0),
                    (norm_mix.rearrange("i (b p) -> (i b) p", p=P), 1, NORM_MIX, 0),
                    (norm_ffn.rearrange("i (b p) -> (i b) p", p=P), 1, NORM_FFN, 0),
                    (ssd_conv_b[0].rearrange("(b p) -> b p", p=P), 1, CONV_B, 0),
                    (ssd_norm[0].rearrange("(b p) -> b p", p=P), 1, SSD_NORM, 0),
                    (attn_subln, 1, SUBLN, 0),
                    (attn_q_gain, 1, Q_GAIN, 0), (attn_q_gain, 1, Q_GAIN, HD),
                    (attn_k_gain, 1, K_GAIN, 0), (attn_k_gain, 1, K_GAIN, HD)):
                n, wd = src.shape
                act.dma_start(rows[r0:r0 + n, part, c0:c0 + wd], src).then_inc(in_rows, 16)
            act.dma_start(small[0:SH, 16:17], ssd_d[0].rearrange("(n a) -> n a", a=1)).then_inc(in_misc, 16)
            act.dma_start(relb[0:BUCKETS, :], rel_bias).then_inc(in_misc, 16)
            act.dma_start(onehot[:, :], hot).then_inc(in_misc, 16)
            act.dma_start(lam_in, attn_lambda.rearrange("o a d -> o (a d)").broadcast_to([P, 4 * HD])).then_inc(in_lam, 16)

            def logs_and_exps():
                nc.scalar.preload_act_table_set("natural_log_exp_and_others")

            logs_and_exps()

            def norm(n):
                for b in range(4):
                    B.released(act, ((("x", "attn_acc", "ffn_acc", "ssd_acc")[n]), b))
                    fn(hT[:, 2 * b:2 * b + 2, :], xT[:, 2 * b:2 * b + 2, :], ACT.Square).then_inc(sq_ready, 1)
                B.ready(act, ("ms", n))
                B.release(fn(rstd[:, :], bank[4][:, 0:T], ACT.Ln, bias=C("eps")), ("ms", n))
                B.released(act, ("ms", n))
                fn(rstd[:, :], rstd[:, :], ACT.Exp, scale=-0.5).then_inc(rstd_ready, 1)

            def norm_hi(n):
                for b in range(4):
                    act.wait_ge(h_ready, KD * n + 2 * b + 2)
                    nc.scalar.copy(h2[:, 0, 2 * b:2 * b + 2, :], hT[:, 2 * b:2 * b + 2, :]).then_inc(h_hi, 1)

            def split(n, q):
                if n == ND:
                    return
                slot = DENSE_SLOT[n % DENSE_RING]
                if q == 0:
                    act.wait_ge(landed[slot], 16 * (n // DENSE_RING + 1))
                i = 4 * n + q
                if i >= SPLITS:
                    act.wait_ge(w_used, i - SPLITS + 1)
                w = view(DT[n][0], slot)
                nc.scalar.copy(wsplit[:, i % SPLITS, 0, :].rearrange("p (k n) -> p k n", n=w.shape[2]),
                               quarter(w, q)).then_inc(w_hi, 1)

            def input_hi(tile, src):
                nc.scalar.copy(row_input(tile)[0][:, 0], src).then_inc(in_hi, 1)

            def qk_squares(t):
                for hf in range(2):
                    i = 2 * t + hf
                    B.ready(act, ("qk", i))
                    if i >= 2:
                        B.ready(act, ("qk_ms", i - 2))
                    fn(sqb[:, hf, :], bank[i % 4][:, :], ACT.Square).then_inc(qk_sq, 1)

            def qk_rms(t):
                for hf in range(2):
                    i = 2 * t + hf
                    B.ready(act, ("qk_ms", i))
                    if i >= 2:
                        B.released(act, ("qk", i - 2))
                    B.release(fn(rq[:, hf, :], bank[4 + hf][:, :], ACT.Ln, bias=C("eps")), ("qk_ms", i))
                    B.released(act, ("qk_ms", i))
                    fn(rq[:, hf, :], rq[:, hf, :], ACT.Exp, scale=-0.5).then_inc(qk_rstd, 1)

            def copy_v(t):
                for tt in range(TT):
                    B.ready(act, ("v", 2 * t + tt))
                    B.release(nc.scalar.copy(V[:, tt, t * 512:(t + 1) * 512], bank[6 + tt][:, :]), ("v", 2 * t + tt))

            def attention():
                for i in range(4):
                    B.ready(act, ("bias", i))
                    B.release(nc.scalar.copy(bias[:, 2 * i:2 * i + 2, :], bank[i][:, :]), ("bias", i))
                for i in range(HEADS + 4):
                    if i < HEADS:
                        act.wait_ge(logit_ready, i + 1)
                        for m in range(2):
                            for qb in range(2):
                                a, n = m * 384 + qb * P, P + qb * P
                                j = 2 * m + qb
                                last = fn(L[:, i % 2, a:a + n], L[:, i % 2, a:a + n], ACT.Exp,
                                          bias=st[:, i % 2, 4 + j:5 + j], accum_out=st[:, i % 2, 8 + j:9 + j])
                        last.then_inc(p_ready, 1)
                    h = i - 2
                    if 0 <= h < HEADS:
                        B.ready(act, ("at", h))
                        if h >= 2:
                            B.ready(act, ("o", h - 2))
                        B.release(nc.scalar.copy(AT[:, h % 2, :], bank[4][:, 0:384]), ("at", h))
                    h = i - 3
                    if 0 <= h < HEADS:
                        B.ready(act, ("o", h))
                        fn(hT[:, h, :], bank[5 + h % 2][:, 0:T], ACT.Square).then_inc(o_sq, 1)
                    if i in PAIR_AT:
                        b = PAIR_AT[i]
                        B.ready(act, ("o_ms", b))
                        B.release(fn(hT[:, 2 * b:2 * b + 2, :], bank[7][:, :], ACT.Ln, bias=C("eps")), ("o_ms", b))
                        B.released(act, ("o_ms", b))
                        fn(hT[:, 2 * b:2 * b + 2, :], hT[:, 2 * b:2 * b + 2, :], ACT.Exp, scale=-0.5)\
                            .then_inc(o_rstd, 1)
                    if i in (9, HEADS + 3):
                        t = int(i > 9)
                        act.wait_ge(o_ready, 2 * t + 2)
                        input_hi(("attn_out", t), oT[:, 4 * t:4 * t + 4, :])

            def silu_gate(c):
                for hf in range(2):
                    B.ready(act, ("g", c, hf))
                    if c >= 2:
                        B.released(act, ("u", c - 2, hf))
                    B.release(fn(sg[:, 2 * (c % 2) + hf, :], bank[4 + hf][:, :], ACT.Silu), ("g", c, hf))

            def hidden_hi(c):
                for hf in range(2):
                    B.released(act, ("u", c, hf))
                if c:
                    dense_tile_end(act, ("ffn_down", c - 1))
                input_hi(("ffn_down", c), hid[:, c % 2, :, :])

            def conv_first_tap(t):
                for i in (2 * t, 2 * t + 1):
                    B.ready(act, ("conv", i))
                    if i >= 2:
                        act.wait_ge(conv_out, i - 1)
                    for j in range(2):
                        blk = conv_block(i) + j
                        last = fn(cvb[:, i % 2, j * T:(j + 1) * T], bank[4 + i % 4][:, j * T:(j + 1) * T], ACT.Identity,
                                  bias=colB[:, CONV_B + blk:CONV_B + blk + 1], scale=colA[:, 72 + blk:73 + blk])
                    last.then_inc(conv_first, 1)

            def conv_silu(k):
                B.released(act, ("conv", k))
                dest = BT if k < 2 else CT if k < 4 else xsT
                at = 2 * k - (0 if k < 2 else 4 if k < 4 else 8)
                fn(dest[:, at:at + 2, :], cvb[:, k % 2, :], ACT.Silu).then_inc(conv_out, 1)

            def ssd_decays():
                act.wait_ge(in_dt, 48)
                fn(alog[:, 0, :], alog[:, 0, :], ACT.Exp).then_inc(a_exp, 1)
                act.wait_ge(sp_abs, 1)
                chain.link(fn(dta[:, :, :], dta[:, :, :], ACT.Exp, scale=-1.0))
                fn(dta[:, :, :], dta[:, :, :], ACT.Ln, bias=C("one")).then_inc(sp_ln, 1)

            def core(g):
                B.ready(act, ("state", g))
                if g >= 2:
                    B.ready(act, ("y", g - 2, 1))
                B.release(nc.scalar.copy(stS[:, g % 2, :], bank[1][:, :]), ("state", g))
                for half in range(2):
                    for c in range(TT):
                        if c == 0:
                            B.released(act, ("ab", g, half, 0))
                        else:
                            act.wait_ge(arg1_ready, 2 * g + half + 1)
                        fn(dec[:, 2 * half + c, :], dec[:, 2 * half + c, :], ACT.Exp).then_inc(dec_ready, 1)
                    B.ready(act, ("ab", g, half, 1))
                    if g:
                        B.ready(act, ("y", g - 1, half))
                    B.release(fn(eC[:, half, :], bank[4 + 2 * half + 1][:, :], ACT.Exp), ("ab", g, half, 1))

            def copy_z(g):
                for hf in range(2):
                    B.ready(act, ("z", g, hf))
                    at = 4 * g + 2 * hf
                    B.release(nc.scalar.copy(zr[:, at:at + 2, :], bank[3 * hf][:, :]), ("z", g, hf))

            def gate_silu(groups):
                for g in groups:
                    for hf in range(2):
                        B.released(act, ("z", g, hf))
                    fn(zr[:, 4 * g:4 * g + 4, :], zr[:, 4 * g:4 * g + 4, :], ACT.Silu).then_inc(z_silu, 1)

            def gated_squares(groups):
                for g in groups:
                    act.wait_ge(gated, g + 1)
                    fn(zr[:, 4 * g:4 * g + 4, :], xsT[:, 4 * g:4 * g + 4, :], ACT.Square).then_inc(y_sq, 1)

            def y_rms(g):
                B.ready(act, ("y_ms", g))
                if g >= 2:
                    act.wait_ge(y_ready, g - 1)
                B.release(fn(rg[:, g % 2, :], bank[4 + g][:, 0:T], ACT.Ln, bias=C("eps")), ("y_ms", g))
                B.released(act, ("y_ms", g))
                fn(rg[:, g % 2, :], rg[:, g % 2, :], ACT.Exp, scale=-0.5).then_inc(y_rstd, 1)

            def y_hi(g):
                act.wait_ge(y_ready, g + 1)
                if g == 3:
                    dense_tile_end(act, ("ssd_out", 0))
                input_hi(("ssd_out", g), xsT[:, 4 * g:4 * g + 4, :])

            norm(0)
            for name, dest, b, p in (("rowsB", colB[:, 0:ROWS_B], 1, P), ("rowsA", colA[:, :], 0, P),
                                     ("dcol", dcol[:, :], 2, P), ("ubias", ubias[:, :], 3, HEADS)):
                B.ready(act, name)
                B.release(nc.scalar.copy(dest, bank[b][0:p, 0:dest.shape[1]]), name)
            split(0, 0)
            for n, (kind, t) in enumerate(DT):
                before = DT[n - 1]
                split(n, 1)
                if n == 0:
                    norm_hi(0)
                elif n <= 4:
                    qk_squares(n - 1)
                elif before[0] == "attn_v":
                    copy_v(before[1])
                if kind == "attn_out" and t == 0:
                    attention()
                if before == ("attn_out", 1):
                    norm(1)
                    norm_hi(1)
                if before[0] == "ffn_gate":
                    silu_gate(before[1])
                if before == ("ffn_gate", 1):
                    hidden_hi(0)
                if before[0] == "ffn_down" and before[1] < NC_F - 2:
                    hidden_hi(before[1] + 1)
                if before == ("ffn_down", NC_F - 1):
                    logs_and_exps()
                    norm(2)
                    norm_hi(2)
                    ssd_decays()
                if before in CONV_TILES:
                    i = CONV_TILES.index(before)
                    if i:
                        conv_silu(2 * i - 1)
                    else:
                        act.wait_ge(w0_arg, 1)
                        fn(w0, w0, ACT.Exp).then_inc(w0_ready, 1)
                    conv_first_tap(i)
                if before[0] == "ssd_z":
                    copy_z(before[1])
                if before == ("ssd_z", GROUPS - 1):
                    gate_silu([GROUPS - 1])
                    logs_and_exps()
                    y_rms(0)
                    gated_squares([GROUPS - 1])
                    for g in range(1, GROUPS):
                        y_rms(g)
                        y_hi(g - 1)
                if before == ("ssd_out", 0):
                    y_hi(GROUPS - 1)
                split(n, 2)
                split(n, 3)
                split(n + 1, 0)
                if 1 <= n <= 4:
                    qk_rms(n - 1)
                if n == 0:
                    act.wait_ge(lam_dot, 2)
                    fn(small[:, 22:24], small[:, 20:22], ACT.Exp).then_inc(lam_exp, 1)
                if (kind, t) == ("ffn_down", NC_F - 2):
                    hidden_hi(NC_F - 1)
                if before in CONV_TILES:
                    conv_silu(2 * CONV_TILES.index(before))
                if (kind, t) == ("ssd_z", 0):
                    conv_silu(11)
                if kind == "ssd_z":
                    core(t)
                    if t == GROUPS - 1:
                        gate_silu(range(t))
                        gated_squares(range(t))

            norm(3)
            for i in range(4):
                B.ready(act, ("xnat", i))
                B.release(nc.scalar.copy(xnat[:, i // 2, (i % 2) * 512:(i % 2 + 1) * 512], bank[i][:, :]), ("xnat", i))
            for i in range(4):
                B.ready(act, ("hnat", i))
                B.release(nc.scalar.copy(hnat[:, i // 2, (i % 2) * 512:(i % 2 + 1) * 512], bank[4 + i][:, :]), ("hnat", i))
            act.wait_ge(top_diff, 1)
            fn(tw[:, 1, 0:TT], tw[:, 0, 0:TT], ACT.Exp).then_inc(top_exp, 1)

            nc.scalar.preload_act_table(ACT.Silu)

            def gathered(job):
                for half in range(2):
                    gather_ready(act, half, job)
                    nc.scalar.copy(hTg[:, 0, 4 * half:4 * half + 4, :], bank[1 + 2 * half][:, 0:4 * SLOTS])\
                        .then_inc(hg_hi, 1)

            def copy_result(job):
                act.wait_ge(w_used, job * 4 * NE + WQ)
                for half in range(2):
                    nc.scalar.copy(ynat[0:SLOTS, half * 512:(half + 1) * 512], bank[4 + half][0:SLOTS, :])\
                        .then_inc(y_ready_e, 1)

            def job_body(job):
                def split(tile):
                    w = expert_landed(act, tile, job)
                    for q in range(4):
                        if tile == ET[0] and q == 2:
                            gathered(job)
                        n = 4 * EXPERT[tile] + q
                        act.wait_ge(w_used, job * 4 * NE + (WQ + n - EXPERT_SPLITS + 1))
                        nc.scalar.copy(wsplit[:, EXPERT_BUFFER[n % EXPERT_SPLITS], 0, :].rearrange("p (k n) -> p k n", n=w.shape[2]),
                                       quarter(w, q)).then_inc(w_hi, 1)

                def hidden_hi(c):
                    job_ready(act, ("hidT", c), job)
                    nc.scalar.copy(ehidT[:, c % 2, 0, :, :], bank[6][:, 0:4 * SLOTS]).then_inc(hid_hi, 1)

                for tile in ET:
                    kind, c = tile
                    split(tile)
                    if kind == "up":
                        if c:
                            hidden_hi(c - 1)
                        tile_finished(act, ("gate", c), job)
                        fn(esg[0:SLOTS, c % 2, :], bank[c % 2][0:SLOTS, :], ACT.Silu).then_inc(free[c % 2], 1)
                    if tile == ("gate", 0):
                        copy_result(job)
                    if tile == ("gate", 2):
                        job_ready(act, "PT", job)
                        nc.scalar.copy(PT[0:SLOTS, :, :], bank[7][0:SLOTS, 0:T]).then_inc(free[7], 1)
                hidden_hi(NC_F - 1)

            with act.Fori(0, E) as job:
                job_body(job)
            act.wait_ge(flag_ready, 1)
            more = act.value_load(flag[0:1, 0:1], min_val=0, max_val=1)
            with act.If(more > 0):
                with act.Fori(E, JOBS) as job:
                    job_body(job)
            copy_result(more * (JOBS - E) + E)

        @block.vector
        def _(dve):
            chain = Chain(dve, dve_step)
            link = chain.link
            V_ = nc.vector
            tt_, ts_, stt = V_.tensor_tensor, V_.tensor_scalar, V_.scalar_tensor_tensor

            for i in range(4):
                B.ready(dve, ("x", i))
                B.release(V_.tensor_copy(xT[:, 2 * i:2 * i + 2, :], bank[4 + i][:, :]), ("x", i))
            dve.wait_ge(in_const, 16)
            dve.wait_ge(in_misc, 16 * N_MISC)
            V_.memset(relb[BUCKETS:BUCKETS + 1, :], MASKED).then_inc(relb_set, 1)
            ts_(small[0:SH, 0:16], C("pair_of", SH), small[0:SH, 16:17], None, ALU.mult).then_inc(relb_set, 1)
            dve.wait_ge(in_lam, 16)
            for j in range(2):
                V_.tensor_tensor_reduce(lam_in[:, 2 * j * HD:(2 * j + 1) * HD], lam_in[:, 2 * j * HD:(2 * j + 1) * HD],
                                        lam_in[:, (2 * j + 1) * HD:(2 * j + 2) * HD], 1.0, 0.0, ALU.mult, ALU.add,
                                        small[:, 20 + j:21 + j]).then_inc(lam_dot, 1)
            B.released(dve, "rowsB")
            link(ts_(small[:, 25:26], colB[:, Q_GAIN:Q_GAIN + 1], HD ** -0.5, None, ALU.mult))
            link(ts_(small[:, 26:27], colB[:, SUBLN:SUBLN + 1], 1.0 - LAMBDA_INIT, None, ALU.mult))

            def norm(n, lo=None):
                col = (NORM_MIX, NORM_FFN)[n % 2] + KD * (n // 2)
                dve.wait_ge(rstd_ready, n + 1)
                for k in range(KD):
                    stt(out=hT[:, k, :], in0=xT[:, k, :], scalar=colB[:, col + k:col + k + 1], in1=rstd[:, :],
                        op0=ALU.mult, op1=ALU.mult).then_inc(h_ready, 1)
                    if lo and k % 2 and k > 1:
                        lo(k // 2 - 1)
                if lo:
                    lo(KD // 2 - 1)

            def residual(acc):
                for b in range(4):
                    B.ready(dve, (acc, b))
                    B.release(tt_(xT[:, 2 * b:2 * b + 2, :], xT[:, 2 * b:2 * b + 2, :],
                                  bank[b][:, :].rearrange("p (a t) -> p a t", a=2), ALU.add), (acc, b))

            def norm_split(n):
                def lo(b):
                    dve.wait_ge(h_hi, 4 * n + b + 1)
                    tt_(h2[:, 1, 2 * b:2 * b + 2, :], hT[:, 2 * b:2 * b + 2, :],
                        h2[:, 0, 2 * b:2 * b + 2, :].bitcast(F32), ALU.subtract).then_inc(h_lo, 1)

                norm(n, lo)

            def split(n, q):
                if n == ND:
                    return
                slot = DENSE_SLOT[n % DENSE_RING]
                if q == 0:
                    dve.wait_ge(landed[slot], 16 * (n // DENSE_RING + 1))
                i = 4 * n + q
                dve.wait_ge(w_hi, i + 1)
                w = view(DT[n][0], slot)
                hi, lo = (wsplit[:, i % SPLITS, part, :].rearrange("p (k n) -> p k n", n=w.shape[2])
                          for part in range(2))
                tt_(lo, quarter(w, q), hi.bitcast(F32), ALU.subtract).then_inc(w_lo, 1)

            def input_lo(tile, src):
                place, i = row_input(tile)
                dve.wait_ge(in_hi, i + 1)
                tt_(place[:, 1], src, place[:, 0].bitcast(F32), ALU.subtract).then_inc(in_lo, 1)

            def lam():
                dve.wait_ge(lam_exp, 1)
                link(tt_(small[:, 24:25], small[:, 23:24], small[:, 22:23], ALU.subtract))
                ts_(small[:, 24:25], small[:, 24:25], -LAMBDA_INIT, None, ALU.add).then_inc(lam_ready, 1)

            def qk_normalise(t):
                dest, gain = (kT, colB[:, K_GAIN:K_GAIN + 1]) if t % 2 else (qT, small[:, 25:26])
                for hf in range(2):
                    i, h = 2 * t + hf, 4 * (t // 2) + 2 * hf
                    dve.wait_ge(qk_rstd, i + 1)
                    B.ready(dve, ("qk", i))
                    B.release(stt(out=dest[:, h:h + 2, :], in0=bank[i % 4][:, :].rearrange("p (a t) -> p a t", a=2),
                                  scalar=gain, in1=rq[:, hf, :].rearrange("p (a t) -> p a t", a=2),
                                  op0=ALU.mult, op1=ALU.mult), ("qk", i))

            def attention():
                for i in range(4):
                    B.released(dve, ("bias", i))
                for i in range(8):
                    B.released(dve, ("qk", i))
                dve.wait_ge(lam_ready, 1)
                for i in range(HEADS + 5):
                    if i < HEADS:
                        s = st[:, i % 2, :]
                        if i >= 2:
                            dve.wait_ge(attn_ready, i - 1)
                        for m in range(2):
                            B.ready(dve, ("s", i, m))
                            b = bank[2 * m + i % 2]
                            for qb in range(2):
                                a, n = qb * P, P + qb * P
                                j = 2 * m + qb
                                last = V_.tensor_tensor_reduce(L[:, i % 2, m * 384 + a:m * 384 + a + n], b[:, a:a + n],
                                                               bias[:, i, T - n:T], 1.0, -3e38, ALU.add, ALU.max,
                                                               s[:, j:j + 1])
                            B.release(last, ("s", i, m))
                        for m in range(2):
                            B.released(dve, ("s", i, m))
                        ts_(s[:, 4:8], s[:, 0:4], -1.0, None, ALU.mult).then_inc(logit_ready, 1)
                    h = i - 4
                    if 0 <= h < HEADS:
                        dve.wait_ge(o_sq, h + 1)
                        B.ready(dve, ("o", h))
                        B.release(V_.tensor_copy(oT[:, h, :], bank[5 + h % 2][:, 0:T]), ("o", h))
                    h = i - 1
                    if 0 <= h < HEADS:
                        s = st[:, h % 2, :]
                        dve.wait_ge(p_ready, h + 1)
                        if h >= 2:
                            B.ready(dve, ("at", h - 2))
                        link(V_.reciprocal(s[:, 8:12], s[:, 8:12]))
                        link(ts_(s[:, 12:14], s[:, 10:12], small[:, 24:25], None, ALU.mult))
                        for qb in range(2):
                            a, n = qb * P, P + qb * P
                            last = ts_(A[:, h % 2, a:a + n], L[:, h % 2, a:a + n], s[:, 8 + qb:9 + qb], None, ALU.mult)
                        link(last)
                        for qb in range(2):
                            a, n = qb * P, P + qb * P
                            last = stt(out=A[:, h % 2, a:a + n], in0=L[:, h % 2, 384 + a:384 + a + n],
                                       scalar=s[:, 12 + qb:13 + qb], in1=A[:, h % 2, a:a + n], op0=ALU.mult,
                                       op1=ALU.add)
                        last.then_inc(attn_ready, 1)
                    if i - 1 in PAIR_AT:
                        b = PAIR_AT[i - 1]
                        for h in (2 * b, 2 * b + 1):
                            B.released(dve, ("o", h))
                        dve.wait_ge(o_rstd, b + 1)
                        stt(out=oT[:, 2 * b:2 * b + 2, :], in0=oT[:, 2 * b:2 * b + 2, :], scalar=small[:, 26:27],
                            in1=hT[:, 2 * b:2 * b + 2, :], op0=ALU.mult, op1=ALU.mult).then_inc(o_ready, 1)
                    if i in (10, HEADS + 4):
                        t = int(i > 10)
                        input_lo(("attn_out", t), oT[:, 4 * t:4 * t + 4, :])

            def hidden(c):
                for hf in range(2):
                    B.released(dve, ("g", c, hf))
                    B.ready(dve, ("u", c, hf))
                    if c >= 2:
                        dve.wait_ge(in_lo, 2 + c - 1)
                    B.release(tt_(hid[:, c % 2, 2 * hf:2 * hf + 2, :],
                                  sg[:, 2 * (c % 2) + hf, :].rearrange("p (a t) -> p a t", a=2),
                                  bank[6 + hf][:, :].rearrange("p (a t) -> p a t", a=2), ALU.mult), ("u", c, hf))

            def hidden_lo(c):
                input_lo(("ffn_down", c), hid[:, c % 2, :, :])

            def step_sizes():
                dve.wait_ge(in_dt, 48)
                B.ready(dve, "dt")
                B.release(tt_(dtv[:, :, :], bank[5][:, 0:TT * SH].rearrange("p (c h) -> p c h", c=TT),
                              alog[:, 1, :].unsqueeze(1).broadcast_to([P, TT, SH]), ALU.add), "dt")
                B.released(dve, "dt")
                stt(out=dta[:, :, :], in0=dtv[:, :, :], scalar=-1.0, in1=dtv[:, :, :], op0=ALU.mult,
                    op1=ALU.max).then_inc(sp_abs, 1)
                dve.wait_ge(sp_ln, 1)
                link(stt(out=dtv[:, :, :], in0=dtv[:, :, :], scalar=0.0, in1=dta[:, :, :], op0=ALU.max, op1=ALU.add))
                dve.wait_ge(a_exp, 1)
                stt(out=da[:, :, :], in0=dtv[:, :, :], scalar=-1.0,
                    in1=alog[:, 0, :].unsqueeze(1).broadcast_to([P, TT, SH]), op0=ALU.mult,
                    op1=ALU.mult).then_inc(da_ready, 1)

            def decay_sums():
                B.ready(dve, "acs")
                link(V_.tensor_copy(acs[:, :, :], bank[6][:, 0:TT * SH].rearrange("p (c h) -> p c h", c=TT)))
                link(tt_(w0, bank[6][:, 64:64 + SH], acs[:, 0, :], ALU.subtract))
                B.release(V_.tensor_copy(small[:, 30:31], small[:, 24:25]), "acs")
                V_.tensor_copy(small[:, 31:32], small[:, 24:25]).then_inc(w0_arg, 1)

            def conv_taps(i):
                dve.wait_ge(conv_first, i + 1)
                for tap in range(3):
                    sh = 3 - tap
                    for j in range(2):
                        blk = conv_block(i) + j
                        o = cvb[:, i % 2, j * T + sh:(j + 1) * T]
                        last = stt(out=o, in0=bank[4 + i % 4][:, j * T:(j + 1) * T - sh],
                                   scalar=colA[:, 24 * tap + blk:24 * tap + blk + 1], in1=o, op0=ALU.mult, op1=ALU.add)
                    if tap < 2:
                        link(last)
                B.release(last, ("conv", i))

            def core_inputs(g):
                for c in range(TT):
                    B.ready(dve, ("xn", g, c))
                    if g >= 2 and c == 0:
                        B.ready(dve, ("y", g - 2, 1))
                    B.release(tt_(xd[:, g % 2, c * 512:(c + 1) * 512].rearrange("p (h d) -> p h d", d=HD),
                                  bank[1 + c][:, :].rearrange("p (h d) -> p h d", d=HD),
                                  dtv[:, c, g * HPG:(g + 1) * HPG].unsqueeze(2).broadcast_to([P, HPG, HD]), ALU.mult),
                              ("xn", g, c))
                    if c == 0:
                        B.ready(dve, ("cb", g))
                        if g >= 2:
                            B.ready(dve, ("state", g - 2))
                        tt_(cbm[:, g % 2, :].rearrange("p (c l) -> p c l", l=P),
                            bank[0][:, 0:T].rearrange("p (c l) -> p c l", l=P),
                            C("upto").unsqueeze(1).broadcast_to([P, TT, P]), ALU.mult).then_inc(cbm_ready, 1)
                        B.release(V_.tensor_copy(Bn[:, g % 2, :], bank[0][:, T:T + P]), ("cb", g))

            def core(g):
                for half in range(2):
                    for c in range(TT):
                        B.ready(dve, ("ab", g, half, c))
                        if g and c == 0:
                            B.ready(dve, ("y", g - 1, half))
                        for q in range(4):
                            h = g * HPG + 4 * half + q
                            last = ts_(dec[:, 2 * half + c, q * P:(q + 1) * P],
                                       bank[4 + 2 * half + c][:, q * P:(q + 1) * P], acs[:, c, h:h + 1], 0.0,
                                       ALU.subtract, ALU.min)
                        if c == 0:
                            B.release(last, ("ab", g, half, 0))
                        else:
                            last.then_inc(arg1_ready, 1)
                dve.wait_ge(cbm_ready, g + 1)
                for half in range(2):
                    for c in range(TT):
                        dve.wait_ge(dec_ready, 4 * g + 2 * half + c + 1)
                        o = dec[:, 2 * half + c, :].rearrange("p (h l) -> p h l", l=P)
                        tt_(o, o, cbm[:, g % 2, c * P:(c + 1) * P].unsqueeze(1).broadcast_to([P, 4, P]),
                            ALU.mult).then_inc(m_ready, 1)

            def skip(g):
                for half in range(2):
                    B.ready(dve, ("y", g, half))
                    for j in range(2):
                        blk = 4 * g + 2 * half + j
                        last = stt(out=xsT[:, blk, :], in0=xsT[:, blk, :], scalar=dcol[:, blk:blk + 1],
                                   in1=bank[1 + half][:, j * T:(j + 1) * T], op0=ALU.mult, op1=ALU.add)
                    B.release(last, ("y", g, half))

            def gate(groups):
                for g in groups:
                    dve.wait_ge(z_silu, g + 1)
                    for half in range(2):
                        B.released(dve, ("y", g, half))
                    tt_(xsT[:, 4 * g:4 * g + 4, :], xsT[:, 4 * g:4 * g + 4, :], zr[:, 4 * g:4 * g + 4, :],
                        ALU.mult).then_inc(gated, 1)

            def ssd_norm_groups():
                for g in range(GROUPS):
                    dve.wait_ge(y_rstd, g + 1)
                    for b in range(4):
                        blk = 4 * g + b
                        last = stt(out=xsT[:, blk, :], in0=xsT[:, blk, :],
                                   scalar=colB[:, SSD_NORM + blk:SSD_NORM + blk + 1], in1=rg[:, g % 2, :],
                                   op0=ALU.mult, op1=ALU.mult)
                    last.then_inc(y_ready, 1)
                    if g:
                        y_lo(g - 1)

            def y_lo(g):
                input_lo(("ssd_out", g), xsT[:, 4 * g:4 * g + 4, :])

            split(0, 0)
            for n, (kind, t) in enumerate(DT):
                before = DT[n - 1]
                split(n, 1)
                if n == 0:
                    norm_split(0)
                if kind == "attn_out" and t == 0:
                    attention()
                if before == ("attn_out", 1):
                    residual("attn_acc")
                    norm_split(1)
                if before[0] == "ffn_up":
                    hidden(before[1])
                if before == ("ffn_gate", 1):
                    hidden_lo(0)
                if before[0] == "ffn_down" and before[1] < NC_F - 2:
                    hidden_lo(before[1] + 1)
                if before == ("ffn_down", NC_F - 1):
                    residual("ffn_acc")
                    norm_split(2)
                    step_sizes()
                if before in CONV_TILES:
                    i = CONV_TILES.index(before)
                    if i == 0:
                        decay_sums()
                    conv_taps(2 * i)
                if before[0] == "ssd_z":
                    skip(before[1])
                if kind == "ssd_z" and t:
                    core_inputs(t)
                if before == ("ssd_z", GROUPS - 1):
                    gate([GROUPS - 1])
                    ssd_norm_groups()
                if before == ("ssd_out", 0):
                    y_lo(GROUPS - 1)
                split(n, 2)
                split(n, 3)
                split(n + 1, 0)
                if n == 0:
                    lam()
                if 1 <= n <= 4:
                    qk_normalise(n - 1)
                if (kind, t) == ("ffn_down", NC_F - 2):
                    hidden_lo(NC_F - 1)
                if before in CONV_TILES:
                    conv_taps(2 * CONV_TILES.index(before) + 1)
                if (kind, t) == CONV_TILES[-1]:
                    core_inputs(0)
                if kind == "ssd_z":
                    core(t)
                    if t == GROUPS - 1:
                        gate(range(t))
            residual("ssd_acc")

            norm(3)
            def per_expert(v):
                return v.rearrange("p (t e) -> p t e", e=E)

            B.ready(dve, "logits")
            lg_ = lg[:, :, :]
            B.release(V_.tensor_copy(lg_, bank[0][:, 0:TT * E].rearrange("p (t e) -> p t e", e=E)), "logits")
            B.released(dve, "logits")
            order = C("rank_of").unsqueeze(1).broadcast_to([P, TT, E])
            tmp = per_expert(tw[:, 2, :])

            def best(v, oh_k, m_k, s_k):
                link(V_.tensor_reduce(m_k, v, AX_X, ALU.max))
                link(tt_(tmp, v, m_k.unsqueeze(2).broadcast_to([P, TT, E]), ALU.is_ge))
                link(tt_(tmp, tmp, order, ALU.mult))
                link(V_.tensor_reduce(s_k, tmp, AX_X, ALU.max))
                link(tt_(oh_k, order, s_k.unsqueeze(2).broadcast_to([P, TT, E]), ALU.is_equal))

            oh1, oh2, sel, comb = (per_expert(oh[:, j, :]) for j in range(4))
            m1, m2, s1, s2 = (tw[:, 3 + j, 0:TT] for j in range(4))
            best(lg_, oh1, m1, s1)
            lg2 = per_expert(tw[:, 7, :])
            link(stt(out=lg2, in0=oh1, scalar=-3e38, in1=lg_, op0=ALU.mult, op1=ALU.add))
            best(lg2, oh2, m2, s2)
            tt_(tw[:, 0, 0:TT], m2, m1, ALU.subtract).then_inc(top_diff, 1)
            tt_(sel, oh1, oh2, ALU.add).then_inc(sel_ready, 1)
            B.ready(dve, "rank")
            dve.wait_ge(sel_ready, 1)
            rank = per_expert(tw[:, 11, :])
            link(stt(out=rank, in0=bank[1][:, 0:2 * E].rearrange("p (t e) -> p t e", e=E), scalar=1.0, in1=sel,
                     op0=ALU.add, op1=ALU.mult))
            for p in range(PASSES):
                link(ts_(rj[:, :, p * E:(p + 1) * E], rank, -1.0 - p * SLOTS, None, ALU.add))
            link(V_.memset(rj[:, :, JOBS:JOBS + 1], -1.0))
            link(V_.tensor_reduce(tw[:, 0, E:E + 1], bank[1][:, 2 * E:3 * E], AX_X, ALU.max))
            B.release(ts_(flag[:, 0:1], tw[:, 0, E:E + 1], float(SLOTS), None, ALU.is_gt), "rank")
            B.released(dve, "rank")
            V_.tensor_copy(flag[:, 1:2], flag[:, 0:1]).then_inc(flag_ready, 1)

            def places(job):
                for tt in range(TT):
                    last = ts_(Pm[:, tt, :], C("slot_no"), rj[:, tt, bass.ds(job, 1)], None, ALU.is_equal)
                last.then_inc(place_ready, 1)

            for i in range(4):
                B.released(dve, ("hnat", i))
            places(0)
            dve.wait_ge(top_exp, 1)
            w1, w2, den = tw[:, 8, 0:TT], tw[:, 9, 0:TT], tw[:, 10, 0:TT]
            link(ts_(den, tw[:, 1, 0:TT], 1.0, None, ALU.add))
            link(V_.reciprocal(w1, den))
            link(tt_(w2, w1, tw[:, 1, 0:TT], ALU.mult))
            link(tt_(comb, oh1, w1.unsqueeze(2).broadcast_to([P, TT, E]), ALU.mult))
            link(tt_(tmp, oh2, w2.unsqueeze(2).broadcast_to([P, TT, E]), ALU.mult))
            link(tt_(comb, comb, tmp, ALU.add))
            for p in range(PASSES):
                link(V_.tensor_copy(cj[:, :, 1 + p * E:1 + (p + 1) * E], comb))
            V_.memset(cj[:, :, 0:1], 0.0)
            V_.memset(PT[0:SLOTS, :, :], 0.0).then_inc(no_result, 1)
            for i in range(4):
                B.released(dve, ("xnat", i))

            def gathered(job):
                for half in range(2):
                    gather_ready(dve, half, job)
                    dve.wait_ge(hg_hi, job * 2 + (half + 1))
                    b = 1 + 2 * half
                    o = hTg[:, :, 4 * half:4 * half + 4, :]
                    tt_(o[:, 1], bank[b][:, 0:4 * SLOTS].rearrange("p (k n) -> p k n", k=4), o[:, 0].bitcast(F32),
                        ALU.subtract).then_inc(free[b], 1)

            def add_result(job):
                for i in range(4):
                    tt, half = i // 2, i % 2
                    job_ready(dve, ("sc", i), job)
                    o = xnat[:, tt, half * 512:(half + 1) * 512]
                    last = stt(out=o, in0=bank[SCATTER_BANK[i]][:, :], scalar=cj[:, tt, bass.ds(job, 1)], in1=o,
                               op0=ALU.mult, op1=ALU.add)
                    last.then_inc(free[SCATTER_BANK[i]], 1)

            def job_body(job):
                def split(tile):
                    w = expert_landed(dve, tile, job)
                    for q in range(4):
                        if tile == ET[0] and q == 2:
                            gathered(job)
                        n = 4 * EXPERT[tile] + q
                        dve.wait_ge(w_hi, job * 4 * NE + (WQ + n + 1))
                        hi, lo = (wsplit[:, EXPERT_BUFFER[n % EXPERT_SPLITS], part, :].rearrange("p (k n) -> p k n", n=w.shape[2])
                                  for part in range(2))
                        tt_(lo, quarter(w, q), hi.bitcast(F32), ALU.subtract).then_inc(w_lo, 1)

                def hidden(c):
                    job_released(dve, ("g", c), job)
                    tile_finished(dve, ("up", c), job)
                    if c:
                        job_ready(dve, ("hidT", c - 1), job)
                    tt_(ehid[0:SLOTS, :], esg[0:SLOTS, c % 2, :], bank[2 + c % 2][0:SLOTS, :], ALU.mult)\
                        .then_inc(hid_ready, 1)

                def hidden_lo(c):
                    dve.wait_ge(hid_hi, job * NC_F + (c + 1))
                    tt_(ehidT[:, c % 2, 1, :, :], bank[6][:, 0:4 * SLOTS].rearrange("p (k n) -> p k n", k=4),
                        ehidT[:, c % 2, 0, :, :].bitcast(F32), ALU.subtract).then_inc(free[6], 1)

                for tile in ET:
                    kind, c = tile
                    split(tile)
                    if kind == "up" and c:
                        hidden_lo(c - 1)
                    if tile == ("up", 0):
                        add_result(job)
                        for i in range(4):
                            job_released(dve, ("sc", i), job)
                    if tile == ("gate", 1):
                        hidden(0)
                    elif kind == "down" and c < NC_F - 1:
                        hidden(c + 1)
                    if tile == ("gate", 2):
                        job_ready(dve, "PT", job)
                        places(job + 1)
                hidden_lo(NC_F - 1)

            with dve.Fori(0, E) as job:
                job_body(job)
            more = dve.value_load(flag[0:1, 0:1], min_val=0, max_val=1)
            with dve.If(more > 0):
                with dve.Fori(E, JOBS) as job:
                    job_body(job)
            add_result(more * (JOBS - E) + E)
            for i in range(4):
                job_released(dve, ("sc", i), more * (JOBS - E) + E)
            V_.memset(small[:, 40:41], 0.0).then_inc(moe_done, 1)


INPUTS = ["x", "rel_bias", "norm_mix", "norm_ffn", "attn_w_in", "attn_q_gain", "attn_k_gain", "attn_lambda",
          "attn_subln", "attn_w_out", "ffn_w_gate", "ffn_w_up", "ffn_w_down", "ssd_w_in", "ssd_conv_w",
          "ssd_conv_b", "ssd_dt_bias", "ssd_a_log", "ssd_d", "ssd_norm", "ssd_w_out", "moe_router",
          "moe_w_gate", "moe_w_up", "moe_w_down"]


def kernel(**inputs):
    import concourse.bacc as bacc
    from concourse.bass_utils import run_bass_kernel_spmd

    nc = bacc.Bacc("TRN2", target_bir_lowering=False, num_devices=1)
    const, hot = constants()
    arrays = {name: np.ascontiguousarray(inputs[name]) for name in INPUTS}
    arrays["const"], arrays["hot"] = const, hot
    args = [nc.dram_tensor(name, a.shape, mybir.dt.from_np(a.dtype), kind="ExternalInput").ap()
            for name, a in arrays.items()]
    args.append(nc.dram_tensor("out", (1, T, D), F32, kind="ExternalOutput").ap())
    hybrid_trunk(nc, *args)
    result = run_bass_kernel_spmd(nc, [arrays], core_ids=[0])
    return result.results[0]["out"]
```
